# Optimizing a Trainium2 kernel written in Bass

```python
import jax, jax.numpy as jnp
from jax import lax
import numpy as np

D_MODEL = 1024
BATCH = 1
SEQ = 512
DEPTH = 2

N_META = 16
BLOCK = 128
HEAD_DIM = 64
RWKV_WIDTH = D_MODEL // 2
FOX_WIDTH = D_MODEL - RWKV_WIDTH
RWKV_HEADS = RWKV_WIDTH // HEAD_DIM
FOX_HEADS = FOX_WIDTH // HEAD_DIM
D_FF = 2816
LORA_DECAY = 64
LORA_A = 64
LORA_V = 32
LORA_G = 160
NORM_EPS = 1e-6
LNX_EPS = 64e-5
NEG_INF = -1e30

N_RWKV_COLS = 3 * RWKV_WIDTH + LORA_DECAY + LORA_A + LORA_G
N_FOX_COLS = 3 * FOX_WIDTH + FOX_HEADS
N_COLS = N_RWKV_COLS + N_FOX_COLS

kernel_name = 'hybrid_rwkv7_fox_macaron_trunk'

def _split(t, sizes):
    return jnp.split(t, np.cumsum(sizes)[:-1].tolist(), axis=-1)

def rms_norm(x, g):
    xf = x.astype(jnp.float32)
    y = xf * lax.rsqrt(jnp.mean(xf * xf, axis=-1, keepdims=True) + NORM_EPS)
    return (y * g.astype(jnp.float32)).astype(x.dtype)

def swiglu(x, w_in, w_out):
    gate, up = jnp.split(x @ w_in, 2, axis=-1)
    return (jax.nn.silu(gate) * up) @ w_out

def token_shift(y, mu):
    prev = jnp.pad(y, ((0, 0), (1, 0), (0, 0)))[:, :-1]
    return y + (prev - y) * mu

def rwkv7_scan(r, decay, k, v, kk, a):
    def step(S, inp):
        r_t, w_t, k_t, v_t, kk_t, a_t = inp
        sa = jnp.einsum('bhvk,bhk->bhv', S, -kk_t)
        S = S * w_t[:, :, None, :] + sa[..., None] * (kk_t * a_t)[:, :, None, :] + v_t[..., None] * k_t[:, :, None, :]
        return S, jnp.einsum('bhvk,bhk->bhv', S, r_t)
    b, _, h, n = r.shape
    s0 = jnp.zeros((b, h, n, n), jnp.float32)
    xs = tuple(jnp.moveaxis(t, 1, 0) for t in (r, decay, k, v, kk, a))
    _, out = lax.scan(step, s0, xs)
    return jnp.moveaxis(out, 0, 1)

def fox_attention(q, k, v, log_f):
    b, L, h, dh = q.shape
    n_blocks = -(-L // BLOCK)
    lp = n_blocks * BLOCK
    pad = lp - L
    c = jnp.cumsum(log_f, axis=1)
    def lpad(t):
        return jnp.pad(t, ((0, 0), (pad, 0)) + ((0, 0),) * (t.ndim - 2))
    qp, kp, vp, cp = lpad(q), lpad(k), lpad(v), lpad(c)
    k_bhkd = kp.transpose(0, 2, 1, 3)
    v_bhkd = vp.transpose(0, 2, 1, 3)
    c_key = cp.transpose(0, 2, 1)
    q_blocks = jnp.moveaxis(qp.reshape(b, n_blocks, BLOCK, h, dh), 1, 0)
    c_blocks = jnp.moveaxis(cp.reshape(b, n_blocks, BLOCK, h), 1, 0)
    key_pos = jnp.arange(lp)
    key_valid = key_pos >= pad
    scale = dh ** -0.5

    def one_block(args):
        i, qb, cb = args
        s = jnp.einsum('bqhd,bhkd->bhqk', qb, k_bhkd).astype(jnp.float32) * scale
        s = s + cb.transpose(0, 2, 1)[..., None] - c_key[:, :, None, :]
        q_pos = i * BLOCK + jnp.arange(BLOCK)
        mask = (key_pos[None, :] <= q_pos[:, None]) & key_valid[None, :]
        p = jax.nn.softmax(jnp.where(mask, s, NEG_INF), axis=-1)
        return jnp.einsum('bhqk,bhkd->bqhd', p.astype(v_bhkd.dtype), v_bhkd)

    out = lax.map(one_block, (jnp.arange(n_blocks), q_blocks, c_blocks))
    return jnp.moveaxis(out, 0, 1).reshape(b, lp, h, dh)[:, pad:]

def token_mixer(u, w_proj, mu, vres, v_first, decay_up, decay_bias, iclr_up, iclr_bias, gate_up,
                k_k, k_a, r_k, ln_x_w, ln_x_b, forget_bias, fox_out_gain, w_out):
    b, L, _ = u.shape
    y = u @ w_proj
    r, k, v, wd, ad, gd = _split(token_shift(y[..., :N_RWKV_COLS], mu),
                                 [RWKV_WIDTH] * 3 + [LORA_DECAY, LORA_A, LORA_G])
    qf, kf, vf, fl = _split(y[..., N_RWKV_COLS:N_COLS], [FOX_WIDTH] * 3 + [FOX_HEADS])

    w_log = -jax.nn.softplus(-(decay_bias + jnp.tanh(wd) @ decay_up)) - 0.5
    decay = jnp.exp(-jnp.exp(w_log.astype(jnp.float32)))
    a = jax.nn.sigmoid(iclr_bias + ad @ iclr_up)
    g = jax.nn.sigmoid(gd) @ gate_up
    if vres is None:
        v_first = v
    else:
        mu_v, v_up, v_bias = vres
        vd = token_shift(y[..., N_COLS:], mu_v)
        v = v + (v_first - v) * jax.nn.sigmoid(v_bias + vd @ v_up)
    def heads(t):
        return t.reshape(b, L, RWKV_HEADS, HEAD_DIM).astype(jnp.float32)
    kk = heads(k * k_k)
    kk = kk / jnp.maximum(jnp.linalg.norm(kk, axis=-1, keepdims=True), 1e-12)
    k = k * (1 + (a - 1) * k_a)
    rh, kh, vh = heads(r), heads(k), heads(v)
    o = rwkv7_scan(rh, heads(decay), kh, vh, kk, heads(a))
    o = (o - o.mean(-1, keepdims=True)) * lax.rsqrt(jnp.var(o, axis=-1, keepdims=True) + LNX_EPS)
    o = o.reshape(b, L, RWKV_WIDTH) * ln_x_w + ln_x_b
    bonus = (jnp.sum(rh * kh * r_k, axis=-1, keepdims=True) * vh).reshape(b, L, RWKV_WIDTH)
    o_rwkv = ((o + bonus) * g).astype(u.dtype)

    def fh(t):
        return t.reshape(b, L, FOX_HEADS, HEAD_DIM)
    log_f = jax.nn.log_sigmoid((fl + forget_bias).astype(jnp.float32))
    of = fox_attention(fh(qf), fh(kf), fh(vf), log_f).astype(jnp.float32)
    of = of * lax.rsqrt(jnp.mean(of * of, axis=-1, keepdims=True) + NORM_EPS)
    o_fox = (of.reshape(b, L, FOX_WIDTH) * fox_out_gain).astype(u.dtype)

    return jnp.concatenate([o_rwkv, o_fox], axis=-1) @ w_out, v_first

def setup_inputs(seed: int = 0) -> dict:
    key = jax.random.key(seed)
    ks = jax.random.split(key, 24)
    f32 = jnp.float32
    def nrm(k, shape, scale):
        return jax.random.normal(k, shape, f32) * scale
    def unif(k, shape, lo, hi):
        return jax.random.uniform(k, shape, f32, lo, hi)
    dm1 = DEPTH - 1
    return {
        'x': nrm(ks[0], (BATCH, SEQ, D_MODEL), 1.0),
        'meta_tokens': nrm(ks[1], (N_META, D_MODEL), 1.0),
        'norm_gains': 1.0 + nrm(ks[2], (DEPTH, 6, D_MODEL), 0.02),
        'ffn_w_in': nrm(ks[3], (DEPTH, 2, D_MODEL, 2 * D_FF), D_MODEL ** -0.5),
        'ffn_w_out': nrm(ks[4], (DEPTH, 2, D_FF, D_MODEL), D_FF ** -0.5),
        'w_in': nrm(ks[5], (DEPTH, D_MODEL, N_COLS), D_MODEL ** -0.5),
        'w_in_vres': nrm(ks[6], (dm1, D_MODEL, LORA_V), D_MODEL ** -0.5),
        'shift_mu': unif(ks[7], (DEPTH, N_RWKV_COLS), 0.0, 1.0),
        'shift_mu_vres': unif(ks[8], (dm1, LORA_V), 0.0, 1.0),
        'decay_up': nrm(ks[9], (DEPTH, LORA_DECAY, RWKV_WIDTH), 0.1),
        'decay_bias': unif(ks[10], (DEPTH, RWKV_WIDTH), -6.0, -1.0),
        'iclr_up': nrm(ks[11], (DEPTH, LORA_A, RWKV_WIDTH), 0.5 * LORA_A ** -0.5),
        'iclr_bias': nrm(ks[12], (DEPTH, RWKV_WIDTH), 0.1),
        'gate_up': nrm(ks[13], (DEPTH, LORA_G, RWKV_WIDTH), LORA_G ** -0.5),
        'vres_up': nrm(ks[14], (dm1, LORA_V, RWKV_WIDTH), 0.5 * LORA_V ** -0.5),
        'vres_bias': 1.0 + nrm(ks[15], (dm1, RWKV_WIDTH), 0.1),
        'k_k': 0.85 + nrm(ks[16], (DEPTH, RWKV_WIDTH), 0.02),
        'k_a': 1.0 + nrm(ks[17], (DEPTH, RWKV_WIDTH), 0.02),
        'r_k': nrm(ks[18], (DEPTH, RWKV_HEADS, HEAD_DIM), 0.1),
        'ln_x_w': 1.0 + nrm(ks[19], (DEPTH, RWKV_WIDTH), 0.02),
        'ln_x_b': nrm(ks[20], (DEPTH, RWKV_WIDTH), 0.02),
        'forget_bias': unif(ks[21], (DEPTH, FOX_HEADS), 1.0, 6.0),
        'fox_out_gain': 1.0 + nrm(ks[22], (DEPTH, FOX_WIDTH), 0.02),
        'w_out': nrm(ks[23], (DEPTH, D_MODEL, D_MODEL), D_MODEL ** -0.5),
    }

def reference(x, meta_tokens, norm_gains, ffn_w_in, ffn_w_out, w_in, w_in_vres, shift_mu, shift_mu_vres,
              decay_up, decay_bias, iclr_up, iclr_bias, gate_up, vres_up, vres_bias, k_k, k_a, r_k,
              ln_x_w, ln_x_b, forget_bias, fox_out_gain, w_out):
    b = x.shape[0]
    meta = jnp.broadcast_to(meta_tokens[None].astype(x.dtype), (b, N_META, D_MODEL))
    h = jnp.concatenate([meta, x], axis=1)
    v_first = None
    for i in range(DEPTH):
        g = norm_gains[i]
        h = h + 0.5 * rms_norm(swiglu(rms_norm(h, g[0]), ffn_w_in[i, 0], ffn_w_out[i, 0]), g[1])
        if i == 0:
            w_proj, vres = w_in[0], None
        else:
            w_proj = jnp.concatenate([w_in[i], w_in_vres[i - 1]], axis=1)
            vres = (shift_mu_vres[i - 1], vres_up[i - 1], vres_bias[i - 1])
        m, v_first = token_mixer(rms_norm(h, g[2]), w_proj, shift_mu[i], vres, v_first,
                                 decay_up[i], decay_bias[i], iclr_up[i], iclr_bias[i], gate_up[i],
                                 k_k[i], k_a[i], r_k[i], ln_x_w[i], ln_x_b[i], forget_bias[i],
                                 fox_out_gain[i], w_out[i])
        h = h + rms_norm(m, g[3])
        h = h + 0.5 * rms_norm(swiglu(rms_norm(h, g[4]), ffn_w_in[i, 1], ffn_w_out[i, 1]), g[5])
    return h[:, N_META:]


_drawn_inputs = setup_inputs


def setup_inputs(seed=0):
    import zlib

    import numpy as np

    out = dict(_drawn_inputs(seed))
    spreads = {}
    factors = {'shift_mu_vres': 29.776,
     'iclr_bias': 3.054,
     'vres_bias': 142.48,
     'k_k': 29.22,
     'k_a': 5.579,
     'ln_x_w': 27.061,
     'ln_x_b': 59.755,
     'fox_out_gain': 12.986,
     'w_in_vres': 8.0,
     'vres_up': 8.0}
    for name, (base, spread) in spreads.items():
        noise = np.random.default_rng([zlib.crc32(name.encode()), seed]).standard_normal(out[name].shape)
        drawn = base * np.exp(spread * noise) if base else spread * noise
        out[name] = __import__('jax').numpy.asarray(drawn.astype(out[name].dtype))
    for name, factor in factors.items():
        out[name] = (out[name] * factor).astype(out[name].dtype)
    return out
```

```python
from contextlib import ExitStack

import numpy as np

import concourse.bass as bass
from concourse import mybir

D_MODEL = 1024
SEQ = 512
N_META = 16
DEPTH = 2
D_FF = 2816
HEAD = 64
WIDTH = 512
P = 128
T = SEQ + N_META
HT = T // 2
DT = D_MODEL // P
WT = WIDTH // P
FT = D_FF // P
FH = FT // 2
CHUNK = 64
N_CHUNK = -(-T // CHUNK)
LAST = T - (N_CHUNK - 1) * CHUNK
QT = [0, 106, 212, 318, 424, 528]
NQ = len(QT) - 1
HEADS = WIDTH // HEAD
NORM_EPS = 1e-6
LNX_EPS = 64e-5
DECAY = float(np.exp(-0.5))
NEG = -1e30

UNIT = 16 * P
OUT_UNIT = FH * P
FFN_UNITS = 2 * (FH + DT)
PROJ_UNITS = 14
WO_UNITS = DT // 2
LAYER_UNITS = 2 * FFN_UNITS + PROJ_UNITS + WO_UNITS

QF, KF, VF, R, K, V, WA, GD, MISC = 0, 4, 8, 12, 16, 20, 24, 25, 26
N_TILES = 27
FORGET_ROW = 64

GAIN, MU = 0, 6 * DT
DBIAS = MU + N_TILES - R
IBIAS, VBIAS, KKG, KAG, RKG, LNW, LNB, FOXG = (DBIAS + WT * n for n in range(1, 9))
FBIAS = FOXG + WT
N_PAR = FBIAS + 1

LEVELS = 6
IDENT, ONES, HEADSUM, CAUSAL, PAIRMASK = 0, 128, 256, 384, 512
LEVEL = PAIRMASK + 256
RESET = LEVEL + LEVELS * P
N_CONST = RESET + T

F32 = mybir.dt.float32
F32R = mybir.dt.float32r
ALU = mybir.AluOpType
ACT = mybir.ActivationFunctionType
AX = mybir.AxisListType


def build(nc, h_in, ffn_in, ffn_out, proj, w_out, lora, params, consts, out):
    ctx = ExitStack()
    with ctx:
        def sb(name, shape, dt=F32):
            return ctx.enter_context(nc.sbuf_tensor(name, shape, dt))

        def sem(name):
            return ctx.enter_context(nc.semaphore(name))

        h = sb("h", [P, DT, T])
        raw = sb("raw", [P, 2, UNIT])
        v_first = sb("v_first", [P, WT, T])
        cst = sb("cst", [P, N_CONST])
        prm = sb("prm", [P, DEPTH * N_PAR])
        root = sb("root", [P, T])
        rs_pre = sb("rs_pre", [P, T])
        rs_post = sb("rs_post", [P, T])
        acc = sb("acc", [P, T])
        sqb = sb("sqb", [P, 2, T])
        eps = sb("eps", [P, 4])

        with ExitStack() as low:
            def lo_sb(name, shape, dt=F32):
                return low.enter_context(nc.sbuf_tensor(name, shape, dt))
            with ExitStack() as a:
                def at_sb(name, shape, dt=F32):
                    return a.enter_context(nc.sbuf_tensor(name, shape, dt))
                qz = at_sb("qz", [P, 2, T])
                vz = at_sb("vz", [P, 2, NQ, P])
                c_all = at_sb("c_all", [P, T])
                c_one = at_sb("c_one", [P, 2, T])
                c_key = at_sb("c_key", [P, 2, T])
                c_tok = at_sb("c_tok", [P, NQ, HEADS])
                score = at_sb("score", [P, 2, T])
                prob = at_sb("prob", [P, 2, T])
                prob_t = at_sb("prob_t", [P, 2, NQ, QT[1]])
                diag = at_sb("diag", [P, 2, P])
                neg_max = at_sb("neg_max", [P, 2])
                row_sum = at_sb("row_sum", [P, 2])
                inv_sum = at_sb("inv_sum", [P, 2])
                fg = at_sb("fg", [P, 2, T])
                v_pair = at_sb("v_pair", [P, T])
            with ExitStack() as c:
                def ch_sb(name, shape, dt=F32):
                    return c.enter_context(nc.sbuf_tensor(name, shape, dt))
                ar = ch_sb("ar", [P, 2, WT, 2 * P])
                bkv = ch_sb("bkv", [P, 2, WT, 3 * P])
                gm = ch_sb("gm", [P, 2, WT, 4 * P])
                tok = ch_sb("tok", [P, 2, WT, 3 * P])
                ym = ch_sb("ym", [P, WT, P])
                zm = ch_sb("zm", [P, WT, P])
                qm = ch_sb("qm", [P, WT, P])
                uo = ch_sb("uo", [P, WT, P])
                rb = ch_sb("rb", [P, WT, P])
                sa = ch_sb("sa", [P, WT, P])
                hs = ch_sb("hs", [P, WT, P])
        x_hi = sb("x_hi", [P, DT, T], F32R)
        x_lo = sb("x_lo", [P, DT, T], F32R)
        w_hi = sb("w_hi", [P, 2, UNIT], F32R)
        w_lo = sb("w_lo", [P, 2, UNIT], F32R)
        with ExitStack() as f:
            def ff_sb(name, shape, dt=F32):
                return f.enter_context(nc.sbuf_tensor(name, shape, dt))
            hid_hi = ff_sb("hid_hi", [P, FH, T], F32R)
            hid_lo = ff_sb("hid_lo", [P, FH, T], F32R)
            y_ffn = ff_sb("y_ffn", [P, DT, T])
            gs = ff_sb("gs", [P, 2, T])
            us = ff_sb("us", [P, 2, T])
            sg = ff_sb("sg", [P, 2, T])
            hid = ff_sb("hid", [P, 2, T])
        tiles = sb("tiles", [P, N_TILES * T])
        aa = sb("aa", [P, WT, T])
        ll = sb("ll", [P, WT, T])
        kk = sb("kk", [P, WT, T])
        bonus = sb("bonus", [P, WT, T])

        ps = ctx.enter_context(nc.psum_tensor("ps", [P, 8, 512], F32))

        def spread(ap, n):
            return ap.unsqueeze(1).broadcast_to([ap.shape[0], n, ap.shape[1]])

        def tile(i, n=1):
            return tiles[:, i * T:(i + n) * T]

        def group(i, c0=0, c1=T, p0=0, p1=P):
            return tiles[p0:p1, i * T:(i + WT) * T].rearrange("p (m t) -> p m t", m=WT)[:, :, c0:c1]

        lora_w = tiles[:, (KF + 2) * T:(KF + 2) * T + 3 * WIDTH]
        gate_w = tiles[:, KF * T:KF * T + 2 * WIDTH]
        tmp = [tile(VF + 1 + n) for n in range(3)]
        y_mix = tiles[:, KF * T:(KF + DT) * T].rearrange("p (m t) -> p m t", m=DT)
        e_fwd = [tmp[0][:, q * 260:(q + 1) * 260].rearrange("p (m t) -> p m t", m=WT) for q in range(2)]
        e_bwd = [tmp[1][:, q * 256:(q + 1) * 256].rearrange("p (m t) -> p m t", m=WT) for q in range(2)]
        shifted = [ll[:, 0:3, :].rearrange("p m t -> p (m t)")[:, q * 532:q * 532 + T + 1] for q in range(2)]
        delta = [kk[:, q, :] for q in range(2)]

        def par(l, col, p0=0, p1=P):
            return prm[p0:p1, l * N_PAR + col:l * N_PAR + col + 1]

        ident = cst[:, IDENT:IDENT + P]
        ones = cst[:, ONES:ONES + P]
        headsum = cst[:, HEADSUM:HEADSUM + P]
        ident4 = spread(ident, WT)

        def pair(b):
            return ps[:, b:b + 2, 0:HT]

        def halves(ap):
            return ap.rearrange("p (a t) -> p a t", a=2)

        raw_loaded = [sem("raw_loaded0"), sem("raw_loaded1")]
        small_loaded = sem("small_loaded")
        h_loaded = sem("h_loaded")
        lora_loaded = sem("lora_loaded")
        gate_loaded = sem("gate_loaded")
        stored = sem("stored")
        hi_ready = sem("hi_ready")
        w_split = sem("w_split")
        unit_done = sem("unit_done")
        evacuated = sem("evacuated")
        gate_done = sem("gate_done")
        gs_ready = sem("gs_ready")
        sg_ready = sem("sg_ready")
        hid_ready = sem("hid_ready")
        hid_hi_ready = sem("hid_hi_ready")
        hid_lo_ready = sem("hid_lo_ready")
        sq_ready = sem("sq_ready")
        acc_added = sem("acc_added")
        stat_done = sem("stat_done")
        root_ready = sem("root_ready")
        rs_ready = sem("rs_ready")
        y_scaled = sem("y_scaled")
        h_ready = sem("h_ready")
        x_hi_ready = sem("x_hi_ready")
        x_lo_ready = sem("x_lo_ready")
        delta_ready = sem("delta_ready")
        tiles_ready = sem("tiles_ready")
        dve_step = sem("dve_step")
        act_step = sem("act_step")
        shift_zero = sem("shift_zero")
        fg_exp = sem("fg_exp")
        fg_abs = sem("fg_abs")
        c_ready = sem("c_ready")
        c_turned = sem("c_turned")
        c_tok_ready = sem("c_tok_ready")
        att_zero = sem("att_zero")
        q_ready = sem("q_ready")
        c_one_ready = sem("c_one_ready")
        c_spread = sem("c_spread")
        c_key_ready = sem("c_key_ready")
        v_turned = sem("v_turned")
        vz_ready = sem("vz_ready")
        scored = sem("scored")
        score_read = sem("score_read")
        max_ready = sem("max_ready")
        prob_ready = sem("prob_ready")
        diag_ready = sem("diag_ready")
        prob_turned = sem("prob_turned")
        prob_t_ready = sem("prob_t_ready")
        att_done = sem("att_done")
        att_read = sem("att_read")
        lora_in = sem("lora_in")
        ksq_ready = sem("ksq_ready")
        decay_done = sem("decay_done")
        iclr_done = sem("iclr_done")
        vres_done = sem("vres_done")
        knorm_done = sem("knorm_done")
        decay_sig = sem("decay_sig")
        iclr_sig = sem("iclr_sig")
        vres_sig = sem("vres_sig")
        kmax_ready = sem("kmax_ready")
        kroot_ready = sem("kroot_ready")
        rk_ready = sem("rk_ready")
        bonus_done = sem("bonus_done")
        bonus_ready = sem("bonus_ready")
        bd_zero = sem("bd_zero")
        e_ready = sem("e_ready")
        ar_built = sem("ar_built")
        bkv_built = sem("bkv_built")
        gram_done = sem("gram_done")
        gram_ready = sem("gram_ready")
        turned = sem("turned")
        tok_ready = sem("tok_ready")
        off_ready = sem("off_ready")
        z0_done = sem("z0_done")
        q_done = sem("q_done")
        qm_ready = sem("qm_ready")
        zd_done = sem("zd_done")
        yd_done = sem("yd_done")
        z_ready = sem("z_ready")
        y_ready = sem("y_ready")
        r_done = sem("r_done")
        rb_ready = sem("rb_ready")
        sa_done = sem("sa_done")
        sa_ready = sem("sa_ready")
        o_done = sem("o_done")
        o_read = sem("o_read")
        hd_done = sem("hd_done")
        state_ready = sem("state_ready")
        mean_done = sem("mean_done")
        oc_ready = sem("oc_ready")
        osq_ready = sem("osq_ready")
        var_done = sem("var_done")
        oroot_ready = sem("oroot_ready")
        g_done = sem("g_done")
        o_ready = sem("o_ready")
        v_copied = sem("v_copied")
        v_mixed = sem("v_mixed")
        v_built = sem("v_built")
        masked = sem("masked")
        inv_ready = sem("inv_ready")
        eps_set = sem("eps_set")
        h_added = sem("h_added")

        def unit_base(l, phase):
            return l * LAYER_UNITS + {"a": 0, "proj": FFN_UNITS, "wo": FFN_UNITS + PROJ_UNITS,
                                      "b": FFN_UNITS + PROJ_UNITS + WO_UNITS}[phase]

        def slot(base, k):
            return (base + k) % 2

        def units(eng, n, body, first=0):
            turns = max(n - 3, 0) // 2
            body(first, 0)
            body(first + 1, 0)
            if turns:
                with eng.Fori(0, turns) as i:
                    body(first + 2, i)
                    body(first + 3, i)
            for k in range(2 + 2 * turns, n):
                body(first + k, 0)

        def chunk_loop(eng, body):
            body(0, 0, CHUNK)
            with eng.Fori(0, (N_CHUNK - 3) // 2) as i:
                body(i * 2 + 1, 1, CHUNK)
                body(i * 2 + 2, 0, CHUNK)
            body(N_CHUNK - 2, (N_CHUNK - 2) % 2, CHUNK)
            body(N_CHUNK - 1, (N_CHUNK - 1) % 2, LAST)

        def wait(eng, semaphore, value):
            if not isinstance(value, int) or value > 0:
                eng.wait_ge(semaphore, value)

        def norm_bank(l, n):
            if n % 2 == 0:
                return 4 * (1 - unit_base(l, ("a", "proj", "b")[n // 2]) % 2)
            end = (unit_base(l, "a") + FFN_UNITS, unit_base(l, "wo") + WO_UNITS, unit_base(l, "b") + FFN_UNITS)[n // 2]
            return 4 * (end % 2)

        def post_count(l, n):
            return DT * (3 * l + {0: 0, 1: 1, 3: 2}[n])

        block = ctx.enter_context(nc.Block())

        @block.sync
        def _(sp):
            def load(source, cols, base, k, i=0):
                u = i * 2 + k
                wait(sp, w_split, u + (base - 1))
                sp.dma_start(raw[:, slot(base, k), 0:cols], source(u)).then_inc(raw_loaded[slot(base, k)], 16)

            def ffn(l, which, f):
                for fh in range(2):
                    base = unit_base(l, which) + fh * (FH + DT)
                    units(sp, FH, lambda k, i: load(lambda u: ffn_in[f, u + fh * FH], UNIT, base, k, i))
                    units(sp, DT, lambda k, i: load(lambda u: ffn_out[f, fh, u], OUT_UNIT, base + FH, k, i))

            sp.dma_start(cst[:, :], consts).then_inc(small_loaded, 16)
            sp.dma_start(prm[:, :], params).then_inc(small_loaded, 16)
            sp.dma_start(h[:, :, :], h_in).then_inc(h_loaded, 16)
            for l in range(DEPTH):
                ffn(l, "a", 2 * l)
                units(sp, PROJ_UNITS, lambda k, i: load(lambda u: proj[l, u], UNIT, unit_base(l, "proj"), k, i))
                sp.wait_ge(scored, WT * 2 * NQ * (l + 1))
                sp.wait_ge(v_copied, WT * (l + 1))
                sp.dma_start(lora_w, lora[l, :, 0:3 * WIDTH]).then_inc(lora_loaded, 16)
                sp.dma_start(gate_w, lora[l, :, 3 * WIDTH:5 * WIDTH]).then_inc(gate_loaded, 16)
                units(sp, WO_UNITS, lambda k, i: load(lambda u: w_out[l, u], UNIT, unit_base(l, "wo"), k, i))
                ffn(l, "b", 2 * l + 1)
            sp.wait_ge(h_ready, DT * 3 * DEPTH)
            sp.dma_start(out, h[:, :, N_META:T]).then_inc(stored, 16)
            sp.wait_ge(stored, 16)

        @block.tensor
        def _(pe):
            def product(out_ap, w, x, first=True, last=True):
                return pe.matmul(out_ap, w, x, start=first, stop=last)

            def gemm(q, n_m, n_k, xh, xl, before=None):
                for m in range(n_m):
                    for k in range(n_k):
                        if before is not None and m == 0:
                            before(k)
                        cols = slice((m * n_k + k) * P, (m * n_k + k + 1) * P)
                        for n, (w, x) in enumerate(((w_hi, xh), (w_hi, xl), (w_lo, xh))):
                            for half in range(2):
                                ins = product(ps[:, 4 * q + 2 * m + half, 0:HT], w[:, q, cols],
                                              x[:, k, half * HT:(half + 1) * HT],
                                              k == 0 and n == 0, k == n_k - 1 and n == 2)
                    yield ins

            def start_unit(u, base):
                pe.wait_ge(w_split, u + (base + 1))
                wait(pe, evacuated, u + (base - 1))

            def both(bank, w, x, first=True, last=True):
                for half in range(2):
                    ins = product(ps[:, bank + half, 0:HT], w, x[:, half * HT:(half + 1) * HT], first, last)
                return ins

            def statistics(l, n, units_before):
                s = 6 * l + n
                pe.wait_ge(sq_ready, DT * (s + 1))
                pe.wait_ge(acc_added, (DT - 1) * (s + 1))
                wait(pe, evacuated, units_before)
                both(norm_bank(l, n), ones, acc).then_inc(stat_done, 1)

            def operand(g):
                return lambda k: pe.wait_ge(x_lo_ready, DT * g + k + 1)

            def ffn(l, which, f, g, n):
                for fh in range(2):
                    base = unit_base(l, which) + fh * (FH + DT)

                    def unit_in(k, i):
                        u = i * 2 + k
                        first = fh == 0 and k == 0
                        if fh == 0 and k == 1:
                            pe.wait_ge(root_ready, 6 * l + n + 1)
                        start_unit(u, base)
                        gate, up = gemm(slot(base, k), 2, DT, x_hi, x_lo, operand(g) if first else None), None
                        next(gate).then_inc(gate_done, 1)
                        next(gate).then_inc(unit_done, 1)
                        if first:
                            statistics(l, n, base)

                    def unit_out(k, i):
                        start_unit(i * 2 + k, base + FH)
                        before = (lambda kt: pe.wait_ge(hid_lo_ready, FH * (2 * f + fh) + kt + 1)) if k == 0 else None
                        next(gemm(slot(base + FH, k), 1, FH, hid_hi, hid_lo, before)).then_inc(unit_done, 1)

                    units(pe, FH, unit_in)
                    units(pe, DT, unit_out)
                statistics(l, n + 1, unit_base(l, which) + FFN_UNITS)
                pe.wait_ge(root_ready, 6 * l + n + 2)

            def projection(l):
                base = unit_base(l, "proj")

                def unit(k, i):
                    if k == 1:
                        pe.wait_ge(root_ready, 6 * l + 3)
                    start_unit(i * 2 + k, base)
                    for ins in gemm(slot(base, k), 1 if k == PROJ_UNITS - 1 else 2, DT, x_hi, x_lo, operand(4 * l + 1) if k == 0 else None):
                        pass
                    ins.then_inc(unit_done, 1)
                    if k == 0:
                        statistics(l, 2, base)
                units(pe, PROJ_UNITS, unit)

            def attention(l):
                pe.wait_ge(evacuated, unit_base(l, "wo"))
                pe.wait_ge(c_ready, l + 1)
                for j in range(NQ):
                    n = QT[j + 1] - QT[j]
                    ins = pe.transpose(ps[0:n, 4 + j // 4, (j % 4) * P:(j % 4 + 1) * P], c_all[:, QT[j]:QT[j + 1]], ident)
                ins.then_inc(c_turned, 1)
                pe.wait_ge(c_tok_ready, l + 1)
                with pe.Fori(0, WT) as pr:
                    pairs = pr + l * WT
                    step = pairs * (2 * NQ)
                    for a in range(2):
                        pe.wait_ge(c_one_ready, pairs * 2 + (a + 1))
                        both(2 * a, ones, c_one[:, a, :]).then_inc(c_spread, 1)
                    pe.wait_ge(v_copied, pairs + 1)
                    for j in range(NQ):
                        n = QT[j + 1] - QT[j]
                        ins = pe.transpose(ps[0:n, 4 + j // 4, (j % 4) * P:(j % 4 + 1) * P], v_pair[:, QT[j]:QT[j + 1]], ident)
                    ins.then_inc(v_turned, 1)

                    def scores(s):
                        j, a = divmod(s, 2)
                        nk = QT[j + 1]
                        if s < 2:
                            pe.wait_ge(q_ready, pairs * 2 + (a + 1))
                            pe.wait_ge(c_key_ready, pairs * 2 + (a + 1))
                        else:
                            pe.wait_ge(score_read, step + (s - 1))
                        parts = [(0, nk)] if nk <= 512 else [(0, HT), (HT, T)]
                        for half, (c0, c1) in enumerate(parts):
                            ins = product(ps[0:nk - QT[j], 2 * a + half, 0:c1 - c0], qz[:, a, QT[j]:nk],
                                          tiles[:, bass.ds((pr + KF) * T + c0, c1 - c0)])
                        ins.then_inc(scored, 1)

                    def turn(s):
                        j, a = divmod(s, 2)
                        n = QT[j + 1] - QT[j]
                        pe.wait_ge(diag_ready, step + (s + 1))
                        if s == 0:
                            pe.wait_ge(vz_ready, pairs + 1)
                        else:
                            pe.wait_ge(prob_t_ready, step + s)
                        for i in range(j + 1):
                            ni = QT[i + 1] - QT[i]
                            ins = product(ps[0:ni, 4 + i // 4, (i % 4) * QT[1]:(i % 4) * QT[1] + n],
                                          prob[0:n, a, QT[i]:QT[i + 1]], diag[0:n, a, 0:n])
                        ins.then_inc(prob_turned, 1)

                    def values(s):
                        j, a = divmod(s, 2)
                        n = QT[j + 1] - QT[j]
                        pe.wait_ge(prob_t_ready, step + (s + 1))
                        if a == 0 and j >= 2:
                            pe.wait_ge(att_read, pairs * NQ + (j - 1))
                        for i in range(j + 1):
                            ni = QT[i + 1] - QT[i]
                            ins = product(ps[:, 6 + j % 2, 0:n], vz[0:ni, a, i, :], prob_t[0:ni, a, i, 0:n],
                                          a == 0 and i == 0, a == 1 and i == j)
                        if a == 1:
                            ins.then_inc(att_done, 1)

                    scores(0)
                    scores(1)
                    for s in range(2 * NQ):
                        turn(s)
                        if s + 2 < 2 * NQ:
                            scores(s + 2)
                        values(s)
                    pe.wait_ge(score_read, step + 2 * NQ)
                    pe.wait_ge(att_read, pairs * NQ + NQ)

            def low_rank(l):
                pe.wait_ge(lora_loaded, 16 * (l + 1))
                pe.wait_ge(lora_in, 3 * (l + 1))
                pe.wait_ge(att_read, WT * NQ * (l + 1))
                for m in range(WT):
                    n = WT * l + m
                    todo = [(WA, decay_done, decay_sig, n), (WA, iclr_done, iclr_sig, n), (MISC, vres_done, vres_sig, n - WT)]
                    for i, (src, done, read, count) in enumerate(todo[:3 if l else 2]):
                        if m:
                            pe.wait_ge(read, count)
                        both(2 * i, lora_w[:, i * WIDTH + m * P:i * WIDTH + (m + 1) * P], tile(src)).then_inc(done, 1)
                    pe.wait_ge(ksq_ready, n + 1)
                    if m:
                        pe.wait_ge(kmax_ready, n)
                    both(6, headsum, sqb[:, m % 2, :]).then_inc(knorm_done, 1)
                pe.wait_ge(iclr_sig, WT * (l + 1))
                for m in range(WT):
                    n = WT * l + m
                    pe.wait_ge(rk_ready, n + 1)
                    if m >= 2:
                        pe.wait_ge(bonus_ready, n - 1)
                    both(2 * (m % 2), headsum, bonus[:, m, :]).then_inc(bonus_done, 1)

            def chunks(l):
                pe.wait_ge(bonus_ready, WT * (l + 1))
                pe.wait_ge(kmax_ready, WT * (l + 1))
                if l:
                    pe.wait_ge(vres_sig, WT * l)
                pe.wait_ge(bd_zero, 2 * (l + 1))

                def chunk(c, b, n):
                    cc = c + l * N_CHUNK
                    pe.wait_ge(ar_built, cc + 1)
                    pe.wait_ge(bkv_built, cc * 4 + 4)
                    pe.wait_ge(v_built, cc + 1)
                    wait(pe, state_ready, cc)
                    wait(pe, o_read, cc)
                    for pr in range(WT):
                        for i in range(2):
                            ins = product(ps[:, pr, i * 256:(i + 1) * 256], bkv[:, b, pr, i * P:(i + 1) * P], ar[:, b, pr, :])
                        ins.then_inc(gram_done, 1)
                    for pr in range(WT):
                        for i in range(3):
                            ins = pe.transpose(ps[:, 4 + pr, i * P:(i + 1) * P], bkv[:, b, pr, i * P:(i + 1) * P], ident)
                        ins.then_inc(turned, 1)
                    pe.wait_ge(off_ready, cc * LEVELS + 1)
                    for pr in range(WT):
                        ins = pe.transpose(ps[:, 0, pr * P:(pr + 1) * P], uo[:, pr, :], ident)
                    ins.then_inc(z0_done, 1)
                    for v in range(1, LEVELS):
                        pe.wait_ge(off_ready, cc * LEVELS + (v + 1))
                        pe.wait_ge(z_ready, cc * 5 + v)
                        if v == 1:
                            pe.wait_ge(tok_ready, cc * WT + WT)
                        for pr in range(WT):
                            ins = product(ps[:, 4, pr * P:(pr + 1) * P], uo[:, pr, :], zm[:, pr, :])
                        ins.then_inc(q_done, 1)
                        pe.wait_ge(qm_ready, cc * 5 + v)
                        pe.wait_ge(y_ready, cc * LEVELS + v)
                        if v < LEVELS - 1:
                            for pr in range(WT):
                                ins = product(ps[:, 6, pr * P:(pr + 1) * P], ym[:, pr, :], qm[:, pr, :])
                            ins.then_inc(zd_done, 1)
                        for pr in range(WT):
                            ins = product(ps[:, 5, pr * P:(pr + 1) * P], qm[:, pr, :], ym[:, pr, :])
                        ins.then_inc(yd_done, 1)
                    pe.wait_ge(gram_ready, cc * WT + WT)
                    for pr in range(WT):
                        product(ps[:, 1, pr * P:(pr + 1) * P], gm[:, b, pr, 256:384], tok[:, b, pr, 256:384], True, False)
                        ins = product(ps[:, 1, pr * P:(pr + 1) * P], ar[:, b, pr, 0:P], hs[:, pr, :], False, True)
                    ins.then_inc(r_done, 1)
                    pe.wait_ge(rb_ready, cc + 1)
                    pe.wait_ge(y_ready, cc * LEVELS + LEVELS)
                    for pr in range(WT):
                        ins = product(ps[:, 2, pr * P:(pr + 1) * P], ym[:, pr, :], rb[:, pr, :])
                    ins.then_inc(sa_done, 1)
                    pe.wait_ge(sa_ready, cc + 1)
                    for pr in range(WT):
                        o = ps[:, 3, pr * P:(pr + 1) * P]
                        product(o, sa[:, pr, :], gm[:, b, pr, 128:256], True, False)
                        product(o, tok[:, b, pr, 256:384], gm[:, b, pr, 384:512], False, False)
                        ins = product(o, hs[:, pr, :], ar[:, b, pr, P:2 * P], False, True)
                    ins.then_inc(o_done, 1)
                    for pr in range(WT):
                        d = ps[:, 7, pr * P:(pr + 1) * P]
                        product(d, tok[:, b, pr, 0:128], sa[:, pr, :], True, False)
                        ins = product(d, tok[:, b, pr, 128:256], tok[:, b, pr, 256:384], False, True)
                    ins.then_inc(hd_done, 1)
                chunk_loop(pe, chunk)

            def head_outputs(l):
                pe.wait_ge(state_ready, N_CHUNK * (l + 1))
                pe.wait_ge(o_read, N_CHUNK * (l + 1))
                pe.wait_ge(gate_loaded, 16 * (l + 1))
                for m in range(WT):
                    n = WT * l + m
                    if m:
                        pe.wait_ge(o_ready, 2 * n)
                    both(0, headsum, tile(R + m)).then_inc(mean_done, 1)
                    both(4, gate_w[:, m * P:(m + 1) * P], tile(GD), True, False)
                    both(4, gate_w[:, WIDTH + m * P:WIDTH + (m + 1) * P], tile(MISC), False, True).then_inc(g_done, 1)
                    for i in range(2):
                        pe.wait_ge(osq_ready, 2 * n + i + 1)
                        both(2 + 4 * i, headsum, sqb[:, i, :]).then_inc(var_done, 1)

            def mixer_out(l):
                base = unit_base(l, "wo")
                pe.wait_ge(o_ready, 2 * WT * (l + 1))

                def unit(k, i):
                    start_unit(i * 2 + k, base)
                    before = (lambda kt: pe.wait_ge(x_lo_ready, DT * (4 * l + 2) + 2 * (kt % WT) + kt // WT + 1)) if k == 0 else None
                    for ins in gemm(slot(base, k), 2, DT, x_hi, x_lo, before):
                        pass
                    ins.then_inc(unit_done, 1)
                units(pe, WO_UNITS, unit)
                statistics(l, 3, base + WO_UNITS)
                pe.wait_ge(root_ready, 6 * l + 4)

            pe.wait_ge(small_loaded, 32)
            for l in range(DEPTH):
                ffn(l, "a", 2 * l, 4 * l, 0)
                projection(l)
                attention(l)
                low_rank(l)
                chunks(l)
                head_outputs(l)
                mixer_out(l)
                ffn(l, "b", 2 * l + 1, 4 * l + 3, 4)

        @block.scalar
        def _(act):
            eps_pre, eps_half, eps_lnx, one = (eps[:, n:n + 1] for n in range(4))

            def copy(dst, src):
                return act.activation(dst, src, ACT.Copy)

            def split_hi(cols, base, k, i=0):
                u = i * 2 + k
                act.wait_ge(raw_loaded[slot(base, k)], i * 16 + 16 * ((base + k) // 2 + 1))
                wait(act, unit_done, u + (base - 1))
                copy(w_hi[:, slot(base, k), 0:cols], raw[:, slot(base, k), 0:cols]).then_inc(hi_ready, 1)

            def square(s, k, i, ap):
                if k == 0:
                    wait(act, stat_done, s)
                    act.activation(acc[:, :], ap, ACT.Square).then_inc(sq_ready, 1)
                else:
                    wait(act, acc_added, i * 2 + ((DT - 1) * s + max(k - 2, 0)))
                    act.activation(sqb[:, k % 2, :], ap, ACT.Square).then_inc(sq_ready, 1)

            def root_of(l, n, scale, bias):
                act.wait_ge(stat_done, 6 * l + n + 1)
                act.activation(halves(root[:, :]), pair(norm_bank(l, n)), ACT.Sqrt, bias=bias, scale=scale).then_inc(root_ready, 1)

            def prepare(l, g, n, units_before):
                wait(act, unit_done, units_before)
                for m in range(DT):
                    wait(act, h_ready, post_count(l, g) and post_count(l, g) - DT + m + 1)
                    act.activation(x_hi[:, m, :], h[:, m, :], ACT.Copy, scale=par(l, GAIN + n * DT + m)).then_inc(x_hi_ready, 1)
                    square(6 * l + n, m, 0, h[:, m, :])

            def ffn(l, which, f, n):
                root_of(l, n, 1.0 / D_MODEL, eps_pre)
                for fh in range(2):
                    base = unit_base(l, which) + fh * (FH + DT)

                    def unit_in(k, i):
                        u, q = i * 2 + k, slot(base, k)
                        act.wait_ge(gs_ready, u + (FH * (2 * f + fh) + 1))
                        act.activation(sg[:, q, :], gs[:, q, :], ACT.Silu).then_inc(sg_ready, 1)
                        if k == FH - 1:
                            split_hi(OUT_UNIT, base, FH)
                        else:
                            split_hi(UNIT, base, k + 1, i)
                        act.wait_ge(hid_ready, u + (FH * (2 * f + fh) + 1))
                        copy(hid_hi[:, u, :], hid[:, q, :]).then_inc(hid_hi_ready, 1)

                    def unit_out(k, i):
                        u = i * 2 + k
                        if k < DT - 1:
                            split_hi(OUT_UNIT, base + FH, k + 1, i)
                        elif not (l == DEPTH - 1 and which == "b" and fh == 1):
                            split_hi(UNIT, base, FH + DT)
                        if fh == 1:
                            act.wait_ge(evacuated, u + (base + FH + 1))
                            square(6 * l + n + 1, k, i, y_ffn[:, u, :])

                    units(act, FH, unit_in)
                    units(act, DT, unit_out)
                root_of(l, n + 1, 4.0 / D_MODEL, eps_half)

            def projection(l):
                base = unit_base(l, "proj")
                root_of(l, 2, 1.0 / D_MODEL, eps_pre)

                def unit(k, i):
                    if k < PROJ_UNITS - 1:
                        split_hi(UNIT // 2 if k == PROJ_UNITS - 2 else UNIT, base, k + 1, i)
                units(act, PROJ_UNITS, unit)

            def attention(l):
                row = slice(FORGET_ROW, FORGET_ROW + HEADS)
                act.wait_ge(fg_abs, l + 1)
                act.activation(fg[row, 1, :], fg[row, 1, :], ACT.Exp).then_inc(act_step, 1)
                act.wait_ge(act_step, l + 1)
                act.activation(fg[row, 1, :], fg[row, 1, :], ACT.Ln, bias=one[row, :]).then_inc(fg_exp, 1)
                act.wait_ge(c_turned, l + 1)
                for j in range(NQ):
                    n = QT[j + 1] - QT[j]
                    c0 = (j % 4) * P + FORGET_ROW
                    ins = copy(c_tok[0:n, j, :], ps[0:n, 4 + j // 4, c0:c0 + HEADS])
                ins.then_inc(c_tok_ready, 1)
                act.wait_ge(att_zero, l + 1)
                with act.Fori(0, WT) as pr:
                    pairs = pr + l * WT
                    step = pairs * (2 * NQ)
                    for a in range(2):
                        rows = slice(a * HEAD, (a + 1) * HEAD)
                        act.activation(qz[rows, a, :], tiles[rows, bass.ds((pr + QF) * T, T)], ACT.Copy, scale=HEAD ** -0.5).then_inc(q_ready, 1)
                    copy(v_pair[:, :], tiles[:, bass.ds((pr + VF) * T, T)]).then_inc(v_copied, 1)
                    for a in range(2):
                        act.wait_ge(c_spread, pairs * 2 + (a + 1))
                        copy(halves(c_key[:, a, :]), pair(2 * a)).then_inc(c_key_ready, 1)
                    act.wait_ge(v_turned, pairs + 1)
                    for a in range(2):
                        cols = slice(a * HEAD, (a + 1) * HEAD)
                        copy(vz[0:QT[1], a, 0:4, cols], ps[0:QT[1], 4, :].rearrange("p (j c) -> p j c", j=4)[:, :, cols])
                        ins = copy(vz[0:T - QT[4], a, 4, cols], ps[0:T - QT[4], 5, cols])
                    ins.then_inc(vz_ready, 1)

                    def exponent(s):
                        j, a = divmod(s, 2)
                        n = QT[j + 1] - QT[j]
                        act.wait_ge(max_ready, step + (s + 1))
                        if s >= 2:
                            act.wait_ge(prob_turned, step + (s - 1))
                        act.activation(prob[0:n, a, 0:QT[j + 1]], score[0:n, a, 0:QT[j + 1]], ACT.Exp,
                                       bias=neg_max[0:n, a:a + 1], accum_out=row_sum[0:n, a:a + 1]).then_inc(prob_ready, 1)

                    def by_key(s):
                        j, a = divmod(s, 2)
                        n = QT[j + 1] - QT[j]
                        act.wait_ge(prob_turned, step + (s + 1))
                        if j:
                            act.wait_ge(att_done, pairs * NQ + j)
                        m = min(j + 1, 4)
                        ins = copy(prob_t[0:QT[1], a, 0:m, 0:n],
                                   ps[0:QT[1], 4, 0:4 * QT[1]].rearrange("p (i c) -> p i c", i=4)[:, 0:m, 0:n])
                        if j == 4:
                            ins = copy(prob_t[0:n, a, 4, 0:n], ps[0:n, 5, 0:n])
                        ins.then_inc(prob_t_ready, 1)

                    exponent(0)
                    for s in range(2 * NQ):
                        if s + 1 < 2 * NQ:
                            exponent(s + 1)
                        by_key(s)
                    act.wait_ge(att_done, pairs * NQ + NQ)

            def low_rank(l):
                act.wait_ge(evacuated, unit_base(l, "wo"))
                act.wait_ge(tiles_ready, 15 * (l + 1))
                act.activation(tile(WA)[0:64, :], tile(WA)[0:64, :], ACT.Tanh).then_inc(lora_in, 1)
                act.activation(tile(GD), tile(GD), ACT.Sigmoid).then_inc(lora_in, 1)
                act.activation(tile(MISC)[0:32, :], tile(MISC)[0:32, :], ACT.Sigmoid).then_inc(lora_in, 1)
                for m in range(WT):
                    n = WT * l + m
                    if m >= 2:
                        act.wait_ge(knorm_done, n - 1)
                    act.activation(sqb[:, m % 2, :], tile(K + m), ACT.Square, scale=par(l, KKG + m)).then_inc(ksq_ready, 1)
                    act.wait_ge(decay_done, n + 1)
                    act.activation(halves(ll[:, m, :]), pair(0), ACT.Sigmoid, bias=par(l, DBIAS + m)).then_inc(decay_sig, 1)
                    act.wait_ge(iclr_done, n + 1)
                    act.activation(halves(aa[:, m, :]), pair(2), ACT.Sigmoid, bias=par(l, IBIAS + m)).then_inc(iclr_sig, 1)
                    act.wait_ge(kmax_ready, n + 1)
                    act.activation(root[:, :], tmp[1], ACT.Sqrt).then_inc(kroot_ready, 1)
                    if l:
                        act.wait_ge(vres_done, n - WT + 1)
                        if m:
                            act.wait_ge(v_mixed, n - WT)
                        act.activation(halves(tmp[0]), pair(4), ACT.Sigmoid, bias=par(l, VBIAS + m)).then_inc(vres_sig, 1)

            def chunks(l):
                act.wait_ge(bonus_ready, WT * (l + 1))
                act.wait_ge(bd_zero, 2 * (l + 1))

                def prepare_chunk(c, b, n):
                    tokens = bass.ds(c * CHUNK, n)
                    act.activation(e_fwd[b][:, :, 1:n + 1], ll[:, :, tokens], ACT.Exp, scale=-DECAY)
                    act.activation(e_bwd[b][:, :, 0:n], ll[:, :, tokens], ACT.Exp, scale=DECAY).then_inc(e_ready, 1)
                    for a in range(2):
                        ins = copy(bkv[a * HEAD:(a + 1) * HEAD, b, :, 2 * P + a * HEAD:2 * P + a * HEAD + n],
                                   group(V, p0=a * HEAD, p1=(a + 1) * HEAD)[:, :, tokens])
                    ins.then_inc(v_built, 1)

                def copy4(dst, bank):
                    return copy(dst[:, :, :], ps[:, bank, :].rearrange("p (m c) -> p m c", m=WT))

                def chunk(c, b, n):
                    cc = c + l * N_CHUNK
                    if isinstance(c, int) and c == 0:
                        prepare_chunk(0, 0, CHUNK)
                    for pr in range(WT):
                        act.wait_ge(turned, cc * WT + (pr + 1))
                        copy(tok[:, b, pr, :], ps[:, 4 + pr, 0:3 * P]).then_inc(tok_ready, 1)
                    if not (isinstance(c, int) and c == N_CHUNK - 1):
                        wait(act, state_ready, cc)
                        prepare_chunk(c + 1, 1 - b, LAST if isinstance(c, int) and c == N_CHUNK - 2 else CHUNK)
                    for v in range(1, LEVELS):
                        act.wait_ge(q_done, cc * 5 + v)
                        copy4(qm, 4).then_inc(qm_ready, 1)
                    act.wait_ge(r_done, cc + 1)
                    copy4(rb, 1).then_inc(rb_ready, 1)
                    act.wait_ge(sa_done, cc + 1)
                    copy4(sa, 2).then_inc(sa_ready, 1)
                    act.wait_ge(o_done, cc + 1)
                    for a in range(2):
                        rows = slice(a * HEAD, (a + 1) * HEAD)
                        ins = copy(group(R, p0=a * HEAD, p1=(a + 1) * HEAD)[:, :, bass.ds(c * CHUNK, n)],
                                   ps[rows, 3, :].rearrange("p (m c) -> p m c", m=WT)[:, :, a * HEAD:a * HEAD + n])
                    ins.then_inc(o_read, 1)
                chunk_loop(act, chunk)

            def head_outputs(l):
                g = 4 * l + 2
                for m in range(WT):
                    n = WT * l + m
                    act.wait_ge(oc_ready, n + 1)
                    act.activation(sqb[:, 0, :], tile(R + m), ACT.Square).then_inc(osq_ready, 1)
                    act.activation(sqb[:, 1, :], tile(QF + m), ACT.Square).then_inc(osq_ready, 1)
                    for i in range(2):
                        act.wait_ge(var_done, 2 * n + i + 1)
                        act.activation(halves(tmp[i]), pair(2 + 4 * i), ACT.Sqrt, bias=(eps_lnx, eps_pre)[i], scale=1.0 / HEAD).then_inc(oroot_ready, 1)
                    for i in range(2):
                        act.wait_ge(o_ready, 2 * n + i + 1)
                        copy(x_hi[:, m + WT * i, :], tile((R, QF)[i] + m)).then_inc(x_hi_ready, 1)

            def mixer_out(l):
                base = unit_base(l, "wo")

                def unit(k, i):
                    if k < WO_UNITS - 1:
                        split_hi(UNIT, base, k + 1, i)
                    else:
                        split_hi(UNIT, base, WO_UNITS)
                    act.wait_ge(evacuated, i * 2 + (base + k + 1))
                    for j in range(2):
                        square(6 * l + 3, 2 * k + j, 0, y_mix[:, 2 * k + j, :])
                for k in range(WO_UNITS):
                    unit(k, 0)
                root_of(l, 3, 1.0 / D_MODEL, eps_pre)

            act.wait_ge(small_loaded, 32)
            act.wait_ge(eps_set, 4)
            act.wait_ge(h_loaded, 16)
            split_hi(UNIT, 0, 0)
            for l in range(DEPTH):
                prepare(l, 0, 0, unit_base(l, "a"))
                ffn(l, "a", 2 * l, 0)
                prepare(l, 1, 2, unit_base(l, "proj"))
                projection(l)
                attention(l)
                low_rank(l)
                chunks(l)
                act.wait_ge(mean_done, WT * l + 1)
                split_hi(UNIT, unit_base(l, "wo"), 0)
                head_outputs(l)
                mixer_out(l)
                prepare(l, 3, 4, unit_base(l, "b"))
                ffn(l, "b", 2 * l + 1, 4)

        @block.vector
        def _(dve):
            links = [0]

            def link(ins):
                links[0] += 1
                ins.then_inc(dve_step, 1)
                dve.wait_ge(dve_step, links[0])

            def split_lo(cols, base, k, i=0):
                q = slot(base, k)
                dve.wait_ge(hi_ready, i * 2 + (base + k + 1))
                dve.tensor_tensor(w_lo[:, q, 0:cols], raw[:, q, 0:cols], w_hi[:, q, 0:cols], ALU.subtract).then_inc(w_split, 1)

            def inverse_rms(l, n, dst):
                dve.wait_ge(root_ready, 6 * l + n + 1)
                dve.reciprocal(dst[:, :], root[:, :]).then_inc(rs_ready, 1)
                dve.wait_ge(rs_ready, 6 * l + n + 1)

            def x_lo_of(l, g, n, m):
                dve.wait_ge(x_hi_ready, DT * (4 * l + g) + m + 1)
                dve.scalar_tensor_tensor(x_lo[:, m, :], h[:, m, :], par(l, GAIN + n * DT + m), x_hi[:, m, :],
                                         ALU.mult, ALU.subtract).then_inc(x_lo_ready, 1)

            def update(l, post, y, following):
                count = DT * (3 * l + post)
                for m in range(DT):
                    dve.wait_ge(y_scaled, count + m + 1)
                    dve.scalar_tensor_tensor(h[:, m, :], y[:, m, :], par(l, GAIN + (2 * post + 1) * DT + m), h[:, m, :],
                                             ALU.mult, ALU.add).then_inc(h_ready, 1)
                    if m and following:
                        x_lo_of(*following, m - 1)
                if following:
                    x_lo_of(*following, DT - 1)

            def ffn(l, which, f, n):
                inverse_rms(l, n, rs_pre)
                for fh in range(2):
                    base = unit_base(l, which) + fh * (FH + DT)

                    def unit_in(k, i):
                        u, q = i * 2 + k, slot(base, k)
                        e = u + (FH * (2 * f + fh) + 1)
                        dve.wait_ge(gate_done, e)
                        dve.tensor_tensor(halves(gs[:, q, :]), pair(4 * q), halves(rs_pre[:, :]), ALU.mult).then_inc(gs_ready, 1)
                        if k == FH - 1:
                            split_lo(OUT_UNIT, base, FH)
                        else:
                            split_lo(UNIT, base, k + 1, i)
                        dve.wait_ge(unit_done, u + (base + 1))
                        dve.tensor_tensor(halves(us[:, q, :]), pair(4 * q + 2), halves(rs_pre[:, :]), ALU.mult).then_inc(evacuated, 1)
                        dve.wait_ge(hid_hi_ready, e)
                        dve.tensor_tensor(hid_lo[:, u, :], hid[:, q, :], hid_hi[:, u, :], ALU.subtract).then_inc(hid_lo_ready, 1)

                    def unit_out(k, i):
                        u, q = i * 2 + k, slot(base + FH, k)
                        if k < DT - 1:
                            split_lo(OUT_UNIT, base + FH, k + 1, i)
                        elif not (l == DEPTH - 1 and which == "b" and fh == 1):
                            split_lo(UNIT, base, FH + DT)
                        dve.wait_ge(unit_done, u + (base + FH + 1))
                        if fh == 0:
                            dve.tensor_copy(halves(y_ffn[:, u, :]), pair(4 * q)).then_inc(evacuated, 1)
                        else:
                            dve.tensor_tensor(halves(y_ffn[:, u, :]), pair(4 * q), halves(y_ffn[:, u, :]), ALU.add).then_inc(evacuated, 1)

                    units(dve, FH, unit_in)
                    units(dve, DT, unit_out)
                inverse_rms(l, n + 1, rs_post)

            def projection(l):
                base = unit_base(l, "proj")
                inverse_rms(l, 2, rs_pre)

                def next_split(k, i):
                    if k < PROJ_UNITS - 1:
                        split_lo(UNIT // 2 if k == PROJ_UNITS - 2 else UNIT, base, k + 1, i)

                def heads_unit(k, i):
                    next_split(k, i)
                    dve.wait_ge(unit_done, i * 2 + (base + k + 1))
                    for j in range(2):
                        dst = tiles[:, bass.ds((i * 4 + (2 * k + j)) * T, T)] if not isinstance(i, int) else tile(2 * k + j)
                        ins = dve.tensor_tensor(halves(dst), pair(4 * slot(base, k) + 2 * j), halves(rs_pre[:, :]), ALU.mult)
                    ins.then_inc(evacuated, 1)

                def shifted_unit(k, i):
                    single = k == PROJ_UNITS - 1
                    next_split(k, i)
                    u = i * 2 + k
                    dve.wait_ge(unit_done, u + (base + 1))
                    wait(dve, tiles_ready, i * 4 + (15 * l + 2 * k - R))
                    for j in range(1 if single else 2):
                        ins = dve.tensor_tensor(halves(shifted[j][:, 1:T + 1]), pair(4 * slot(base, k) + 2 * j), halves(rs_pre[:, :]), ALU.mult)
                    ins.then_inc(evacuated, 1)
                    for j in range(1 if single else 2):
                        number = 2 * k + j - R
                        dve.wait_ge(delta_ready, i * 4 + (15 * l + number + 1))
                        if isinstance(i, int):
                            dst, mu = tile(R + number), par(l, MU + number)
                        else:
                            dst = tiles[:, bass.ds((i * 4 + (R + number)) * T, T)]
                            mu = prm[:, bass.ds(i * 4 + (l * N_PAR + MU + number), 1)]
                        dve.scalar_tensor_tensor(dst, delta[j], mu, shifted[j][:, 1:T + 1], ALU.mult, ALU.add).then_inc(tiles_ready, 1)

                for j in range(2):
                    link(dve.memset(shifted[j][:, 0:1], 0.0))
                units(dve, R // 2, heads_unit)
                units(dve, PROJ_UNITS - R // 2, shifted_unit, R // 2)

            def attention(l):
                row = slice(FORGET_ROW, FORGET_ROW + HEADS)
                link(dve.memset(c_all[:, :], 0.0))
                dve.wait_ge(tiles_ready, 15 * (l + 1))
                link(dve.tensor_scalar(fg[row, 0, :], tile(MISC)[row, :], par(l, FBIAS, FORGET_ROW, FORGET_ROW + HEADS), None, ALU.add))
                dve.scalar_tensor_tensor(fg[row, 1, :], fg[row, 0, :], -1.0, fg[row, 0, :], ALU.mult, ALU.min).then_inc(fg_abs, 1)
                dve.wait_ge(fg_exp, l + 1)
                link(dve.scalar_tensor_tensor(fg[row, 0, :], fg[row, 0, :], 0.0, fg[row, 1, :], ALU.min, ALU.subtract))
                dve.tensor_tensor_scan(c_all[row, :], cst[row, ONES:ONES + 1].broadcast_to([HEADS, T]), fg[row, 0, :], 0.0,
                                       ALU.mult, ALU.add).then_inc(c_ready, 1)
                dve.wait_ge(c_ready, l + 1)
                dve.wait_ge(c_tok_ready, l + 1)
                with dve.Fori(0, WT) as pr:
                    pairs = pr + l * WT
                    step = pairs * (2 * NQ)
                    for a in range(2):
                        dve.tensor_scalar(c_one[:, a, :], c_all[:, :], cst[:, bass.ds(pr * 2 + (IDENT + FORGET_ROW + a), 1)], -1.0,
                                          ALU.mult, ALU.mult).then_inc(c_one_ready, 1)

                    def soft(s):
                        j, a = divmod(s, 2)
                        nk = QT[j + 1]
                        n = nk - QT[j]
                        dve.wait_ge(scored, step + (s + 1))
                        c_query = c_tok[0:n, j, bass.ds(pr * 2 + a, 1)]
                        if nk <= 512:
                            dve.scalar_tensor_tensor(score[0:n, a, 0:nk], ps[0:n, 2 * a, 0:nk], c_query, c_key[0:n, a, 0:nk],
                                                     ALU.add, ALU.add).then_inc(score_read, 1)
                        else:
                            dve.scalar_tensor_tensor(halves(score[0:n, a, :]), ps[0:n, 2 * a:2 * a + 2, 0:HT], c_query, halves(c_key[0:n, a, :]),
                                                     ALU.add, ALU.add).then_inc(score_read, 1)
                        dve.wait_ge(score_read, step + (s + 1))
                        own = score[0:n, a, QT[j]:nk]
                        dve.tensor_tensor(own, own, cst[0:n, CAUSAL:CAUSAL + n], ALU.add).then_inc(masked, 1)
                        dve.wait_ge(masked, step + (s + 1))
                        dve.tensor_reduce(neg_max[0:n, a:a + 1], score[0:n, a, 0:nk], AX.X, ALU.max, negate=True).then_inc(max_ready, 1)

                    def scale(s):
                        j, a = divmod(s, 2)
                        n = QT[j + 1] - QT[j]
                        dve.wait_ge(prob_ready, step + (s + 1))
                        dve.reciprocal(inv_sum[0:n, a:a + 1], row_sum[0:n, a:a + 1]).then_inc(inv_ready, 1)
                        dve.wait_ge(inv_ready, step + (s + 1))
                        if s >= 2:
                            dve.wait_ge(prob_turned, step + (s - 1))
                        dve.tensor_scalar(diag[0:n, a, 0:n], cst[0:n, IDENT:IDENT + n], inv_sum[0:n, a:a + 1], None, ALU.mult).then_inc(diag_ready, 1)

                    def read(j):
                        n = QT[j + 1] - QT[j]
                        dve.wait_ge(att_done, pairs * NQ + (j + 1))
                        dve.tensor_copy(tiles[:, bass.ds((pr + QF) * T + QT[j], n)], ps[:, 6 + j % 2, 0:n]).then_inc(att_read, 1)

                    soft(0)
                    for s in range(2 * NQ):
                        if s + 1 < 2 * NQ:
                            soft(s + 1)
                        scale(s)
                        if s % 2 == 0 and s:
                            read(s // 2 - 1)
                    read(NQ - 1)
                    dve.wait_ge(prob_turned, step + 2 * NQ)

            def low_rank(l):
                for m in range(WT):
                    n = WT * l + m
                    dve.wait_ge(decay_sig, n + 1)
                    link(dve.tensor_tensor_scan(ll[:, m, :], cst[:, RESET:RESET + T], ll[:, m, :], 0.0, ALU.mult, ALU.add))
                    link(dve.tensor_scalar(kk[:, m, :], tile(K + m), par(l, KKG + m), None, ALU.mult))
                    dve.wait_ge(knorm_done, n + 1)
                    dve.tensor_scalar(halves(tmp[1]), pair(6), 1e-24, None, ALU.max).then_inc(kmax_ready, 1)
                    dve.wait_ge(kroot_ready, n + 1)
                    link(dve.reciprocal(tmp[2], root[:, :]))
                    link(dve.tensor_tensor(kk[:, m, :], kk[:, m, :], tmp[2], ALU.mult))
                    dve.wait_ge(iclr_sig, n + 1)
                    link(dve.tensor_scalar(tmp[2], aa[:, m, :], 1.0, par(l, KAG + m), ALU.subtract, ALU.mult))
                    dve.wait_ge(ksq_ready, n + 1)
                    link(dve.scalar_tensor_tensor(tile(K + m), tmp[2], 1.0, tile(K + m), ALU.add, ALU.mult))
                    link(dve.tensor_tensor(aa[:, m, :], kk[:, m, :], aa[:, m, :], ALU.mult))
                    if l == 0:
                        link(dve.tensor_copy(v_first[:, m, :], tile(V + m)))
                    else:
                        dve.wait_ge(vres_sig, n - WT + 1)
                        link(dve.tensor_tensor(tmp[2], v_first[:, m, :], tile(V + m), ALU.subtract))
                        dve.tensor_tensor(tmp[2], tmp[2], tmp[0], ALU.mult).then_inc(v_mixed, 1)
                        dve.wait_ge(v_mixed, n - WT + 1)
                        link(dve.tensor_tensor(tile(V + m), tile(V + m), tmp[2], ALU.add))
                    dve.scalar_tensor_tensor(bonus[:, m, :], tile(R + m), par(l, RKG + m), tile(K + m), ALU.mult, ALU.mult).then_inc(rk_ready, 1)
                for m in range(WT):
                    n = WT * l + m
                    dve.wait_ge(bonus_done, n + 1)
                    dve.tensor_tensor(halves(bonus[:, m, :]), pair(2 * (m % 2)), halves(tile(V + m)), ALU.mult).then_inc(bonus_ready, 1)
                dve.wait_ge(bonus_ready, WT * (l + 1))

            def chunks(l):
                dve.wait_ge(att_read, WT * NQ * (l + 1))
                for b in range(2):
                    dve.memset(e_fwd[b][:, :, 0:1], 1.0)
                dve.memset(hs[:, :, :], 0.0)
                dve.memset(ar[:, :, :, :], 0.0).then_inc(bd_zero, 1)
                dve.wait_ge(bd_zero, 2 * (l + 1))

                def build_ar(c, b, n, cc):
                    tokens = bass.ds(c * CHUNK, n)
                    dve.wait_ge(e_ready, cc + 1)
                    for a in range(2):
                        rows = slice(a * HEAD, (a + 1) * HEAD)
                        dve.scalar_tensor_tensor(ar[rows, b, :, a * HEAD:a * HEAD + n], kk[rows, :, tokens], -1.0, e_fwd[b][rows, :, 0:n], ALU.mult, ALU.mult)
                        ins = dve.tensor_tensor(ar[rows, b, :, P + a * HEAD:P + a * HEAD + n],
                                                group(R, p0=a * HEAD, p1=(a + 1) * HEAD)[:, :, tokens], e_fwd[b][rows, :, 1:n + 1], ALU.mult)
                    ins.then_inc(ar_built, 1)

                def bank4(bank):
                    return ps[:, bank, :].rearrange("p (m c) -> p m c", m=WT)

                def chunk(c, b, n):
                    cc = c + l * N_CHUNK
                    if isinstance(c, int) and c == 0:
                        build_ar(0, 0, CHUNK, cc)
                    for pr in range(WT):
                        dve.wait_ge(gram_done, cc * WT + (pr + 1))
                        dve.tensor_tensor(gm[:, b, pr, :].rearrange("p (i c) -> p i c", i=2), ps[:, pr, :].rearrange("p (i c) -> p i c", i=2),
                                          spread(cst[:, PAIRMASK:PAIRMASK + 256], 2), ALU.mult).then_inc(gram_ready, 1)
                    dve.wait_ge(off_ready, cc * LEVELS + 1)
                    dve.tensor_tensor(ym[:, :, :], uo[:, :, :], ident4, ALU.add).then_inc(y_ready, 1)
                    dve.wait_ge(z0_done, cc + 1)
                    dve.tensor_tensor(zm[:, :, :], bank4(0), ident4, ALU.add).then_inc(z_ready, 1)
                    for v in range(1, LEVELS):
                        if v < LEVELS - 1:
                            dve.wait_ge(zd_done, cc * 4 + v)
                            dve.tensor_tensor(zm[:, :, :], bank4(6), zm[:, :, :], ALU.add).then_inc(z_ready, 1)
                        dve.wait_ge(yd_done, cc * 5 + v)
                        dve.tensor_tensor(ym[:, :, :], bank4(5), ym[:, :, :], ALU.add).then_inc(y_ready, 1)
                        if v == 2 and not (isinstance(c, int) and c == N_CHUNK - 1):
                            build_ar(c + 1, 1 - b, LAST if isinstance(c, int) and c == N_CHUNK - 2 else CHUNK, cc + 1)
                    dve.wait_ge(hd_done, cc + 1)
                    dve.tensor_tensor(hs[:, :, :], bank4(7), hs[:, :, :], ALU.add).then_inc(h_added, 1)
                    dve.wait_ge(h_added, cc + 1)
                    dve.tensor_tensor(hs[:, :, :], hs[:, :, :], e_fwd[b][:, :, n:n + 1].broadcast_to([P, WT, P]), ALU.mult).then_inc(state_ready, 1)
                chunk_loop(dve, chunk)

            def head_outputs(l):
                g = 4 * l + 2
                for m in range(WT):
                    n = WT * l + m
                    o, of = tile(R + m), tile(QF + m)
                    dve.wait_ge(mean_done, n + 1)
                    dve.scalar_tensor_tensor(halves(o), pair(0), -1.0 / HEAD, halves(o), ALU.mult, ALU.add).then_inc(oc_ready, 1)
                    dve.wait_ge(oroot_ready, 2 * n + 1)
                    link(dve.reciprocal(tmp[2], tmp[0]))
                    link(dve.tensor_tensor(o, o, tmp[2], ALU.mult))
                    link(dve.tensor_scalar(o, o, par(l, LNW + m), par(l, LNB + m), ALU.mult, ALU.add))
                    link(dve.tensor_tensor(o, o, bonus[:, m, :], ALU.add))
                    dve.wait_ge(g_done, n + 1)
                    dve.tensor_tensor(halves(o), halves(o), pair(4), ALU.mult).then_inc(o_ready, 1)
                    dve.wait_ge(oroot_ready, 2 * n + 2)
                    link(dve.reciprocal(tmp[2], tmp[1]))
                    dve.scalar_tensor_tensor(of, of, par(l, FOXG + m), tmp[2], ALU.mult, ALU.mult).then_inc(o_ready, 1)
                    for i, src in enumerate((o, of)):
                        dve.wait_ge(x_hi_ready, DT * g + 2 * m + i + 1)
                        dve.tensor_tensor(x_lo[:, m + WT * i, :], src, x_hi[:, m + WT * i, :], ALU.subtract).then_inc(x_lo_ready, 1)

            def mixer_out(l):
                base = unit_base(l, "wo")

                for k in range(WO_UNITS):
                    q = slot(base, k)
                    split_lo(UNIT, base, k + 1)
                    dve.wait_ge(unit_done, base + k + 1)
                    for j in range(2):
                        ins = dve.tensor_copy(halves(y_mix[:, 2 * k + j, :]), pair(4 * q + 2 * j))
                    ins.then_inc(evacuated, 1)
                inverse_rms(l, 3, rs_post)

            dve.memset(eps[:, 0:1], NORM_EPS).then_inc(eps_set, 1)
            dve.memset(eps[:, 1:2], 4 * NORM_EPS).then_inc(eps_set, 1)
            dve.memset(eps[:, 2:3], LNX_EPS).then_inc(eps_set, 1)
            dve.memset(eps[:, 3:4], 1.0).then_inc(eps_set, 1)
            dve.wait_ge(small_loaded, 32)
            dve.wait_ge(h_loaded, 16)
            split_lo(UNIT, 0, 0)
            for m in range(DT):
                x_lo_of(0, 0, 0, m)
            for l in range(DEPTH):
                ffn(l, "a", 2 * l, 0)
                update(l, 0, y_ffn, (l, 1, 2))
                projection(l)
                attention(l)
                low_rank(l)
                chunks(l)
                split_lo(UNIT, unit_base(l, "wo"), 0)
                head_outputs(l)
                mixer_out(l)
                update(l, 1, y_mix, (l, 3, 4))
                ffn(l, "b", 2 * l + 1, 4)
                update(l, 2, y_ffn, (l + 1, 0, 0) if l + 1 < DEPTH else None)

        @block.gpsimd
        def _(pool):
            def add_squares(s, k, i=0):
                if k == 0:
                    return
                count = i * 2 + ((DT - 1) * s + k)
                pool.wait_ge(sq_ready, i * 2 + (DT * s + k + 1))
                wait(pool, acc_added, count - 1)
                pool.tensor_tensor(acc[:, :], acc[:, :], sqb[:, k % 2, :], ALU.add).then_inc(acc_added, 1)

            def ffn(l, which, f, n):
                for m in range(DT):
                    add_squares(6 * l + n, m)
                for fh in range(2):
                    base = unit_base(l, which) + fh * (FH + DT)

                    def unit_in(k, i):
                        u, q = i * 2 + k, slot(base, k)
                        pool.wait_ge(sg_ready, u + (FH * (2 * f + fh) + 1))
                        pool.wait_ge(evacuated, u + (base + 1))
                        pool.tensor_tensor(hid[:, q, :], sg[:, q, :], us[:, q, :], ALU.mult).then_inc(hid_ready, 1)
                    units(pool, FH, unit_in)
                    if fh == 1:
                        units(pool, DT, lambda k, i: add_squares(6 * l + n + 1, k, i))

            def scale_y(l, post, y):
                pool.wait_ge(rs_ready, 6 * l + 2 * post + 2)
                for m in range(DT):
                    pool.tensor_tensor(y[:, m, :], y[:, m, :], rs_post[:, :], ALU.mult).then_inc(y_scaled, 1)

            def projection(l):
                for m in range(DT):
                    add_squares(6 * l + 2, m)
                base = unit_base(l, "proj")

                def unit(k, i):
                    pool.wait_ge(evacuated, i * 2 + (base + k + 1))
                    for j in range(1 if k == PROJ_UNITS - 1 else 2):
                        pool.tensor_tensor(delta[j], shifted[j][:, 0:T], shifted[j][:, 1:T + 1], ALU.subtract).then_inc(delta_ready, 1)
                units(pool, PROJ_UNITS - R // 2, unit, R // 2)

            def chunks(l):
                pool.wait_ge(att_read, WT * NQ * (l + 1))
                pool.memset(bkv[:, :, :, :], 0.0).then_inc(bd_zero, 1)
                pool.wait_ge(bd_zero, 2 * (l + 1))
                pool.wait_ge(bonus_ready, WT * (l + 1))

                def build_bk(c, b, n, cc):
                    tokens = bass.ds(c * CHUNK, n)
                    pool.wait_ge(e_ready, cc + 1)
                    for a in range(2):
                        rows = slice(a * HEAD, (a + 1) * HEAD)
                        for i, src in enumerate((aa[rows, :, :], group(K, p0=a * HEAD, p1=(a + 1) * HEAD))):
                            pool.tensor_tensor(bkv[rows, b, :, i * P + a * HEAD:i * P + a * HEAD + n], src[:, :, tokens],
                                               e_bwd[b][rows, :, 0:n], ALU.mult).then_inc(bkv_built, 1)
                            pool.wait_ge(bkv_built, cc * 4 + (2 * a + i + 1))

                def chunk(c, b, n):
                    cc = c + l * N_CHUNK
                    if isinstance(c, int) and c == 0:
                        build_bk(0, 0, CHUNK, cc)
                    pool.wait_ge(gram_ready, cc * WT + WT)
                    for v in range(LEVELS):
                        if v == 1:
                            pool.wait_ge(z0_done, cc + 1)
                            pool.wait_ge(y_ready, cc * LEVELS + 1)
                        if v > 1:
                            pool.wait_ge(q_done, cc * 5 + (v - 1))
                        pool.tensor_tensor(uo[:, :, :], gm[:, b, :, 0:P], spread(cst[:, LEVEL + v * P:LEVEL + (v + 1) * P], WT), ALU.mult).then_inc(off_ready, 1)
                        if v == 2 and not (isinstance(c, int) and c == N_CHUNK - 1):
                            pool.wait_ge(off_ready, cc * LEVELS + 3)
                            build_bk(c + 1, 1 - b, LAST if isinstance(c, int) and c == N_CHUNK - 2 else CHUNK, cc + 1)
                chunk_loop(pool, chunk)

            for l in range(DEPTH):
                ffn(l, "a", 2 * l, 0)
                scale_y(l, 0, y_ffn)
                projection(l)
                pool.wait_ge(evacuated, unit_base(l, "wo"))
                pool.wait_ge(tiles_ready, 15 * (l + 1))
                pool.memset(qz[:, :, :], 0.0)
                pool.memset(vz[:, :, :, :], 0.0).then_inc(att_zero, 1)
                chunks(l)
                for m in range(DT):
                    add_squares(6 * l + 3, m)
                scale_y(l, 1, y_mix)
                ffn(l, "b", 2 * l + 1, 4)
                scale_y(l, 2, y_ffn)


_OUT = (P, DT, SEQ)


def constants():
    c = np.zeros((P, N_CONST), np.float32)
    s, t = np.arange(P)[:, None], np.arange(P)[None, :]
    same = s // HEAD == t // HEAD
    c[:, IDENT:IDENT + P] = s == t
    c[:, ONES:ONES + P] = 1
    c[:, HEADSUM:HEADSUM + P] = same
    c[:, CAUSAL:CAUSAL + P] = np.where(t > s, NEG, 0)
    c[:, PAIRMASK:PAIRMASK + P] = same & (s < t)
    c[:, PAIRMASK + P:PAIRMASK + 2 * P] = same & (s <= t)
    for v in range(LEVELS):
        b = 1 << v
        c[:, LEVEL + v * P:LEVEL + (v + 1) * P] = same & (s < t) & (s // (2 * b) == t // (2 * b)) & (s // b != t // b)
    c[:, RESET:RESET + T] = np.arange(T)[None, :] % CHUNK != 0
    return c


def lay_out(x, meta_tokens, norm_gains, ffn_w_in, ffn_w_out, w_in, w_in_vres, shift_mu, shift_mu_vres,
            decay_up, decay_bias, iclr_up, iclr_bias, gate_up, vres_up, vres_bias, k_k, k_a, r_k,
            ln_x_w, ln_x_b, forget_bias, fox_out_gain, w_out):
    f = np.float32
    tokens = np.concatenate([meta_tokens, x[0]], axis=0)
    h_in = tokens.T.reshape(DT, P, T).transpose(1, 0, 2)
    win = ffn_w_in.reshape(DEPTH * 2, DT, P, 2, FT, P).transpose(0, 4, 2, 3, 1, 5).reshape(DEPTH * 2, FT, P, UNIT)
    wout = ffn_w_out.reshape(DEPTH * 2, 2, FH, P, DT, P).transpose(0, 1, 4, 3, 2, 5).reshape(DEPTH * 2, 2, DT, P, OUT_UNIT)
    w3 = 3 * WIDTH
    n_rwkv = w3 + 64 + 64 + 160
    cols = np.zeros((DEPTH, D_MODEL, (N_TILES + 1) * P), f)
    mu = np.zeros((DEPTH, (N_TILES - R) * P), f)
    cols[:, :, 0:w3] = w_in[:, :, n_rwkv:n_rwkv + w3]
    cols[:, :, w3:2 * w3 + 256] = w_in[:, :, 0:w3 + 256]
    mu[:, 0:w3 + 256] = shift_mu[:, 0:w3 + 256]
    misc = MISC * P
    cols[:, :, misc:misc + 32] = w_in[:, :, w3 + 256:n_rwkv]
    mu[:, misc - R * P:misc - R * P + 32] = shift_mu[:, w3 + 256:n_rwkv]
    cols[1:, :, misc + 32:misc + 64] = w_in_vres
    mu[1:, misc - R * P + 32:misc - R * P + 64] = shift_mu_vres
    cols[:, :, misc + FORGET_ROW:misc + FORGET_ROW + HEADS] = w_in[:, :, n_rwkv + w3:]
    proj = cols.reshape(DEPTH, DT, P, PROJ_UNITS, 2, P).transpose(0, 3, 2, 4, 1, 5).reshape(DEPTH, PROJ_UNITS, P, UNIT)
    wo = w_out.reshape(DEPTH, DT, P, WO_UNITS, 2, P).transpose(0, 3, 2, 4, 1, 5).reshape(DEPTH, WO_UNITS, P, UNIT)
    lora = np.zeros((DEPTH, P, 5 * WIDTH), f)
    lora[:, 0:64, 0:WIDTH] = decay_up
    lora[:, 64:128, WIDTH:2 * WIDTH] = iclr_up
    lora[1:, 32:64, 2 * WIDTH:3 * WIDTH] = vres_up
    lora[:, :, 3 * WIDTH:4 * WIDTH] = gate_up[:, 0:P]
    lora[:, 0:32, 4 * WIDTH:5 * WIDTH] = gate_up[:, P:]
    params = np.zeros((P, DEPTH, N_PAR), f)

    def columns(col, a):
        a = a.reshape(DEPTH, -1, P).transpose(2, 0, 1)
        params[:, :, col:col + a.shape[2]] = a
    columns(GAIN, norm_gains)
    columns(MU, mu)
    vb = np.zeros((DEPTH, WIDTH), f)
    vb[1:] = vres_bias
    for col, a in ((DBIAS, decay_bias), (IBIAS, iclr_bias), (VBIAS, vb), (KKG, k_k), (KAG, k_a), (RKG, r_k),
                   (LNW, ln_x_w), (LNB, ln_x_b), (FOXG, fox_out_gain)):
        columns(col, a)
    params[FORGET_ROW:FORGET_ROW + HEADS, :, FBIAS] = forget_bias.T
    return {"h_in": h_in, "ffn_in": win, "ffn_out": wout, "proj": proj, "w_out": wo, "lora": lora,
            "params": params.reshape(P, DEPTH * N_PAR), "consts": constants()}


def kernel(**inputs):
    import concourse.bacc as bacc
    from concourse.bass_utils import run_bass_kernel_spmd

    arrays = {k: np.ascontiguousarray(v) for k, v in lay_out(**{k: np.asarray(v) for k, v in inputs.items()}).items()}
    nc = bacc.Bacc("TRN2", target_bir_lowering=False, num_devices=1, dynamic_dma_scratch_size=1024)
    args = [nc.dram_tensor(f"in_{k}", a.shape, F32, kind="ExternalInput").ap() for k, a in arrays.items()]
    out = nc.dram_tensor("out_h", _OUT, F32, kind="ExternalOutput").ap()
    build(nc, *args, out)
    r = run_bass_kernel_spmd(nc, [{f"in_{k}": a for k, a in arrays.items()}], core_ids=[0])
    got = r.results[0]["out_h"]
    return np.ascontiguousarray(got.transpose(2, 1, 0)).reshape(1, SEQ, D_MODEL)
```

```python
from contextlib import ExitStack

import numpy as np

import concourse.bass as bass
from concourse import mybir

D_MODEL = 1024
SEQ = 512
N_META = 16
DEPTH = 2
D_FF = 2816
HEAD = 64
WIDTH = 512
P = 128
T = SEQ + N_META
HT = T // 2
DT = D_MODEL // P
WT = WIDTH // P
FT = D_FF // P
FH = FT // 2
CHUNK = 64
N_CHUNK = -(-T // CHUNK)
LAST = T - (N_CHUNK - 1) * CHUNK
QT = [0, 107, 214, 321, 428, 528]
NQ = len(QT) - 1
HEADS = WIDTH // HEAD
NORM_EPS = 1e-6
LNX_EPS = 64e-5
DECAY = float(np.exp(-0.5))
NEG = -1e30

POOL_TILES = (0, 2, 4)

UNIT = 16 * P
OUT_UNIT = FH * P
FFN_UNITS = 2 * (FH + DT)
PROJ_UNITS = 14
WO_UNITS = DT // 2
LAYER_UNITS = 2 * FFN_UNITS + PROJ_UNITS + WO_UNITS

QF, KF, VF, R, K, V, WA, GD, MISC = 0, 4, 8, 12, 16, 20, 24, 25, 26
N_TILES = 27
FORGET_ROW = 64

GAIN, MU = 0, 6 * DT
DBIAS = MU + N_TILES - R
IBIAS, VBIAS, KKG, KAG, RKG, LNW, LNB, FOXG = (DBIAS + WT * n for n in range(1, 9))
FBIAS = FOXG + WT
N_PAR = FBIAS + 1

LEVELS = 6
IDENT, ONES, HEADSUM, CAUSAL, PAIRMASK = 0, 128, 256, 384, 512
LEVEL = PAIRMASK + 256
RESET = LEVEL + LEVELS * P
N_CONST = RESET + T

F32 = mybir.dt.float32
F32R = mybir.dt.float32r
ALU = mybir.AluOpType
ACT = mybir.ActivationFunctionType
AX = mybir.AxisListType


def build(nc, h_in, ffn_in, ffn_out, proj, w_out, lora, params, consts, out):
    ctx = ExitStack()
    with ctx:
        def sb(name, shape, dt=F32):
            return ctx.enter_context(nc.sbuf_tensor(name, shape, dt))

        def sem(name):
            return ctx.enter_context(nc.semaphore(name))

        h = sb("h", [P, DT, T])
        raw = sb("raw", [P, 2, UNIT])
        v_first = sb("v_first", [P, WT, T])
        cst = sb("cst", [P, N_CONST])
        prm = sb("prm", [P, DEPTH * N_PAR])
        root = sb("root", [P, T])
        rs_pre = sb("rs_pre", [P, T])
        rs_post = sb("rs_post", [P, T])
        acc = sb("acc", [P, T])
        sqb = sb("sqb", [P, 2, T])
        eps = sb("eps", [P, 4])
        warm = sb("warm", [P, 3 * DEPTH])

        e_all = sb("e_all", [P, 2, WT * (2 * CHUNK + 1)])

        with ExitStack() as low:
            def lo_sb(name, shape, dt=F32):
                return low.enter_context(nc.sbuf_tensor(name, shape, dt))
            qz = lo_sb("qz", [P, 2, T])
            vz = lo_sb("vz", [P, 2, NQ, P])
            prob_t = lo_sb("prob_t", [P, 2, NQ, QT[1]])
            diag = lo_sb("diag", [P, 2, P])
            c_tok = lo_sb("c_tok", [P, NQ, HEADS])
            neg_max = lo_sb("neg_max", [P, 2])
            row_sum = lo_sb("row_sum", [P, 2])
            inv_sum = lo_sb("inv_sum", [P, 2])
            ar = lo_sb("ar", [P, 2, WT, 2 * P])
            bkv = lo_sb("bkv", [P, 2, WT, 3 * P])
            gm = lo_sb("gm", [P, WT, 4 * P])
            tok = lo_sb("tok", [P, WT, 3 * P])
            work = lo_sb("work", [P, 7, WT, P])
        x_hi = sb("x_hi", [P, DT, T], F32R)
        x_lo = sb("x_lo", [P, DT, T], F32R)
        w_hi = sb("w_hi", [P, 2, UNIT], F32R)
        w_lo = sb("w_lo", [P, 2, UNIT], F32R)
        with ExitStack() as f:
            def ff_sb(name, shape, dt=F32):
                return f.enter_context(nc.sbuf_tensor(name, shape, dt))
            hid_hi = ff_sb("hid_hi", [P, FH, T], F32R)
            hid_lo = ff_sb("hid_lo", [P, FH, T], F32R)
            y_ffn = ff_sb("y_ffn", [P, DT, T])
            gs = ff_sb("gs", [P, 2, T])
            us = ff_sb("us", [P, 2, T])
            sg = ff_sb("sg", [P, 2, T])
            hid = ff_sb("hid", [P, 2, T])
        tiles = sb("tiles", [P, N_TILES * T])
        aa = sb("aa", [P, WT, T])
        ll = sb("ll", [P, WT, T])
        kk = sb("kk", [P, WT, T])
        bonus = sb("bonus", [P, WT, T])

        ps = ctx.enter_context(nc.psum_tensor("ps", [P, 8, 512], F32))

        def spread(ap, n):
            return ap.unsqueeze(1).broadcast_to([ap.shape[0], n, ap.shape[1]])

        def tile(i, n=1):
            return tiles[:, i * T:(i + n) * T]

        def group(i, c0=0, c1=T, p0=0, p1=P):
            return tiles[p0:p1, i * T:(i + WT) * T].rearrange("p (m t) -> p m t", m=WT)[:, :, c0:c1]

        ym, zm, qm, uo, rb, sa, hs = (work[:, n, :, :] for n in range(7))
        lora_w = gm[:, :, :].rearrange("p m c -> p (m c)")[:, 0:3 * WIDTH]
        spare = work[:, :, :, :].rearrange("p n m c -> p (n m c)")
        tmp = [spare[:, n * T:(n + 1) * T] for n in range(3)]
        k_square = [spare[:, n * T:(n + 1) * T] for n in (3, 4)]
        gate_w = tiles[:, KF * T:KF * T + 2 * WIDTH]
        y_mix = tiles[:, KF * T:(KF + DT) * T].rearrange("p (m t) -> p m t", m=DT)
        slots = raw[:, :, :].rearrange("p q c -> p (q c)")
        prob, c_one, c_key = (slots[:, 2 * n * T:2 * (n + 1) * T].rearrange("p (a t) -> p a t", a=2) for n in range(3))
        v_pair = slots[:, 6 * T:7 * T]
        score = sqb
        c_all = acc
        fg = score
        e_fwd = [e_all[:, q, 0:WT * (CHUNK + 1)].rearrange("p (m t) -> p m t", m=WT) for q in range(2)]
        e_bwd = [e_all[:, q, WT * (CHUNK + 1):].rearrange("p (m t) -> p m t", m=WT) for q in range(2)]
        shifted = [ll[:, 0:3, :].rearrange("p m t -> p (m t)")[:, q * 532:q * 532 + T + 1] for q in range(2)]
        delta = [kk[:, q, :] for q in range(2)]

        def par(l, col, p0=0, p1=P):
            return prm[p0:p1, l * N_PAR + col:l * N_PAR + col + 1]

        ident = cst[:, IDENT:IDENT + P]
        ones = cst[:, ONES:ONES + P]
        headsum = cst[:, HEADSUM:HEADSUM + P]
        ident4 = spread(ident, WT)

        def pair(b):
            return ps[:, b:b + 2, 0:HT]

        def halves(ap):
            return ap.rearrange("p (a t) -> p a t", a=2)

        raw_loaded = [sem("raw_loaded0"), sem("raw_loaded1")]
        small_loaded = sem("small_loaded")
        cst_loaded = sem("cst_loaded")
        h_loaded = [sem(f"h_loaded{m}") for m in range(DT)]
        lora_loaded = sem("lora_loaded")
        gate_loaded = sem("gate_loaded")
        stored = sem("stored")
        hi_ready = sem("hi_ready")
        w_split = sem("w_split")
        unit_done = sem("unit_done")
        evacuated = sem("evacuated")
        gate_done = sem("gate_done")
        gs_ready = sem("gs_ready")
        sg_ready = sem("sg_ready")
        hid_ready = sem("hid_ready")
        hid_hi_ready = sem("hid_hi_ready")
        hid_lo_ready = sem("hid_lo_ready")
        sq_ready = sem("sq_ready")
        acc_added = sem("acc_added")
        stat_done = sem("stat_done")
        root_ready = sem("root_ready")
        rs_ready = sem("rs_ready")
        y_scaled = sem("y_scaled")
        y_scaled_dve = sem("y_scaled_dve")
        h_ready = sem("h_ready")
        x_hi_ready = sem("x_hi_ready")
        x_lo_ready = sem("x_lo_ready")
        delta_ready = sem("delta_ready")
        tiles_ready = sem("tiles_ready")
        dve_step = sem("dve_step")
        act_step = sem("act_step")
        shift_zero = sem("shift_zero")
        fg_exp = sem("fg_exp")
        fg_abs = sem("fg_abs")
        c_ready = sem("c_ready")
        c_turned = sem("c_turned")
        c_tok_ready = sem("c_tok_ready")
        att_zero = sem("att_zero")
        q_ready = sem("q_ready")
        c_one_ready = sem("c_one_ready")
        c_spread = sem("c_spread")
        c_key_ready = sem("c_key_ready")
        v_turned = sem("v_turned")
        vz_ready = sem("vz_ready")
        scored = sem("scored")
        score_read = sem("score_read")
        max_ready = sem("max_ready")
        prob_ready = sem("prob_ready")
        diag_ready = sem("diag_ready")
        prob_turned = sem("prob_turned")
        prob_t_ready = sem("prob_t_ready")
        att_done = sem("att_done")
        att_read = sem("att_read")
        lora_in = sem("lora_in")
        ksq_ready = sem("ksq_ready")
        decay_done = sem("decay_done")
        iclr_done = sem("iclr_done")
        vres_done = sem("vres_done")
        knorm_done = sem("knorm_done")
        decay_sig = sem("decay_sig")
        iclr_sig = sem("iclr_sig")
        vres_sig = sem("vres_sig")
        kmax_ready = sem("kmax_ready")
        kroot_ready = sem("kroot_ready")
        rk_ready = sem("rk_ready")
        bonus_done = sem("bonus_done")
        bonus_ready = sem("bonus_ready")
        bd_zero = sem("bd_zero")
        e_ready = sem("e_ready")
        ar_built = sem("ar_built")
        bkv_built = sem("bkv_built")
        gram_done = sem("gram_done")
        gram_ready = sem("gram_ready")
        turned = sem("turned")
        tok_ready = sem("tok_ready")
        off_ready = sem("off_ready")
        z0_done = sem("z0_done")
        q_done = sem("q_done")
        qm_ready = sem("qm_ready")
        zd_done = sem("zd_done")
        yd_done = sem("yd_done")
        z_ready = sem("z_ready")
        y_ready = sem("y_ready")
        r_done = sem("r_done")
        rb_ready = sem("rb_ready")
        sa_done = sem("sa_done")
        sa_ready = sem("sa_ready")
        o_done = sem("o_done")
        o_read = sem("o_read")
        hd_done = sem("hd_done")
        state_ready = sem("state_ready")
        fsq_ready = sem("fsq_ready")
        fsum_done = sem("fsum_done")
        fln_ready = sem("fln_ready")
        frs_ready = sem("frs_ready")
        oln_ready = sem("oln_ready")
        ors_ready = sem("ors_ready")
        f_ready = sem("f_ready")
        mean_done = sem("mean_done")
        oc_ready = sem("oc_ready")
        osq_ready = sem("osq_ready")
        var_done = sem("var_done")
        oroot_ready = sem("oroot_ready")
        g_done = sem("g_done")
        o_ready = sem("o_ready")
        v_copied = sem("v_copied")
        v_mixed = sem("v_mixed")
        v_built = sem("v_built")
        masked = sem("masked")
        inv_ready = sem("inv_ready")
        eps_set = sem("eps_set")
        h_added = sem("h_added")

        def unit_base(l, phase):
            return l * LAYER_UNITS + {"a": 0, "proj": FFN_UNITS, "wo": FFN_UNITS + PROJ_UNITS,
                                      "b": FFN_UNITS + PROJ_UNITS + WO_UNITS}[phase]

        def slot(base, k):
            return (base + k) % 2

        def units(eng, n, body, first=0):
            turns = max(n - 3, 0) // 2
            body(first, 0)
            body(first + 1, 0)
            if turns:
                with eng.Fori(0, turns) as i:
                    body(first + 2, i)
                    body(first + 3, i)
            for k in range(2 + 2 * turns, n):
                body(first + k, 0)

        def pair_loop(eng, body):
            with eng.Fori(0, WT - 1) as i:
                body(i, False)
            body(WT - 1, True)

        PIECES = (2, 1, 1, 1, 1, 1, 1, 1, 1, 1, 1, 1, 1, 2, 2)

        def pieces(second, place):
            start = second * sum(PIECES) + sum(PIECES[:place])
            return range(start, min(start + PIECES[place], 5 + 6 * NQ))

        def step_piece(n):
            return divmod(n - 5, 3)

        def wait(eng, semaphore, value):
            if not isinstance(value, int) or value > 0:
                eng.wait_ge(semaphore, value)

        def norm_bank(l, n):
            if n % 2 == 0:
                return 4 * (1 - unit_base(l, ("a", "proj", "b")[n // 2]) % 2) + 2
            end = (unit_base(l, "a") + FFN_UNITS, unit_base(l, "wo") + WO_UNITS, unit_base(l, "b") + FFN_UNITS)[n // 2]
            return 4 * (end % 2)

        def post_count(l, n):
            return DT * (3 * l + {0: 0, 1: 1, 3: 2}[n])

        block = ctx.enter_context(nc.Block())

        @block.sync
        def _(sp):
            def load(source, cols, base, k, i=0):
                u = i * 2 + k
                wait(sp, w_split, u + (base - 1))
                sp.dma_start(raw[:, slot(base, k), 0:cols], source(u)).then_inc(raw_loaded[slot(base, k)], 16)

            def ffn(l, which, f):
                for fh in range(2):
                    base = unit_base(l, which) + fh * (FH + DT)
                    units(sp, FH, lambda k, i: load(lambda u: ffn_in[f, u + fh * FH], UNIT, base, k, i))
                    units(sp, DT, lambda k, i: load(lambda u: ffn_out[f, fh, u], OUT_UNIT, base + FH, k, i))

            sp.dma_start(prm[:, :], params).then_inc(small_loaded, 16)
            for l in range(DEPTH):
                ffn(l, "a", 2 * l)
                units(sp, PROJ_UNITS, lambda k, i: load(lambda u: proj[l, u], UNIT, unit_base(l, "proj"), k, i))
                sp.wait_ge(evacuated, unit_base(l, "wo"))
                sp.dma_start(lora_w, lora[l, :, 0:3 * WIDTH]).then_inc(lora_loaded, 16)
                sp.wait_ge(att_read, WT * NQ * (l + 1))
                sp.dma_start(gate_w, lora[l, :, 3 * WIDTH:5 * WIDTH]).then_inc(gate_loaded, 16)
                units(sp, WO_UNITS, lambda k, i: load(lambda u: w_out[l, u], UNIT, unit_base(l, "wo"), k, i))
                ffn(l, "b", 2 * l + 1)
            sp.wait_ge(h_ready, DT * 3 * DEPTH)
            sp.dma_start(out, h[:, :, N_META:T]).then_inc(stored, 16)
            sp.wait_ge(stored, 16)

        @block.tensor
        def _(pe):
            def product(out_ap, w, x, first=True, last=True):
                return pe.matmul(out_ap, w, x, start=first, stop=last)

            def gemm(q, n_m, n_k, xh, xl, before=None):
                for m in range(n_m):
                    for k in range(n_k):
                        if before is not None and m == 0:
                            before(k)
                        cols = slice((m * n_k + k) * P, (m * n_k + k + 1) * P)
                        for n, (w, x) in enumerate(((w_hi, xh), (w_hi, xl), (w_lo, xh))):
                            for half in range(2):
                                ins = product(ps[:, 4 * q + 2 * m + half, 0:HT], w[:, q, cols],
                                              x[:, k, half * HT:(half + 1) * HT],
                                              k == 0 and n == 0, k == n_k - 1 and n == 2)
                    yield ins

            def first_gemm(q, xh, xl, hi_ready_for, lo_ready_for, order=tuple(range(DT))):
                def two(m, k, w, x, start, stop):
                    cols = slice((m * DT + k) * P, (m * DT + k + 1) * P)
                    for half in range(2):
                        ins = product(ps[:, 4 * q + 2 * m + half, 0:HT], w[:, q, cols], x[:, k, half * HT:(half + 1) * HT], start, stop)
                    return ins
                for k in order:
                    hi_ready_for(k)
                    for m in range(2):
                        two(m, k, w_hi, xh, k == order[0], False)
                        two(m, k, w_lo, xh, False, False)
                for m in range(2):
                    for k in order:
                        if m == 0:
                            lo_ready_for(k)
                        ins = two(m, k, w_hi, xl, False, k == order[-1])
                    yield ins

            def start_unit(u, base):
                pe.wait_ge(w_split, u + (base + 1))
                wait(pe, evacuated, u + (base - 1))

            def both(bank, w, x, first=True, last=True):
                for half in range(2):
                    ins = product(ps[:, bank + half, 0:HT], w, x[:, half * HT:(half + 1) * HT], first, last)
                return ins

            def statistics(l, n, units_before):
                s = 6 * l + n
                wait(pe, evacuated, units_before)
                pe.wait_ge(acc_added, (DT - 2) * (s + 1))
                both(norm_bank(l, n), ones, acc, True, False)
                pe.wait_ge(sq_ready, DT * (s + 1))
                both(norm_bank(l, n), ones, sqb[:, (DT - 1) % 2, :], False, True).then_inc(stat_done, 1)

            def operand(g):
                return lambda k: pe.wait_ge(x_hi_ready, DT * g + k + 1), lambda k: pe.wait_ge(x_lo_ready, DT * g + k + 1)

            def ffn(l, which, f, g, n):
                for fh in range(2):
                    base = unit_base(l, which) + fh * (FH + DT)

                    def unit_in(k, i):
                        u = i * 2 + k
                        start_unit(u, base)
                        if fh == 0 and k == 0:
                            products = first_gemm(slot(base, k), x_hi, x_lo, *operand(g))
                        else:
                            products = gemm(slot(base, k), 2, DT, x_hi, x_lo)
                        if fh == 0 and k == 1:
                            statistics(l, n, base)
                        next(products).then_inc(gate_done, 1)
                        if fh == 0 and k == 1:
                            pe.wait_ge(root_ready, 6 * l + n + 1)
                        next(products).then_inc(unit_done, 1)

                    def unit_out(k, i):
                        start_unit(i * 2 + k, base + FH)
                        before = (lambda kt: pe.wait_ge(hid_lo_ready, FH * (2 * f + fh) + kt + 1)) if k == 0 else None
                        next(gemm(slot(base + FH, k), 1, FH, hid_hi, hid_lo, before)).then_inc(unit_done, 1)

                    units(pe, FH, unit_in)
                    units(pe, DT, unit_out)
                statistics(l, n + 1, unit_base(l, which) + FFN_UNITS - 1)
                pe.wait_ge(root_ready, 6 * l + n + 2)

            def projection(l):
                base = unit_base(l, "proj")

                def unit(k, i):
                    start_unit(i * 2 + k, base)
                    if k == 0:
                        products = first_gemm(slot(base, k), x_hi, x_lo, *operand(4 * l + 1))
                    else:
                        products = gemm(slot(base, k), 1 if k == PROJ_UNITS - 1 else 2, DT, x_hi, x_lo)
                    if k == 1:
                        statistics(l, 2, base)
                    for m, ins in enumerate(products):
                        if k == 1 and m == 0:
                            pe.wait_ge(root_ready, 6 * l + 3)
                    ins.then_inc(unit_done, 1)
                units(pe, PROJ_UNITS, unit)

            def forget_gates(l):
                pe.wait_ge(evacuated, unit_base(l, "wo"))
                pe.wait_ge(c_ready, l + 1)
                for j in range(NQ):
                    n = QT[j + 1] - QT[j]
                    ins = pe.transpose(ps[0:n, 4 + j // 4, (j % 4) * P:(j % 4 + 1) * P], c_all[:, QT[j]:QT[j + 1]], ident)
                ins.then_inc(c_turned, 1)
                pe.wait_ge(c_tok_ready, l + 1)

            def attend(l, pr, n_piece):
                pairs = pr + l * WT
                step = pairs * (2 * NQ)

                def scores(s):
                    j, a = divmod(s, 2)
                    nk = QT[j + 1]
                    wide = nk > 512
                    if s < 2:
                        pe.wait_ge(q_ready, pairs * 2 + (a + 1))
                        pe.wait_ge(c_key_ready, pairs * 2 + 2)
                    else:
                        pe.wait_ge(score_read, step + (s if wide else s - 1))
                    for half, (c0, c1) in enumerate([(0, HT), (HT, T)] if wide else [(0, nk)]):
                        ins = product(ps[0:nk - QT[j], 4 + (half if wide else a), 0:c1 - c0], qz[:, a, QT[j]:nk],
                                      tiles[:, bass.ds((pr + KF) * T + c0, c1 - c0)])
                    ins.then_inc(scored, 1)

                def turn(s):
                    j, a = divmod(s, 2)
                    n = QT[j + 1] - QT[j]
                    pe.wait_ge(diag_ready, step + (s + 1))
                    if s == 0:
                        pe.wait_ge(vz_ready, pairs + 1)
                    else:
                        pe.wait_ge(prob_t_ready, step + s)
                    for i in range(j + 1):
                        ni = QT[i + 1] - QT[i]
                        ins = product(ps[0:ni, 6, i * n:(i + 1) * n], prob[0:n, a, QT[i]:QT[i + 1]], diag[0:n, a, 0:n])
                    ins.then_inc(prob_turned, 1)

                def values(s):
                    j, a = divmod(s, 2)
                    n = QT[j + 1] - QT[j]
                    pe.wait_ge(prob_t_ready, step + (s + 1))
                    if a == 0 and j:
                        pe.wait_ge(att_read, pairs * NQ + j)
                    for i in range(j + 1):
                        ni = QT[i + 1] - QT[i]
                        ins = product(ps[:, 7, 0:n], vz[0:ni, a, i, :], prob_t[0:ni, a, i, 0:n],
                                      a == 0 and i == 0, a == 1 and i == j)
                    if a == 1:
                        ins.then_inc(att_done, 1)

                if n_piece in (1, 3):
                    a = n_piece // 2
                    pe.wait_ge(c_one_ready, pairs * 2 + (a + 1))
                    if a:
                        pe.wait_ge(c_key_ready, pairs * 2 + 1)
                    both(4, ones, c_one[:, a, :]).then_inc(c_spread, 1)
                elif n_piece == 2:
                    pe.wait_ge(v_copied, pairs + 1)
                    for j in range(NQ):
                        n = QT[j + 1] - QT[j]
                        ins = pe.transpose(ps[0:n, 6 + j // 4, (j % 4) * P:(j % 4 + 1) * P], v_pair[:, QT[j]:QT[j + 1]], ident)
                    ins.then_inc(v_turned, 1)
                elif n_piece == 4:
                    scores(0)
                elif n_piece > 4:
                    s, kind = step_piece(n_piece)
                    if kind == 0 and s + 1 < 2 * NQ:
                        scores(s + 1)
                    elif kind == 1:
                        turn(s)
                    elif kind == 2:
                        values(s)

            def low_rank(l):
                pe.wait_ge(lora_loaded, 16 * (l + 1))
                pe.wait_ge(lora_in, 3 * (l + 1))
                for m in range(WT):
                    n = WT * l + m
                    todo = [(WA, decay_done, decay_sig, n), (WA, iclr_done, iclr_sig, n), (MISC, vres_done, vres_sig, n - WT)]
                    for i, (src, done, read, count) in enumerate(todo[:3 if l else 2]):
                        if m:
                            pe.wait_ge(read, count)
                        both(2 * i, lora_w[:, i * WIDTH + m * P:i * WIDTH + (m + 1) * P], tile(src)).then_inc(done, 1)
                    pe.wait_ge(ksq_ready, n + 1)
                    if m:
                        pe.wait_ge(kmax_ready, n)
                    both(6, headsum, k_square[m % 2]).then_inc(knorm_done, 1)
                pe.wait_ge(iclr_sig, WT * (l + 1))
                for m in range(WT):
                    n = WT * l + m
                    pe.wait_ge(rk_ready, n + 1)
                    if m >= 2:
                        pe.wait_ge(bonus_ready, n - 1)
                    both(2 * (m % 2), headsum, bonus[:, m, :]).then_inc(bonus_done, 1)

            def chunks(l):
                pe.wait_ge(bonus_ready, WT * (l + 1))
                pe.wait_ge(kmax_ready, WT * (l + 1))
                if l:
                    pe.wait_ge(vres_sig, WT * l)
                pe.wait_ge(bd_zero, 2 * (l + 1))

                def chunk(c, b, n, beside):
                    cc = c + l * N_CHUNK
                    pe.wait_ge(ar_built, cc + 1)
                    pe.wait_ge(bkv_built, cc * 4 + 4)
                    pe.wait_ge(v_built, cc + 1)
                    for pr in range(WT):
                        if pr >= 2:
                            pe.wait_ge(gram_ready, cc * WT + (pr - 1))
                        for i in range(2):
                            ins = product(ps[:, pr % 2, i * 256:(i + 1) * 256], bkv[:, b, pr, i * P:(i + 1) * P], ar[:, b, pr, :])
                        ins.then_inc(gram_done, 1)
                        if pr >= 2:
                            pe.wait_ge(tok_ready, cc * WT + (pr - 1))
                        for i in range(3):
                            ins = pe.transpose(ps[:, 2 + pr % 2, i * P:(i + 1) * P], bkv[:, b, pr, i * P:(i + 1) * P], ident)
                        ins.then_inc(turned, 1)
                    beside(0)
                    pe.wait_ge(gram_ready, cc * WT + WT)
                    pe.wait_ge(off_ready, cc * LEVELS + 1)
                    for pr in range(WT):
                        ins = pe.transpose(ps[:, 0, pr * P:(pr + 1) * P], uo[:, pr, :], ident)
                    ins.then_inc(z0_done, 1)
                    beside(1)
                    pe.wait_ge(tok_ready, cc * WT + WT)
                    for v in range(1, LEVELS):
                        pe.wait_ge(off_ready, cc * LEVELS + (v + 1))
                        pe.wait_ge(z_ready, cc * 5 + v)
                        for pr in range(WT):
                            ins = product(ps[:, 1, pr * P:(pr + 1) * P], uo[:, pr, :], zm[:, pr, :])
                        ins.then_inc(q_done, 1)
                        beside(2 * v)
                        pe.wait_ge(qm_ready, cc * 5 + v)
                        pe.wait_ge(y_ready, cc * LEVELS + v)
                        if v < LEVELS - 1:
                            for pr in range(WT):
                                ins = product(ps[:, 2, pr * P:(pr + 1) * P], ym[:, pr, :], qm[:, pr, :])
                            ins.then_inc(zd_done, 1)
                        for pr in range(WT):
                            ins = product(ps[:, 3, pr * P:(pr + 1) * P], qm[:, pr, :], ym[:, pr, :])
                        ins.then_inc(yd_done, 1)
                        beside(2 * v + 1)
                    for pr in range(WT):
                        product(ps[:, 0, pr * P:(pr + 1) * P], gm[:, pr, 256:384], tok[:, pr, 256:384], True, False)
                        ins = product(ps[:, 0, pr * P:(pr + 1) * P], ar[:, b, pr, 0:P], hs[:, pr, :], False, True)
                    ins.then_inc(r_done, 1)
                    beside(12)
                    pe.wait_ge(rb_ready, cc + 1)
                    pe.wait_ge(y_ready, cc * LEVELS + LEVELS)
                    for pr in range(WT):
                        ins = product(ps[:, 1, pr * P:(pr + 1) * P], ym[:, pr, :], rb[:, pr, :])
                    ins.then_inc(sa_done, 1)
                    beside(13)
                    pe.wait_ge(sa_ready, cc + 1)
                    for pr in range(WT):
                        o = ps[:, 2, pr * P:(pr + 1) * P]
                        product(o, sa[:, pr, :], gm[:, pr, 128:256], True, False)
                        product(o, tok[:, pr, 256:384], gm[:, pr, 384:512], False, False)
                        ins = product(o, hs[:, pr, :], ar[:, b, pr, P:2 * P], False, True)
                    ins.then_inc(o_done, 1)
                    for pr in range(WT):
                        d = ps[:, 3, pr * P:(pr + 1) * P]
                        product(d, tok[:, pr, 0:128], sa[:, pr, :], True, False)
                        ins = product(d, tok[:, pr, 128:256], tok[:, pr, 256:384], False, True)
                    ins.then_inc(hd_done, 1)
                    beside(14)
                    pe.wait_ge(state_ready, cc + 1)
                    pe.wait_ge(o_read, cc + 1)

                def pair_of_chunks(pr, last):
                    for second in range(2):
                        chunk(pr * 2 + second, second, CHUNK, lambda place: [attend(l, pr, n) for n in pieces(second, place)])
                    pe.wait_ge(score_read, (pr + l * WT) * (2 * NQ) + 2 * NQ)
                    pe.wait_ge(att_read, (pr + l * WT) * NQ + NQ)

                pair_loop(pe, pair_of_chunks)
                chunk(N_CHUNK - 1, 0, LAST, lambda place: None)

            def head_outputs(l):
                pe.wait_ge(state_ready, N_CHUNK * (l + 1))
                pe.wait_ge(o_read, N_CHUNK * (l + 1))
                pe.wait_ge(gate_loaded, 16 * (l + 1))

                def mean(m):
                    if m >= 2:
                        pe.wait_ge(oc_ready, WT * l + m - 1)
                    both(2 * (m % 2), headsum, tile(R + m)).then_inc(mean_done, 1)

                def fox_sum(m):
                    pe.wait_ge(fsq_ready, WT * l + m + 1)
                    if m >= 2:
                        pe.wait_ge(fln_ready, WT * l + m - 1)
                    both(4 + 2 * (m % 2), headsum, ll[:, m, :]).then_inc(fsum_done, 1)

                def variance(m):
                    pe.wait_ge(osq_ready, WT * l + m + 1)
                    if m >= 2:
                        pe.wait_ge(oln_ready, WT * l + m - 1)
                    both(2 * (m % 2), headsum, aa[:, m, :]).then_inc(var_done, 1)

                def gate(m):
                    if m >= 2:
                        pe.wait_ge(o_ready, WT * l + m - 1)
                    b = 4 + 2 * (m % 2)
                    both(b, gate_w[:, m * P:(m + 1) * P], tile(GD), True, False)
                    both(b, gate_w[:, WIDTH + m * P:WIDTH + (m + 1) * P], tile(MISC), False, True).then_inc(g_done, 1)

                for m in (0, 1):
                    mean(m)
                for m in (0, 1):
                    fox_sum(m)
                for m in (2, 3):
                    mean(m)
                for m in (2, 3):
                    fox_sum(m)
                pe.wait_ge(oc_ready, WT * (l + 1))
                variance(0)
                variance(1)
                pe.wait_ge(fln_ready, WT * (l + 1))
                gate(0)
                gate(1)
                variance(2)
                variance(3)
                gate(2)
                gate(3)

            def mixer_out(l):
                base = unit_base(l, "wo")
                order = [m + first for m in range(WT) for first in (WT, 0)]

                def unit(k, i):
                    start_unit(i * 2 + k, base)
                    if k == 0:
                        pe.wait_ge(oln_ready, WT * (l + 1))
                        if slot(base, 0) == 1:
                            pe.wait_ge(o_ready, WT * (l + 1))
                        count = {kt: DT * (4 * l + 2) + n + 1 for n, kt in enumerate(order)}
                        products = first_gemm(slot(base, k), x_hi, x_lo, lambda kt: pe.wait_ge(x_hi_ready, count[kt]),
                                              lambda kt: pe.wait_ge(x_lo_ready, count[kt]), order)
                    else:
                        if k == 1:
                            pe.wait_ge(o_ready, WT * (l + 1))
                        products = gemm(slot(base, k), 2, DT, x_hi, x_lo)
                    for ins in products:
                        pass
                    ins.then_inc(unit_done, 1)
                units(pe, WO_UNITS, unit)
                statistics(l, 3, base + WO_UNITS - 1)
                pe.wait_ge(root_ready, 6 * l + 4)

            pe.wait_ge(cst_loaded, 16)
            for l in range(DEPTH):
                ffn(l, "a", 2 * l, 4 * l, 0)
                projection(l)
                forget_gates(l)
                low_rank(l)
                chunks(l)
                head_outputs(l)
                mixer_out(l)
                ffn(l, "b", 2 * l + 1, 4 * l + 3, 4)

        @block.scalar
        def _(act):
            eps_pre, eps_half, eps_lnx, one = (eps[:, n:n + 1] for n in range(4))

            def copy(dst, src):
                return act.activation(dst, src, ACT.Copy)

            def split_hi(cols, base, k, i=0):
                u = i * 2 + k
                act.wait_ge(raw_loaded[slot(base, k)], i * 16 + 16 * ((base + k) // 2 + 1))
                wait(act, unit_done, u + (base - 1))
                copy(w_hi[:, slot(base, k), 0:cols], raw[:, slot(base, k), 0:cols]).then_inc(hi_ready, 1)

            def square(s, k, i, ap):
                if k == 0:
                    wait(act, stat_done, s)
                    act.activation(acc[:, :], ap, ACT.Square).then_inc(sq_ready, 1)
                else:
                    wait(act, acc_added, i * 2 + ((DT - 2) * s + max(k - 2, 0)))
                    act.activation(sqb[:, k % 2, :], ap, ACT.Square).then_inc(sq_ready, 1)

            def load_ln(n):
                act.activation(warm[:, n:n + 1], one, ACT.Ln)

            def inverse_root(l, n, scale, bias):
                count = 6 * l + n + 1
                act.wait_ge(stat_done, count)
                act.activation(halves(root[:, :]), pair(norm_bank(l, n)), ACT.Ln, bias=bias, scale=scale).then_inc(root_ready, 1)
                act.wait_ge(root_ready, count)
                act.activation((rs_pre, rs_post)[n % 2][:, :], root[:, :], ACT.Exp, scale=-0.5).then_inc(rs_ready, 1)

            def prepare(l, g, n, units_before):
                wait(act, unit_done, units_before)
                for m in range(DT):
                    if post_count(l, g):
                        act.wait_ge(h_ready, post_count(l, g) - DT + m + 1)
                    else:
                        act.wait_ge(h_loaded[m], 16)
                    act.activation(x_hi[:, m, :], h[:, m, :], ACT.Copy, scale=par(l, GAIN + n * DT + m)).then_inc(x_hi_ready, 1)
                    square(6 * l + n, m, 0, h[:, m, :])

            def ffn(l, which, f, n):
                for fh in range(2):
                    base = unit_base(l, which) + fh * (FH + DT)

                    def unit_in(k, i):
                        u, q = i * 2 + k, slot(base, k)
                        if k == FH - 1:
                            split_hi(OUT_UNIT, base, FH)
                        elif not (fh == 0 and k == 0):
                            split_hi(UNIT, base, k + 1, i)
                        if fh == 0 and k == 0:
                            inverse_root(l, n, 1.0 / D_MODEL, eps_pre)
                        act.wait_ge(gs_ready, u + (FH * (2 * f + fh) + 1))
                        act.activation(sg[:, q, :], gs[:, q, :], ACT.Silu).then_inc(sg_ready, 1)
                        act.wait_ge(hid_ready, u + (FH * (2 * f + fh) + 1))
                        copy(hid_hi[:, u, :], hid[:, q, :]).then_inc(hid_hi_ready, 1)

                    def unit_out(k, i):
                        u = i * 2 + k
                        if k < DT - 1:
                            split_hi(OUT_UNIT, base + FH, k + 1, i)
                        elif not (l == DEPTH - 1 and which == "b" and fh == 1):
                            split_hi(UNIT, base, FH + DT)
                        if fh == 1:
                            act.wait_ge(evacuated, u + (base + FH + 1))
                            square(6 * l + n + 1, k, i, y_ffn[:, u, :])

                    units(act, FH, unit_in)
                    if fh == 1:
                        load_ln(3 * l + n // 2)
                    units(act, DT, unit_out)
                if not (l == DEPTH - 1 and which == "b"):
                    split_hi(UNIT, base + FH + DT, 1)
                inverse_root(l, n + 1, 4.0 / D_MODEL, eps_half)

            def projection(l):
                base = unit_base(l, "proj")

                def unit(k, i):
                    if 0 < k < PROJ_UNITS - 1:
                        split_hi(UNIT // 2 if k == PROJ_UNITS - 2 else UNIT, base, k + 1, i)
                    if k == 0:
                        inverse_root(l, 2, 1.0 / D_MODEL, eps_pre)
                units(act, PROJ_UNITS, unit)

            def forget_gates(l):
                row = slice(FORGET_ROW, FORGET_ROW + HEADS)
                act.wait_ge(fg_abs, l + 1)
                act.activation(fg[row, 1, :], fg[row, 1, :], ACT.Exp).then_inc(act_step, 1)
                act.wait_ge(act_step, l + 1)
                act.activation(fg[row, 1, :], fg[row, 1, :], ACT.Ln, bias=one[row, :]).then_inc(fg_exp, 1)
                act.wait_ge(c_turned, l + 1)
                for j in range(NQ):
                    n = QT[j + 1] - QT[j]
                    c0 = (j % 4) * P + FORGET_ROW
                    ins = copy(c_tok[0:n, j, :], ps[0:n, 4 + j // 4, c0:c0 + HEADS])
                ins.then_inc(c_tok_ready, 1)

            def attend(l, pr, n_piece):
                pairs = pr + l * WT
                step = pairs * (2 * NQ)

                def exponent(s):
                    j, a = divmod(s, 2)
                    n = QT[j + 1] - QT[j]
                    act.wait_ge(max_ready, step + (s + 1))
                    if s >= 2:
                        act.wait_ge(prob_turned, step + (s - 1))
                    act.activation(prob[0:n, a, 0:QT[j + 1]], score[0:n, a, 0:QT[j + 1]], ACT.Exp,
                                   bias=neg_max[0:n, a:a + 1], accum_out=row_sum[0:n, a:a + 1]).then_inc(prob_ready, 1)

                def by_key(s):
                    j, a = divmod(s, 2)
                    n = QT[j + 1] - QT[j]
                    act.wait_ge(prob_turned, step + (s + 1))
                    if j:
                        act.wait_ge(att_done, pairs * NQ + j)
                    m = min(j + 1, 4)
                    ins = copy(prob_t[0:QT[1], a, 0:m, 0:n], ps[0:QT[1], 6, 0:m * n].rearrange("p (i c) -> p i c", i=m))
                    if j == 4:
                        ins = copy(prob_t[0:n, a, 4, 0:n], ps[0:n, 6, 4 * n:5 * n])
                    ins.then_inc(prob_t_ready, 1)

                if n_piece == 0:
                    for a in range(2):
                        rows = slice(a * HEAD, (a + 1) * HEAD)
                        act.activation(qz[rows, a, :], tiles[rows, bass.ds((pr + QF) * T, T)], ACT.Copy, scale=HEAD ** -0.5).then_inc(q_ready, 1)
                    copy(v_pair[:, :], tiles[:, bass.ds((pr + VF) * T, T)]).then_inc(v_copied, 1)
                elif n_piece in (1, 3):
                    act.wait_ge(c_spread, pairs * 2 + (n_piece // 2 + 1))
                    copy(halves(c_key[:, n_piece // 2, :]), pair(4)).then_inc(c_key_ready, 1)
                elif n_piece == 2:
                    act.wait_ge(v_turned, pairs + 1)
                    for a in range(2):
                        cols = slice(a * HEAD, (a + 1) * HEAD)
                        copy(vz[0:QT[1], a, 0:4, cols], ps[0:QT[1], 6, :].rearrange("p (j c) -> p j c", j=4)[:, :, cols])
                        ins = copy(vz[0:T - QT[4], a, 4, cols], ps[0:T - QT[4], 7, cols])
                    ins.then_inc(vz_ready, 1)
                elif n_piece == 4:
                    exponent(0)
                else:
                    s, kind = step_piece(n_piece)
                    if kind == 0 and s + 1 < 2 * NQ:
                        exponent(s + 1)
                    elif kind == 1:
                        by_key(s)

            def low_rank(l):
                act.wait_ge(evacuated, unit_base(l, "wo"))
                act.wait_ge(tiles_ready, 15 * (l + 1))
                act.activation(tile(WA)[0:64, :], tile(WA)[0:64, :], ACT.Tanh).then_inc(lora_in, 1)
                act.activation(tile(GD), tile(GD), ACT.Sigmoid).then_inc(lora_in, 1)
                act.activation(tile(MISC)[0:32, :], tile(MISC)[0:32, :], ACT.Sigmoid).then_inc(lora_in, 1)
                for m in range(WT):
                    n = WT * l + m
                    if m >= 2:
                        act.wait_ge(knorm_done, n - 1)
                    act.activation(k_square[m % 2], tile(K + m), ACT.Square, scale=par(l, KKG + m)).then_inc(ksq_ready, 1)
                    act.wait_ge(decay_done, n + 1)
                    act.activation(halves(ll[:, m, :]), pair(0), ACT.Sigmoid, bias=par(l, DBIAS + m)).then_inc(decay_sig, 1)
                    act.wait_ge(iclr_done, n + 1)
                    act.activation(halves(aa[:, m, :]), pair(2), ACT.Sigmoid, bias=par(l, IBIAS + m)).then_inc(iclr_sig, 1)
                    act.wait_ge(kmax_ready, n + 1)
                    act.activation(root[:, :], tmp[1], ACT.Sqrt).then_inc(kroot_ready, 1)
                    if l:
                        act.wait_ge(vres_done, n - WT + 1)
                        if m:
                            act.wait_ge(v_mixed, n - WT)
                        act.activation(halves(tmp[0]), pair(4), ACT.Sigmoid, bias=par(l, VBIAS + m)).then_inc(vres_sig, 1)

            def chunks(l):
                act.wait_ge(bonus_ready, WT * (l + 1))
                act.wait_ge(bd_zero, 2 * (l + 1))
                act.wait_ge(att_zero, l + 1)

                def prepare_chunk(c, b, n):
                    tokens = bass.ds(c * CHUNK, n)
                    act.activation(e_fwd[b][:, :, 1:n + 1], ll[:, :, tokens], ACT.Exp, scale=-DECAY)
                    act.activation(e_bwd[b][:, :, 0:n], ll[:, :, tokens], ACT.Exp, scale=DECAY).then_inc(e_ready, 1)
                    for a in range(2):
                        ins = copy(bkv[a * HEAD:(a + 1) * HEAD, b, :, 2 * P + a * HEAD:2 * P + a * HEAD + n],
                                   group(V, p0=a * HEAD, p1=(a + 1) * HEAD)[:, :, tokens])
                    ins.then_inc(v_built, 1)

                def copy4(dst, bank):
                    return copy(dst, ps[:, bank, :].rearrange("p (m c) -> p m c", m=WT))

                def chunk(c, b, n, following, beside):
                    cc = c + l * N_CHUNK
                    for pr in range(WT):
                        act.wait_ge(turned, cc * WT + (pr + 1))
                        copy(tok[:, pr, :], ps[:, 2 + pr % 2, 0:3 * P]).then_inc(tok_ready, 1)
                    beside(0)
                    if following:
                        prepare_chunk(c + 1, 1 - b, following)
                    beside(1)
                    for v in range(1, LEVELS):
                        act.wait_ge(q_done, cc * 5 + v)
                        copy4(qm, 1).then_inc(qm_ready, 1)
                        beside(2 * v)
                        beside(2 * v + 1)
                    act.wait_ge(r_done, cc + 1)
                    copy4(rb, 0).then_inc(rb_ready, 1)
                    beside(12)
                    act.wait_ge(sa_done, cc + 1)
                    copy4(sa, 1).then_inc(sa_ready, 1)
                    beside(13)
                    act.wait_ge(o_done, cc + 1)
                    for a in range(2):
                        rows = slice(a * HEAD, (a + 1) * HEAD)
                        ins = copy(group(R, p0=a * HEAD, p1=(a + 1) * HEAD)[:, :, bass.ds(c * CHUNK, n)],
                                   ps[rows, 2, :].rearrange("p (m c) -> p m c", m=WT)[:, :, a * HEAD:a * HEAD + n])
                    ins.then_inc(o_read, 1)
                    beside(14)

                def pair_of_chunks(pr, last):
                    for second in range(2):
                        chunk(pr * 2 + second, second, CHUNK, LAST if last and second else CHUNK,
                              lambda place: [attend(l, pr, n) for n in pieces(second, place)])
                    act.wait_ge(att_done, (pr + l * WT) * NQ + NQ)

                prepare_chunk(0, 0, CHUNK)
                pair_loop(act, pair_of_chunks)
                chunk(N_CHUNK - 1, 0, LAST, 0, lambda place: None)

            def head_outputs(l):
                g, n = 4 * l + 2, WT * l

                def inv_root(dst, bank, bias, read):
                    act.activation(halves(dst), pair(bank), ACT.Ln, bias=bias, scale=1.0 / HEAD).then_inc(read, 1)

                act.wait_ge(mean_done, n + 1)
                for m in range(WT):
                    act.activation(ll[:, m, :], tile(QF + m), ACT.Square).then_inc(fsq_ready, 1)
                for m in range(WT):
                    act.wait_ge(oc_ready, n + m + 1)
                    act.activation(aa[:, m, :], tile(R + m), ACT.Square).then_inc(osq_ready, 1)
                    act.wait_ge(fsum_done, n + m + 1)
                    inv_root(ll[:, m, :], 4 + 2 * (m % 2), eps_pre, fln_ready)
                act.wait_ge(fln_ready, n + WT)
                for m in range(WT):
                    act.activation(ll[:, m, :], ll[:, m, :], ACT.Exp, scale=-0.5).then_inc(frs_ready, 1)
                for m in range(WT):
                    act.wait_ge(var_done, n + m + 1)
                    inv_root(aa[:, m, :], 2 * (m % 2), eps_lnx, oln_ready)
                    act.wait_ge(oln_ready, n + m + 1)
                    act.activation(aa[:, m, :], aa[:, m, :], ACT.Exp, scale=-0.5).then_inc(ors_ready, 1)
                    if m:
                        operands(m - 1, g, n)
                operands(WT - 1, g, n)

            def operands(m, g, n):
                act.wait_ge(f_ready, n + m + 1)
                copy(x_hi[:, m + WT, :], tile(QF + m)).then_inc(x_hi_ready, 1)
                act.wait_ge(o_ready, n + m + 1)
                copy(x_hi[:, m, :], tile(R + m)).then_inc(x_hi_ready, 1)

            def mixer_out(l):
                base = unit_base(l, "wo")

                def unit(k, i):
                    if k < WO_UNITS - 1:
                        split_hi(UNIT, base, k + 1, i)
                    else:
                        split_hi(UNIT, base, WO_UNITS)
                    act.wait_ge(evacuated, i * 2 + (base + k + 1))
                    for j in range(2):
                        square(6 * l + 3, 2 * k + j, 0, y_mix[:, 2 * k + j, :])
                load_ln(3 * l + 1)
                for k in range(WO_UNITS):
                    unit(k, 0)
                split_hi(UNIT, base + WO_UNITS, 1)
                inverse_root(l, 3, 1.0 / D_MODEL, eps_pre)

            for m in range(DT):
                act.dma_start(h[:, m, :], h_in[:, m, :]).then_inc(h_loaded[m], 16)
            act.dma_start(cst[:, :], consts).then_inc(cst_loaded, 16)
            act.wait_ge(small_loaded, 16)
            act.wait_ge(eps_set, 4)
            split_hi(UNIT, 0, 0)
            split_hi(UNIT, 0, 1)
            for l in range(DEPTH):
                prepare(l, 0, 0, unit_base(l, "a"))
                ffn(l, "a", 2 * l, 0)
                prepare(l, 1, 2, unit_base(l, "proj"))
                projection(l)
                forget_gates(l)
                low_rank(l)
                chunks(l)
                act.wait_ge(mean_done, WT * l + 1)
                split_hi(UNIT, unit_base(l, "wo"), 0)
                head_outputs(l)
                mixer_out(l)
                prepare(l, 3, 4, unit_base(l, "b"))
                ffn(l, "b", 2 * l + 1, 4)

        @block.vector
        def _(dve):
            links = [0]

            def link(ins):
                links[0] += 1
                ins.then_inc(dve_step, 1)
                dve.wait_ge(dve_step, links[0])

            def split_lo(cols, base, k, i=0):
                q = slot(base, k)
                dve.wait_ge(hi_ready, i * 2 + (base + k + 1))
                dve.tensor_tensor(w_lo[:, q, 0:cols], raw[:, q, 0:cols], w_hi[:, q, 0:cols], ALU.subtract).then_inc(w_split, 1)

            def x_lo_of(l, g, n, m):
                dve.wait_ge(x_hi_ready, DT * (4 * l + g) + m + 1)
                dve.scalar_tensor_tensor(x_lo[:, m, :], h[:, m, :], par(l, GAIN + n * DT + m), x_hi[:, m, :],
                                         ALU.mult, ALU.subtract).then_inc(x_lo_ready, 1)

            def update(l, post, y, following):
                by_pool, own = len(POOL_TILES) * (3 * l + post), (DT - len(POOL_TILES)) * (3 * l + post)
                dve.wait_ge(rs_ready, 6 * l + 2 * post + 2)

                def scale(m):
                    dve.tensor_tensor(y[:, m, :], y[:, m, :], rs_post[:, :], ALU.mult).then_inc(y_scaled_dve, 1)

                todo = [m for m in range(DT) if m not in POOL_TILES]
                scale(todo[0])
                for m in range(DT):
                    if m + 1 < len(todo):
                        scale(todo[m + 1])
                    if m in POOL_TILES:
                        by_pool += 1
                        dve.wait_ge(y_scaled, by_pool)
                    else:
                        own += 1
                        dve.wait_ge(y_scaled_dve, own)
                    dve.scalar_tensor_tensor(h[:, m, :], y[:, m, :], par(l, GAIN + (2 * post + 1) * DT + m), h[:, m, :],
                                             ALU.mult, ALU.add).then_inc(h_ready, 1)
                if following:
                    for m in range(DT):
                        x_lo_of(*following, m)

            def ffn(l, which, f, n):
                for fh in range(2):
                    base = unit_base(l, which) + fh * (FH + DT)

                    def unit_in(k, i):
                        u, q = i * 2 + k, slot(base, k)
                        e = u + (FH * (2 * f + fh) + 1)
                        if k == FH - 1:
                            split_lo(OUT_UNIT, base, FH)
                        elif not (fh == 0 and k == 0):
                            split_lo(UNIT, base, k + 1, i)
                        dve.wait_ge(gate_done, e)
                        if fh == 0 and k == 0:
                            dve.wait_ge(rs_ready, 6 * l + n + 1)
                        dve.tensor_tensor(halves(gs[:, q, :]), pair(4 * q), halves(rs_pre[:, :]), ALU.mult).then_inc(gs_ready, 1)
                        dve.wait_ge(unit_done, u + (base + 1))
                        dve.tensor_tensor(halves(us[:, q, :]), pair(4 * q + 2), halves(rs_pre[:, :]), ALU.mult).then_inc(evacuated, 1)
                        dve.wait_ge(hid_hi_ready, e)
                        dve.tensor_tensor(hid_lo[:, u, :], hid[:, q, :], hid_hi[:, u, :], ALU.subtract).then_inc(hid_lo_ready, 1)

                    def unit_out(k, i):
                        u, q = i * 2 + k, slot(base + FH, k)
                        if k < DT - 1:
                            split_lo(OUT_UNIT, base + FH, k + 1, i)
                        elif not (l == DEPTH - 1 and which == "b" and fh == 1):
                            split_lo(UNIT, base, FH + DT)
                        dve.wait_ge(unit_done, u + (base + FH + 1))
                        if fh == 0:
                            dve.tensor_copy(halves(y_ffn[:, u, :]), pair(4 * q)).then_inc(evacuated, 1)
                        else:
                            dve.tensor_tensor(halves(y_ffn[:, u, :]), pair(4 * q), halves(y_ffn[:, u, :]), ALU.add).then_inc(evacuated, 1)

                    units(dve, FH, unit_in)
                    units(dve, DT, unit_out)
                if not (l == DEPTH - 1 and which == "b"):
                    split_lo(UNIT, base + FH + DT, 1)

            def projection(l):
                base = unit_base(l, "proj")

                def next_split(k, i):
                    if 0 < k < PROJ_UNITS - 1:
                        split_lo(UNIT // 2 if k == PROJ_UNITS - 2 else UNIT, base, k + 1, i)

                def heads_unit(k, i):
                    next_split(k, i)
                    dve.wait_ge(unit_done, i * 2 + (base + k + 1))
                    if k == 0:
                        dve.wait_ge(rs_ready, 6 * l + 3)
                    for j in range(2):
                        dst = tiles[:, bass.ds((i * 4 + (2 * k + j)) * T, T)] if not isinstance(i, int) else tile(2 * k + j)
                        ins = dve.tensor_tensor(halves(dst), pair(4 * slot(base, k) + 2 * j), halves(rs_pre[:, :]), ALU.mult)
                    ins.then_inc(evacuated, 1)

                def shifted_unit(k, i):
                    single = k == PROJ_UNITS - 1
                    next_split(k, i)
                    u = i * 2 + k
                    dve.wait_ge(unit_done, u + (base + 1))
                    wait(dve, tiles_ready, i * 4 + (15 * l + 2 * k - R))
                    for j in range(1 if single else 2):
                        ins = dve.tensor_tensor(halves(shifted[j][:, 1:T + 1]), pair(4 * slot(base, k) + 2 * j), halves(rs_pre[:, :]), ALU.mult)
                    ins.then_inc(evacuated, 1)
                    for j in range(1 if single else 2):
                        number = 2 * k + j - R
                        dve.wait_ge(delta_ready, i * 4 + (15 * l + number + 1))
                        if isinstance(i, int):
                            dst, mu = tile(R + number), par(l, MU + number)
                        else:
                            dst = tiles[:, bass.ds((i * 4 + (R + number)) * T, T)]
                            mu = prm[:, bass.ds(i * 4 + (l * N_PAR + MU + number), 1)]
                        dve.scalar_tensor_tensor(dst, delta[j], mu, shifted[j][:, 1:T + 1], ALU.mult, ALU.add).then_inc(tiles_ready, 1)

                for j in range(2):
                    link(dve.memset(shifted[j][:, 0:1], 0.0))
                units(dve, R // 2, heads_unit)
                units(dve, PROJ_UNITS - R // 2, shifted_unit, R // 2)

            def forget_gates(l):
                row = slice(FORGET_ROW, FORGET_ROW + HEADS)
                link(dve.memset(c_all[:, :], 0.0))
                dve.wait_ge(tiles_ready, 15 * (l + 1))
                link(dve.tensor_scalar(fg[row, 0, :], tile(MISC)[row, :], par(l, FBIAS, FORGET_ROW, FORGET_ROW + HEADS), None, ALU.add))
                dve.scalar_tensor_tensor(fg[row, 1, :], fg[row, 0, :], -1.0, fg[row, 0, :], ALU.mult, ALU.min).then_inc(fg_abs, 1)
                dve.wait_ge(fg_exp, l + 1)
                link(dve.scalar_tensor_tensor(fg[row, 0, :], fg[row, 0, :], 0.0, fg[row, 1, :], ALU.min, ALU.subtract))
                dve.tensor_tensor_scan(c_all[row, :], cst[row, ONES:ONES + 1].broadcast_to([HEADS, T]), fg[row, 0, :], 0.0,
                                       ALU.mult, ALU.add).then_inc(c_ready, 1)

            def attend(l, pr, n_piece):
                pairs = pr + l * WT
                step = pairs * (2 * NQ)

                def soft(s):
                    j, a = divmod(s, 2)
                    nk = QT[j + 1]
                    n = nk - QT[j]
                    dve.wait_ge(scored, step + (s + 1))
                    c_query = c_tok[0:n, j, bass.ds(pr * 2 + a, 1)]
                    if nk <= 512:
                        dve.scalar_tensor_tensor(score[0:n, a, 0:nk], ps[0:n, 4 + a, 0:nk], c_query, c_key[0:n, a, 0:nk],
                                                 ALU.add, ALU.add).then_inc(score_read, 1)
                    else:
                        dve.scalar_tensor_tensor(halves(score[0:n, a, :]), ps[0:n, 4:6, 0:HT], c_query, halves(c_key[0:n, a, :]),
                                                 ALU.add, ALU.add).then_inc(score_read, 1)
                    dve.wait_ge(score_read, step + (s + 1))
                    own = score[0:n, a, QT[j]:nk]
                    dve.tensor_tensor(own, own, cst[0:n, CAUSAL:CAUSAL + n], ALU.add).then_inc(masked, 1)
                    dve.wait_ge(masked, step + (s + 1))
                    dve.tensor_reduce(neg_max[0:n, a:a + 1], score[0:n, a, 0:nk], AX.X, ALU.max, negate=True).then_inc(max_ready, 1)

                def scale(s):
                    j, a = divmod(s, 2)
                    n = QT[j + 1] - QT[j]
                    dve.wait_ge(prob_ready, step + (s + 1))
                    dve.reciprocal(inv_sum[0:n, a:a + 1], row_sum[0:n, a:a + 1]).then_inc(inv_ready, 1)
                    dve.wait_ge(inv_ready, step + (s + 1))
                    if s >= 2:
                        dve.wait_ge(prob_turned, step + (s - 1))
                    dve.tensor_scalar(diag[0:n, a, 0:n], cst[0:n, IDENT:IDENT + n], inv_sum[0:n, a:a + 1], None, ALU.mult).then_inc(diag_ready, 1)

                if n_piece == 0:
                    for a in range(2):
                        dve.tensor_scalar(c_one[:, a, :], c_all[:, :], cst[:, bass.ds(pr * 2 + (IDENT + FORGET_ROW + a), 1)], -1.0,
                                          ALU.mult, ALU.mult).then_inc(c_one_ready, 1)
                elif n_piece == 4:
                    soft(0)
                elif n_piece > 4:
                    s, kind = step_piece(n_piece)
                    j, a = divmod(s, 2)
                    if kind == 0:
                        scale(s)
                        if s + 1 < 2 * NQ:
                            soft(s + 1)
                    elif kind == 2 and a == 1:
                        n = QT[j + 1] - QT[j]
                        dve.wait_ge(att_done, pairs * NQ + (j + 1))
                        dve.tensor_copy(tiles[:, bass.ds((pr + QF) * T + QT[j], n)], ps[:, 7, 0:n]).then_inc(att_read, 1)

            def low_rank(l):
                for m in range(WT):
                    n = WT * l + m
                    dve.wait_ge(decay_sig, n + 1)
                    link(dve.tensor_tensor_scan(ll[:, m, :], cst[:, RESET:RESET + T], ll[:, m, :], 0.0, ALU.mult, ALU.add))
                    link(dve.tensor_scalar(kk[:, m, :], tile(K + m), par(l, KKG + m), None, ALU.mult))
                    dve.wait_ge(knorm_done, n + 1)
                    dve.tensor_scalar(halves(tmp[1]), pair(6), 1e-24, None, ALU.max).then_inc(kmax_ready, 1)
                    dve.wait_ge(kroot_ready, n + 1)
                    link(dve.reciprocal(tmp[2], root[:, :]))
                    link(dve.tensor_tensor(kk[:, m, :], kk[:, m, :], tmp[2], ALU.mult))
                    dve.wait_ge(iclr_sig, n + 1)
                    link(dve.tensor_scalar(tmp[2], aa[:, m, :], 1.0, par(l, KAG + m), ALU.subtract, ALU.mult))
                    dve.wait_ge(ksq_ready, n + 1)
                    link(dve.scalar_tensor_tensor(tile(K + m), tmp[2], 1.0, tile(K + m), ALU.add, ALU.mult))
                    link(dve.tensor_tensor(aa[:, m, :], kk[:, m, :], aa[:, m, :], ALU.mult))
                    if l == 0:
                        link(dve.tensor_copy(v_first[:, m, :], tile(V + m)))
                    else:
                        dve.wait_ge(vres_sig, n - WT + 1)
                        link(dve.tensor_tensor(tmp[2], v_first[:, m, :], tile(V + m), ALU.subtract))
                        dve.tensor_tensor(tmp[2], tmp[2], tmp[0], ALU.mult).then_inc(v_mixed, 1)
                        dve.wait_ge(v_mixed, n - WT + 1)
                        link(dve.tensor_tensor(tile(V + m), tile(V + m), tmp[2], ALU.add))
                    dve.scalar_tensor_tensor(bonus[:, m, :], tile(R + m), par(l, RKG + m), tile(K + m), ALU.mult, ALU.mult).then_inc(rk_ready, 1)
                for m in range(WT):
                    n = WT * l + m
                    dve.wait_ge(bonus_done, n + 1)
                    dve.tensor_tensor(halves(bonus[:, m, :]), pair(2 * (m % 2)), halves(tile(V + m)), ALU.mult).then_inc(bonus_ready, 1)
                dve.wait_ge(bonus_ready, WT * (l + 1))

            def chunks(l):
                for b in range(2):
                    dve.memset(e_fwd[b][:, :, 0:1], 1.0)
                dve.memset(hs, 0.0)
                dve.memset(ar[:, :, :, :], 0.0).then_inc(bd_zero, 1)
                dve.wait_ge(bd_zero, 2 * (l + 1))

                def build_ar(c, b, n, cc):
                    tokens = bass.ds(c * CHUNK, n)
                    dve.wait_ge(e_ready, cc + 1)
                    for a in range(2):
                        rows = slice(a * HEAD, (a + 1) * HEAD)
                        dve.scalar_tensor_tensor(ar[rows, b, :, a * HEAD:a * HEAD + n], kk[rows, :, tokens], -1.0, e_fwd[b][rows, :, 0:n], ALU.mult, ALU.mult)
                        ins = dve.tensor_tensor(ar[rows, b, :, P + a * HEAD:P + a * HEAD + n],
                                                group(R, p0=a * HEAD, p1=(a + 1) * HEAD)[:, :, tokens], e_fwd[b][rows, :, 1:n + 1], ALU.mult)
                    ins.then_inc(ar_built, 1)

                def bank4(bank):
                    return ps[:, bank, :].rearrange("p (m c) -> p m c", m=WT)

                def chunk(c, b, n, following, beside):
                    cc = c + l * N_CHUNK
                    for pr in range(WT):
                        dve.wait_ge(gram_done, cc * WT + (pr + 1))
                        dve.tensor_tensor(gm[:, pr, :].rearrange("p (i c) -> p i c", i=2), ps[:, pr % 2, :].rearrange("p (i c) -> p i c", i=2),
                                          spread(cst[:, PAIRMASK:PAIRMASK + 256], 2), ALU.mult).then_inc(gram_ready, 1)
                    beside(0)
                    dve.wait_ge(off_ready, cc * LEVELS + 1)
                    dve.tensor_tensor(ym, uo, ident4, ALU.add).then_inc(y_ready, 1)
                    dve.wait_ge(z0_done, cc + 1)
                    dve.tensor_tensor(zm, bank4(0), ident4, ALU.add).then_inc(z_ready, 1)
                    beside(1)
                    for v in range(1, LEVELS):
                        beside(2 * v)
                        if v < LEVELS - 1:
                            dve.wait_ge(zd_done, cc * 4 + v)
                            dve.tensor_tensor(zm, bank4(2), zm, ALU.add).then_inc(z_ready, 1)
                        dve.wait_ge(yd_done, cc * 5 + v)
                        dve.tensor_tensor(ym, bank4(3), ym, ALU.add).then_inc(y_ready, 1)
                        beside(2 * v + 1)
                        if v == 2 and following:
                            build_ar(c + 1, 1 - b, following, cc + 1)
                    beside(12)
                    beside(13)
                    dve.wait_ge(hd_done, cc + 1)
                    dve.tensor_tensor(hs, bank4(3), hs, ALU.add).then_inc(h_added, 1)
                    dve.wait_ge(h_added, cc + 1)
                    dve.tensor_tensor(hs, hs, e_fwd[b][:, :, n:n + 1].broadcast_to([P, WT, P]), ALU.mult).then_inc(state_ready, 1)
                    beside(14)

                def pair_of_chunks(pr, last):
                    for second in range(2):
                        chunk(pr * 2 + second, second, CHUNK, LAST if last and second else CHUNK,
                              lambda place: [attend(l, pr, n) for n in pieces(second, place)])
                    dve.wait_ge(prob_turned, (pr + l * WT) * (2 * NQ) + 2 * NQ)

                build_ar(0, 0, CHUNK, l * N_CHUNK)
                pair_loop(dve, pair_of_chunks)
                chunk(N_CHUNK - 1, 0, LAST, 0, lambda place: None)

            def head_outputs(l):
                g, n = 4 * l + 2, WT * l

                def lows(m):
                    for i, (src, k) in enumerate(((tile(QF + m), m + WT), (tile(R + m), m))):
                        dve.wait_ge(x_hi_ready, DT * g + 2 * m + i + 1)
                        dve.tensor_tensor(x_lo[:, k, :], src, x_hi[:, k, :], ALU.subtract).then_inc(x_lo_ready, 1)

                for m in range(WT):
                    dve.wait_ge(mean_done, n + m + 1)
                    dve.scalar_tensor_tensor(halves(tile(R + m)), pair(2 * (m % 2)), -1.0 / HEAD, halves(tile(R + m)), ALU.mult, ALU.add).then_inc(oc_ready, 1)
                for m in range(WT):
                    o, of = tile(R + m), tile(QF + m)
                    dve.wait_ge(frs_ready, n + m + 1)
                    dve.scalar_tensor_tensor(of, of, par(l, FOXG + m), ll[:, m, :], ALU.mult, ALU.mult).then_inc(f_ready, 1)
                    dve.wait_ge(ors_ready, n + m + 1)
                    link(dve.tensor_tensor(o, o, aa[:, m, :], ALU.mult))
                    link(dve.tensor_scalar(o, o, par(l, LNW + m), par(l, LNB + m), ALU.mult, ALU.add))
                    link(dve.tensor_tensor(o, o, bonus[:, m, :], ALU.add))
                    dve.wait_ge(g_done, n + m + 1)
                    dve.tensor_tensor(halves(o), halves(o), pair(4 + 2 * (m % 2)), ALU.mult).then_inc(o_ready, 1)
                    if m:
                        lows(m - 1)
                lows(WT - 1)

            def mixer_out(l):
                base = unit_base(l, "wo")

                for k in range(WO_UNITS):
                    q = slot(base, k)
                    split_lo(UNIT, base, k + 1)
                    dve.wait_ge(unit_done, base + k + 1)
                    for j in range(2):
                        ins = dve.tensor_copy(halves(y_mix[:, 2 * k + j, :]), pair(4 * q + 2 * j))
                    ins.then_inc(evacuated, 1)
                split_lo(UNIT, base + WO_UNITS, 1)

            dve.memset(eps[:, 0:1], NORM_EPS).then_inc(eps_set, 1)
            dve.memset(eps[:, 1:2], 4 * NORM_EPS).then_inc(eps_set, 1)
            dve.memset(eps[:, 2:3], LNX_EPS).then_inc(eps_set, 1)
            dve.memset(eps[:, 3:4], 1.0).then_inc(eps_set, 1)
            dve.wait_ge(small_loaded, 16)
            split_lo(UNIT, 0, 0)
            split_lo(UNIT, 0, 1)
            for m in range(DT):
                dve.wait_ge(h_loaded[m], 16)
                x_lo_of(0, 0, 0, m)
            dve.wait_ge(cst_loaded, 16)
            for l in range(DEPTH):
                ffn(l, "a", 2 * l, 0)
                update(l, 0, y_ffn, (l, 1, 2))
                projection(l)
                forget_gates(l)
                low_rank(l)
                chunks(l)
                split_lo(UNIT, unit_base(l, "wo"), 0)
                head_outputs(l)
                mixer_out(l)
                update(l, 1, y_mix, (l, 3, 4))
                ffn(l, "b", 2 * l + 1, 4)
                update(l, 2, y_ffn, (l + 1, 0, 0) if l + 1 < DEPTH else None)

        @block.gpsimd
        def _(pool):
            def add_squares(s, k, i=0):
                if k in (0, DT - 1):
                    return
                count = i * 2 + ((DT - 2) * s + k)
                pool.wait_ge(sq_ready, i * 2 + (DT * s + k + 1))
                wait(pool, acc_added, count - 1)
                pool.tensor_tensor(acc[:, :], acc[:, :], sqb[:, k % 2, :], ALU.add).then_inc(acc_added, 1)

            def ffn(l, which, f, n):
                for m in range(DT):
                    add_squares(6 * l + n, m)
                for fh in range(2):
                    base = unit_base(l, which) + fh * (FH + DT)

                    def unit_in(k, i):
                        u, q = i * 2 + k, slot(base, k)
                        pool.wait_ge(sg_ready, u + (FH * (2 * f + fh) + 1))
                        pool.wait_ge(evacuated, u + (base + 1))
                        pool.tensor_tensor(hid[:, q, :], sg[:, q, :], us[:, q, :], ALU.mult).then_inc(hid_ready, 1)
                    units(pool, FH, unit_in)
                    if fh == 1:
                        units(pool, DT, lambda k, i: add_squares(6 * l + n + 1, k, i))

            def scale_y(l, post, y):
                pool.wait_ge(rs_ready, 6 * l + 2 * post + 2)
                for m in POOL_TILES:
                    pool.tensor_tensor(y[:, m, :], y[:, m, :], rs_post[:, :], ALU.mult).then_inc(y_scaled, 1)

            def projection(l):
                for m in range(DT):
                    add_squares(6 * l + 2, m)
                base = unit_base(l, "proj")

                def unit(k, i):
                    pool.wait_ge(evacuated, i * 2 + (base + k + 1))
                    for j in range(1 if k == PROJ_UNITS - 1 else 2):
                        pool.tensor_tensor(delta[j], shifted[j][:, 0:T], shifted[j][:, 1:T + 1], ALU.subtract).then_inc(delta_ready, 1)
                units(pool, PROJ_UNITS - R // 2, unit, R // 2)

            def chunks(l):
                pool.memset(bkv[:, :, :, :], 0.0).then_inc(bd_zero, 1)
                pool.wait_ge(bd_zero, 2 * (l + 1))
                pool.wait_ge(bonus_ready, WT * (l + 1))

                def build_bk(c, b, n, cc):
                    tokens = bass.ds(c * CHUNK, n)
                    pool.wait_ge(e_ready, cc + 1)
                    for a in range(2):
                        rows = slice(a * HEAD, (a + 1) * HEAD)
                        for i, src in enumerate((aa[rows, :, :], group(K, p0=a * HEAD, p1=(a + 1) * HEAD))):
                            pool.tensor_tensor(bkv[rows, b, :, i * P + a * HEAD:i * P + a * HEAD + n], src[:, :, tokens],
                                               e_bwd[b][rows, :, 0:n], ALU.mult).then_inc(bkv_built, 1)
                            pool.wait_ge(bkv_built, cc * 4 + (2 * a + i + 1))

                def chunk(c, b, n, following):
                    cc = c + l * N_CHUNK
                    pool.wait_ge(gram_ready, cc * WT + WT)
                    for v in range(LEVELS):
                        if v == 1:
                            pool.wait_ge(z0_done, cc + 1)
                            pool.wait_ge(y_ready, cc * LEVELS + 1)
                        if v > 1:
                            pool.wait_ge(q_done, cc * 5 + (v - 1))
                        pool.tensor_tensor(uo, gm[:, :, 0:P], spread(cst[:, LEVEL + v * P:LEVEL + (v + 1) * P], WT), ALU.mult).then_inc(off_ready, 1)
                        if v == 2 and following:
                            pool.wait_ge(off_ready, cc * LEVELS + 3)
                            build_bk(c + 1, 1 - b, following, cc + 1)

                def pair_of_chunks(pr, last):
                    chunk(pr * 2, 0, CHUNK, CHUNK)
                    chunk(pr * 2 + 1, 1, CHUNK, LAST if last else CHUNK)

                build_bk(0, 0, CHUNK, l * N_CHUNK)
                pair_loop(pool, pair_of_chunks)
                chunk(N_CHUNK - 1, 0, LAST, 0)

            for l in range(DEPTH):
                ffn(l, "a", 2 * l, 0)
                scale_y(l, 0, y_ffn)
                projection(l)
                pool.wait_ge(evacuated, unit_base(l, "wo"))
                pool.wait_ge(tiles_ready, 15 * (l + 1))
                pool.memset(qz[:, :, :], 0.0)
                pool.memset(vz[:, :, :, :], 0.0).then_inc(att_zero, 1)
                chunks(l)
                for m in range(DT):
                    add_squares(6 * l + 3, m)
                scale_y(l, 1, y_mix)
                ffn(l, "b", 2 * l + 1, 4)
                scale_y(l, 2, y_ffn)


_OUT = (P, DT, SEQ)


def constants():
    c = np.zeros((P, N_CONST), np.float32)
    s, t = np.arange(P)[:, None], np.arange(P)[None, :]
    same = s // HEAD == t // HEAD
    c[:, IDENT:IDENT + P] = s == t
    c[:, ONES:ONES + P] = 1
    c[:, HEADSUM:HEADSUM + P] = same
    c[:, CAUSAL:CAUSAL + P] = np.where(t > s, NEG, 0)
    c[:, PAIRMASK:PAIRMASK + P] = same & (s < t)
    c[:, PAIRMASK + P:PAIRMASK + 2 * P] = same & (s <= t)
    for v in range(LEVELS):
        b = 1 << v
        c[:, LEVEL + v * P:LEVEL + (v + 1) * P] = same & (s < t) & (s // (2 * b) == t // (2 * b)) & (s // b != t // b)
    c[:, RESET:RESET + T] = np.arange(T)[None, :] % CHUNK != 0
    return c


def lay_out(x, meta_tokens, norm_gains, ffn_w_in, ffn_w_out, w_in, w_in_vres, shift_mu, shift_mu_vres,
            decay_up, decay_bias, iclr_up, iclr_bias, gate_up, vres_up, vres_bias, k_k, k_a, r_k,
            ln_x_w, ln_x_b, forget_bias, fox_out_gain, w_out):
    f = np.float32
    tokens = np.concatenate([meta_tokens, x[0]], axis=0)
    h_in = tokens.T.reshape(DT, P, T).transpose(1, 0, 2)
    win = ffn_w_in.reshape(DEPTH * 2, DT, P, 2, FT, P).transpose(0, 4, 2, 3, 1, 5).reshape(DEPTH * 2, FT, P, UNIT)
    wout = ffn_w_out.reshape(DEPTH * 2, 2, FH, P, DT, P).transpose(0, 1, 4, 3, 2, 5).reshape(DEPTH * 2, 2, DT, P, OUT_UNIT)
    w3 = 3 * WIDTH
    n_rwkv = w3 + 64 + 64 + 160
    cols = np.zeros((DEPTH, D_MODEL, (N_TILES + 1) * P), f)
    mu = np.zeros((DEPTH, (N_TILES - R) * P), f)
    cols[:, :, 0:w3] = w_in[:, :, n_rwkv:n_rwkv + w3]
    cols[:, :, w3:2 * w3 + 256] = w_in[:, :, 0:w3 + 256]
    mu[:, 0:w3 + 256] = shift_mu[:, 0:w3 + 256]
    misc = MISC * P
    cols[:, :, misc:misc + 32] = w_in[:, :, w3 + 256:n_rwkv]
    mu[:, misc - R * P:misc - R * P + 32] = shift_mu[:, w3 + 256:n_rwkv]
    cols[1:, :, misc + 32:misc + 64] = w_in_vres
    mu[1:, misc - R * P + 32:misc - R * P + 64] = shift_mu_vres
    cols[:, :, misc + FORGET_ROW:misc + FORGET_ROW + HEADS] = w_in[:, :, n_rwkv + w3:]
    proj = cols.reshape(DEPTH, DT, P, PROJ_UNITS, 2, P).transpose(0, 3, 2, 4, 1, 5).reshape(DEPTH, PROJ_UNITS, P, UNIT)
    wo = w_out.reshape(DEPTH, DT, P, WO_UNITS, 2, P).transpose(0, 3, 2, 4, 1, 5).reshape(DEPTH, WO_UNITS, P, UNIT)
    lora = np.zeros((DEPTH, P, 5 * WIDTH), f)
    lora[:, 0:64, 0:WIDTH] = decay_up
    lora[:, 64:128, WIDTH:2 * WIDTH] = iclr_up
    lora[1:, 32:64, 2 * WIDTH:3 * WIDTH] = vres_up
    lora[:, :, 3 * WIDTH:4 * WIDTH] = gate_up[:, 0:P]
    lora[:, 0:32, 4 * WIDTH:5 * WIDTH] = gate_up[:, P:]
    params = np.zeros((P, DEPTH, N_PAR), f)

    def columns(col, a):
        a = a.reshape(DEPTH, -1, P).transpose(2, 0, 1)
        params[:, :, col:col + a.shape[2]] = a
    columns(GAIN, norm_gains)
    columns(MU, mu)
    vb = np.zeros((DEPTH, WIDTH), f)
    vb[1:] = vres_bias
    for col, a in ((DBIAS, decay_bias), (IBIAS, iclr_bias), (VBIAS, vb), (KKG, k_k), (KAG, k_a), (RKG, r_k),
                   (LNW, ln_x_w), (LNB, ln_x_b), (FOXG, fox_out_gain)):
        columns(col, a)
    params[FORGET_ROW:FORGET_ROW + HEADS, :, FBIAS] = forget_bias.T
    return {"h_in": h_in, "ffn_in": win, "ffn_out": wout, "proj": proj, "w_out": wo, "lora": lora,
            "params": params.reshape(P, DEPTH * N_PAR), "consts": constants()}


def kernel(**inputs):
    import concourse.bacc as bacc
    from concourse.bass_utils import run_bass_kernel_spmd

    arrays = {k: np.ascontiguousarray(v) for k, v in lay_out(**{k: np.asarray(v) for k, v in inputs.items()}).items()}
    nc = bacc.Bacc("TRN2", target_bir_lowering=False, num_devices=1, dynamic_dma_scratch_size=1024)
    args = [nc.dram_tensor(f"in_{k}", a.shape, F32, kind="ExternalInput").ap() for k, a in arrays.items()]
    out = nc.dram_tensor("out_h", _OUT, F32, kind="ExternalOutput").ap()
    build(nc, *args, out)
    r = run_bass_kernel_spmd(nc, [{f"in_{k}": a for k, a in arrays.items()}], core_ids=[0])
    got = r.results[0]["out_h"]
    return np.ascontiguousarray(got.transpose(2, 1, 0)).reshape(1, SEQ, D_MODEL)
```

```python
from contextlib import ExitStack

import numpy as np

import concourse.bass as bass
from concourse import mybir

D_MODEL = 1024
SEQ = 512
N_META = 16
DEPTH = 2
D_FF = 2816
HEAD = 64
WIDTH = 512
P = 128
T = SEQ + N_META
HT = T // 2
DT = D_MODEL // P
WT = WIDTH // P
FT = D_FF // P
FH = FT // 2
CHUNK = 64
N_CHUNK = -(-T // CHUNK)
LAST = T - (N_CHUNK - 1) * CHUNK
LEVEL_COUNT = {CHUNK: 6, LAST: 4}
QT = [0, 107, 214, 321, 428, 528]
NQ = len(QT) - 1
HEADS = WIDTH // HEAD
NORM_EPS = 1e-6
LNX_EPS = 64e-5
DECAY = float(np.exp(-0.5))
NEG = -1e30

BONUS_BANKS = (0, 2, 6, 4)
POOL_TILES = (0, 2, 4)

UNIT = 16 * P
OUT_UNIT = FH * P
FFN_UNITS = 2 * (FH + DT)
PROJ_UNITS = 14
WO_UNITS = DT // 2
LAYER_UNITS = 2 * FFN_UNITS + PROJ_UNITS + WO_UNITS

QF, KF, VF, R, K, V, WA, GD, MISC = 0, 4, 8, 12, 16, 20, 24, 25, 26
N_TILES = 27
FORGET_ROW = 64

GAIN, MU = 0, 6 * DT
DBIAS = MU + N_TILES - R
IBIAS, VBIAS, KKG, KAG, RKG, LNW, LNB, FOXG = (DBIAS + WT * n for n in range(1, 9))
FBIAS = FOXG + WT
N_PAR = FBIAS + 1

LEVELS = 6
IDENT, ONES, HEADSUM, CAUSAL = 0, 128, 256, 384
MASK = {CHUNK: 512, LAST: 512 + 3 * CHUNK}
LEVEL = MASK[LAST] + 3 * LAST
RESET = LEVEL + LEVELS * P
N_CONST = RESET + T

F32 = mybir.dt.float32
F32R = mybir.dt.float32r
ALU = mybir.AluOpType
ACT = mybir.ActivationFunctionType
AX = mybir.AxisListType


def build(nc, h_in, ffn_in, ffn_out, proj, w_out, lora, params, consts, out):
    ctx = ExitStack()
    with ctx:
        def sb(name, shape, dt=F32):
            return ctx.enter_context(nc.sbuf_tensor(name, shape, dt))

        def sem(name):
            return ctx.enter_context(nc.semaphore(name))

        h = sb("h", [P, DT, T])
        raw = sb("raw", [P, 2, UNIT])
        v_first = sb("v_first", [P, WT, T])
        cst = sb("cst", [P, N_CONST])
        prm = sb("prm", [P, DEPTH * N_PAR])
        root = sb("root", [P, T])
        rs_pre = sb("rs_pre", [P, T])
        rs_post = sb("rs_post", [P, T])
        acc = sb("acc", [P, T])
        sqb = sb("sqb", [P, 2, T])
        eps = sb("eps", [P, 4])
        warm = sb("warm", [P, 3 * DEPTH])

        e_all = sb("e_all", [P, 2, WT * (2 * CHUNK + 1)])

        with ExitStack() as low:
            def lo_sb(name, shape, dt=F32):
                return low.enter_context(nc.sbuf_tensor(name, shape, dt))
            qz = lo_sb("qz", [P, 2, T])
            vz = lo_sb("vz", [P, 2, NQ, P])
            prob_t = lo_sb("prob_t", [P, 2, NQ, QT[1]])
            diag = lo_sb("diag", [P, 2, P])
            c_tok = lo_sb("c_tok", [P, NQ, HEADS])
            neg_max = lo_sb("neg_max", [P, 2])
            row_sum = lo_sb("row_sum", [P, 2])
            inv_sum = lo_sb("inv_sum", [P, 2])
            ar = lo_sb("ar", [P, 2, WT, P])
            a_blocks = lo_sb("a_blocks", [P, 2, WT, P])
            bkv = lo_sb("bkv", [P, 2, WT, 3 * P])
            gm = lo_sb("gm", [P, WT, 3 * P])
            tok = lo_sb("tok", [P, WT, 3 * P])
            work = lo_sb("work", [P, 7, WT, P])
        x_hi = sb("x_hi", [P, DT, T], F32R)
        x_lo = sb("x_lo", [P, DT, T], F32R)
        w_hi = sb("w_hi", [P, 2, UNIT], F32R)
        w_lo = sb("w_lo", [P, 2, UNIT], F32R)
        with ExitStack() as f:
            def ff_sb(name, shape, dt=F32):
                return f.enter_context(nc.sbuf_tensor(name, shape, dt))
            hid_hi = ff_sb("hid_hi", [P, FH, T], F32R)
            hid_lo = ff_sb("hid_lo", [P, FH, T], F32R)
            y_ffn = ff_sb("y_ffn", [P, DT, T])
            gs = ff_sb("gs", [P, 2, T])
            us = ff_sb("us", [P, 2, T])
            sg = ff_sb("sg", [P, 2, T])
            hid = ff_sb("hid", [P, 2, T])
        tiles = sb("tiles", [P, N_TILES * T])
        aa = sb("aa", [P, WT, T])
        ll = sb("ll", [P, WT, T])
        kk = sb("kk", [P, WT, T])
        bonus = sb("bonus", [P, WT, T])

        ps = ctx.enter_context(nc.psum_tensor("ps", [P, 8, 512], F32))

        def spread(ap, n):
            return ap.unsqueeze(1).broadcast_to([ap.shape[0], n, ap.shape[1]])

        def tile(i, n=1):
            return tiles[:, i * T:(i + n) * T]

        def group(i, c0=0, c1=T, p0=0, p1=P):
            return tiles[p0:p1, i * T:(i + WT) * T].rearrange("p (m t) -> p m t", m=WT)[:, :, c0:c1]

        ym, zm, qm, uo, rb, sa, hs = (work[:, n, :, :] for n in range(7))
        lora_w = gm[:, :, :].rearrange("p m c -> p (m c)")[:, 0:3 * WIDTH]
        spare = work[:, :, :, :].rearrange("p n m c -> p (n m c)")
        v_weight = [spare[:, n * T:(n + 1) * T] for n in range(WT)]
        k_inverse = [root[:, :], rs_post[:, :]] + [spare[:, n * T:(n + 1) * T] for n in (4, 5)]
        gate_w = tiles[:, KF * T:KF * T + 2 * WIDTH]
        y_mix = tiles[:, KF * T:(KF + DT) * T].rearrange("p (m t) -> p m t", m=DT)
        slots = raw[:, :, :].rearrange("p q c -> p (q c)")
        prob, c_one, c_key = (slots[:, 2 * n * T:2 * (n + 1) * T].rearrange("p (a t) -> p a t", a=2) for n in range(3))
        v_pair = slots[:, 6 * T:7 * T]
        k_square = [prob[:, q, :] for q in range(2)]
        v_mix = [c_one[:, q, :] for q in range(2)]
        score = sqb
        c_all = acc
        fg = score
        e_fwd = [e_all[:, q, 0:WT * (CHUNK + 1)].rearrange("p (m t) -> p m t", m=WT) for q in range(2)]
        e_bwd = [e_all[:, q, WT * (CHUNK + 1):].rearrange("p (m t) -> p m t", m=WT) for q in range(2)]
        shifted = [ll[:, 0:3, :].rearrange("p m t -> p (m t)")[:, q * 532:q * 532 + T + 1] for q in range(2)]
        delta = [kk[:, q, :] for q in range(2)]

        def par(l, col, p0=0, p1=P):
            return prm[p0:p1, l * N_PAR + col:l * N_PAR + col + 1]

        ident = cst[:, IDENT:IDENT + P]
        ones = cst[:, ONES:ONES + P]
        headsum = cst[:, HEADSUM:HEADSUM + P]
        ident4 = spread(ident, WT)

        def pair(b):
            return ps[:, b:b + 2, 0:HT]

        def halves(ap):
            return ap.rearrange("p (a t) -> p a t", a=2)

        raw_loaded = [sem("raw_loaded0"), sem("raw_loaded1")]
        small_loaded = sem("small_loaded")
        cst_loaded = sem("cst_loaded")
        h_loaded = [sem(f"h_loaded{m}") for m in range(DT)]
        lora_loaded = sem("lora_loaded")
        gate_loaded = sem("gate_loaded")
        stored = sem("stored")
        hi_ready = sem("hi_ready")
        w_split = sem("w_split")
        unit_done = sem("unit_done")
        evacuated = sem("evacuated")
        gate_done = sem("gate_done")
        gs_ready = sem("gs_ready")
        sg_ready = sem("sg_ready")
        hid_ready = sem("hid_ready")
        hid_hi_ready = sem("hid_hi_ready")
        hid_lo_ready = sem("hid_lo_ready")
        sq_ready = sem("sq_ready")
        acc_added = sem("acc_added")
        stat_done = sem("stat_done")
        root_ready = sem("root_ready")
        rs_ready = sem("rs_ready")
        y_scaled = sem("y_scaled")
        y_scaled_dve = sem("y_scaled_dve")
        h_ready = sem("h_ready")
        x_hi_ready = sem("x_hi_ready")
        x_lo_ready = sem("x_lo_ready")
        delta_ready = sem("delta_ready")
        tiles_ready = sem("tiles_ready")
        dve_step = sem("dve_step")
        act_step = sem("act_step")
        fg_exp = sem("fg_exp")
        fg_abs = sem("fg_abs")
        c_ready = sem("c_ready")
        c_turned = sem("c_turned")
        c_tok_ready = sem("c_tok_ready")
        att_zero = sem("att_zero")
        q_ready = sem("q_ready")
        c_one_ready = sem("c_one_ready")
        c_spread = sem("c_spread")
        c_key_ready = sem("c_key_ready")
        v_turned = sem("v_turned")
        vz_ready = sem("vz_ready")
        scored = sem("scored")
        score_read = sem("score_read")
        max_ready = sem("max_ready")
        prob_ready = sem("prob_ready")
        diag_ready = sem("diag_ready")
        prob_turned = sem("prob_turned")
        prob_t_ready = sem("prob_t_ready")
        att_done = sem("att_done")
        att_read = sem("att_read")
        lora_in = sem("lora_in")
        ksq_ready = sem("ksq_ready")
        decay_done = sem("decay_done")
        iclr_done = sem("iclr_done")
        vres_done = sem("vres_done")
        knorm_done = sem("knorm_done")
        decay_sig = sem("decay_sig")
        iclr_sig = sem("iclr_sig")
        vres_sig = sem("vres_sig")
        kmax_ready = sem("kmax_ready")
        kln_ready = sem("kln_ready")
        kinv_ready = sem("kinv_ready")
        v_step = sem("v_step")
        rk_ready = sem("rk_ready")
        bonus_done = sem("bonus_done")
        bonus_ready = sem("bonus_ready")
        bd_zero = sem("bd_zero")
        e_ready = sem("e_ready")
        ar_built = sem("ar_built")
        bkv_built = sem("bkv_built")
        gram_done = sem("gram_done")
        gram_ready = sem("gram_ready")
        turned = sem("turned")
        tok_ready = sem("tok_ready")
        off_ready = sem("off_ready")
        z0_done = sem("z0_done")
        q_done = sem("q_done")
        qm_ready = sem("qm_ready")
        zd_done = sem("zd_done")
        yd_done = sem("yd_done")
        z_ready = sem("z_ready")
        y_ready = sem("y_ready")
        r_done = sem("r_done")
        rb_ready = sem("rb_ready")
        sa_done = sem("sa_done")
        sa_ready = sem("sa_ready")
        o_done = sem("o_done")
        o_read = sem("o_read")
        hd_done = sem("hd_done")
        state_ready = sem("state_ready")
        fsq_ready = sem("fsq_ready")
        fsum_done = sem("fsum_done")
        fln_ready = sem("fln_ready")
        frs_ready = sem("frs_ready")
        oln_ready = sem("oln_ready")
        ors_ready = sem("ors_ready")
        f_ready = sem("f_ready")
        mean_done = sem("mean_done")
        oc_ready = sem("oc_ready")
        osq_ready = sem("osq_ready")
        var_done = sem("var_done")
        g_done = sem("g_done")
        g_kept = sem("g_kept")
        o_built = sem("o_built")
        o_ready = sem("o_ready")
        v_copied = sem("v_copied")
        v_mixed = sem("v_mixed")
        v_built = sem("v_built")
        masked = sem("masked")
        inv_ready = sem("inv_ready")
        eps_set = sem("eps_set")
        h_added = sem("h_added")

        def unit_base(l, phase):
            return l * LAYER_UNITS + {"a": 0, "proj": FFN_UNITS, "wo": FFN_UNITS + PROJ_UNITS,
                                      "b": FFN_UNITS + PROJ_UNITS + WO_UNITS}[phase]

        def slot(base, k):
            return (base + k) % 2

        def units(eng, n, body, first=0):
            turns = max(n - 3, 0) // 2
            body(first, 0)
            body(first + 1, 0)
            if turns:
                with eng.Fori(0, turns) as i:
                    body(first + 2, i)
                    body(first + 3, i)
            for k in range(2 + 2 * turns, n):
                body(first + k, 0)

        def so_far(l, c, less):
            full, last = LEVEL_COUNT[CHUNK] - less, LEVEL_COUNT[LAST] - less
            return c * full + l * ((N_CHUNK - 1) * full + last)

        def pair_loop(eng, body):
            with eng.Fori(0, WT - 1) as i:
                body(i, False)
            body(WT - 1, True)

        PIECES = (2, 1, 1, 1, 1, 1, 1, 1, 1, 1, 1, 1, 1, 2, 2)

        def pieces(second, place):
            start = second * sum(PIECES) + sum(PIECES[:place])
            return range(start, min(start + PIECES[place], 5 + 6 * NQ))

        def step_piece(n):
            return divmod(n - 5, 3)

        def wait(eng, semaphore, value):
            if not isinstance(value, int) or value > 0:
                eng.wait_ge(semaphore, value)

        def norm_bank(l, n):
            if n % 2 == 0:
                return 4 * (1 - unit_base(l, ("a", "proj", "b")[n // 2]) % 2) + 2
            end = (unit_base(l, "a") + FFN_UNITS, unit_base(l, "wo") + WO_UNITS, unit_base(l, "b") + FFN_UNITS)[n // 2]
            return 4 * (end % 2)

        def post_count(l, n):
            return DT * (3 * l + {0: 0, 1: 1, 3: 2}[n])

        block = ctx.enter_context(nc.Block())

        @block.sync
        def _(sp):
            def load(source, cols, base, k, i=0):
                u = i * 2 + k
                wait(sp, w_split, u + (base - 1))
                sp.dma_start(raw[:, slot(base, k), 0:cols], source(u)).then_inc(raw_loaded[slot(base, k)], 16)

            def ffn(l, which, f):
                for fh in range(2):
                    base = unit_base(l, which) + fh * (FH + DT)
                    units(sp, FH, lambda k, i: load(lambda u: ffn_in[f, u + fh * FH], UNIT, base, k, i))
                    units(sp, DT, lambda k, i: load(lambda u: ffn_out[f, fh, u], OUT_UNIT, base + FH, k, i))

            sp.dma_start(prm[:, :], params).then_inc(small_loaded, 16)
            for l in range(DEPTH):
                ffn(l, "a", 2 * l)
                units(sp, PROJ_UNITS, lambda k, i: load(lambda u: proj[l, u], UNIT, unit_base(l, "proj"), k, i))
                sp.wait_ge(evacuated, unit_base(l, "wo"))
                sp.dma_start(lora_w, lora[l, :, 0:3 * WIDTH]).then_inc(lora_loaded, 16)
                sp.wait_ge(att_read, WT * NQ * (l + 1))
                sp.dma_start(gate_w, lora[l, :, 3 * WIDTH:5 * WIDTH]).then_inc(gate_loaded, 16)
                units(sp, WO_UNITS, lambda k, i: load(lambda u: w_out[l, u], UNIT, unit_base(l, "wo"), k, i))
                ffn(l, "b", 2 * l + 1)
            for m in range(DT):
                sp.wait_ge(h_ready, DT * (3 * DEPTH - 1) + m + 1)
                sp.dma_start(out[:, m, :], h[:, m, N_META:T]).then_inc(stored, 16)
            sp.wait_ge(stored, 16 * DT)

        @block.tensor
        def _(pe):
            def product(out_ap, w, x, first=True, last=True):
                return pe.matmul(out_ap, w, x, start=first, stop=last)

            def gemm(q, n_m, n_k, xh, xl, before=None):
                for m in range(n_m):
                    for k in range(n_k):
                        if before is not None and m == 0:
                            before(k)
                        cols = slice((m * n_k + k) * P, (m * n_k + k + 1) * P)
                        for n, (w, x) in enumerate(((w_hi, xh), (w_hi, xl), (w_lo, xh))):
                            for half in range(2):
                                ins = product(ps[:, 4 * q + 2 * m + half, 0:HT], w[:, q, cols],
                                              x[:, k, half * HT:(half + 1) * HT],
                                              k == 0 and n == 0, k == n_k - 1 and n == 2)
                    yield ins

            def first_gemm(q, xh, xl, hi_ready_for, lo_ready_for, order=tuple(range(DT))):
                def two(m, k, w, x, start, stop):
                    cols = slice((m * DT + k) * P, (m * DT + k + 1) * P)
                    for half in range(2):
                        ins = product(ps[:, 4 * q + 2 * m + half, 0:HT], w[:, q, cols], x[:, k, half * HT:(half + 1) * HT], start, stop)
                    return ins
                for k in order:
                    hi_ready_for(k)
                    for m in range(2):
                        two(m, k, w_hi, xh, k == order[0], False)
                        two(m, k, w_lo, xh, False, False)
                for m in range(2):
                    for k in order:
                        if m == 0:
                            lo_ready_for(k)
                        ins = two(m, k, w_hi, xl, False, k == order[-1])
                    yield ins

            def start_unit(u, base):
                pe.wait_ge(w_split, u + (base + 1))
                wait(pe, evacuated, u + (base - 1))

            def both(bank, w, x, first=True, last=True):
                for half in range(2):
                    ins = product(ps[:, bank + half, 0:HT], w, x[:, half * HT:(half + 1) * HT], first, last)
                return ins

            def statistics(l, n, units_before):
                s = 6 * l + n
                if s == 0:
                    pe.wait_ge(cst_loaded, 16)
                wait(pe, evacuated, units_before)
                pe.wait_ge(acc_added, (DT - 2) * (s + 1))
                both(norm_bank(l, n), ones, acc, True, False)
                pe.wait_ge(sq_ready, DT * (s + 1))
                both(norm_bank(l, n), ones, sqb[:, (DT - 1) % 2, :], False, True).then_inc(stat_done, 1)

            def operand(g):
                return lambda k: pe.wait_ge(x_hi_ready, DT * g + k + 1), lambda k: pe.wait_ge(x_lo_ready, DT * g + k + 1)

            def ffn(l, which, f, g, n):
                for fh in range(2):
                    base = unit_base(l, which) + fh * (FH + DT)

                    def unit_in(k, i):
                        u = i * 2 + k
                        start_unit(u, base)
                        if fh == 0 and k == 0:
                            products = first_gemm(slot(base, k), x_hi, x_lo, *operand(g))
                        else:
                            products = gemm(slot(base, k), 2, DT, x_hi, x_lo)
                        if fh == 0 and k == 1:
                            statistics(l, n, base)
                        next(products).then_inc(gate_done, 1)
                        if fh == 0 and k == 1:
                            pe.wait_ge(root_ready, 6 * l + n + 1)
                        next(products).then_inc(unit_done, 1)

                    def unit_out(k, i):
                        start_unit(i * 2 + k, base + FH)
                        before = (lambda kt: pe.wait_ge(hid_lo_ready, FH * (2 * f + fh) + kt + 1)) if k == 0 else None
                        next(gemm(slot(base + FH, k), 1, FH, hid_hi, hid_lo, before)).then_inc(unit_done, 1)

                    units(pe, FH, unit_in)
                    units(pe, DT, unit_out)
                statistics(l, n + 1, unit_base(l, which) + FFN_UNITS - 1)
                pe.wait_ge(root_ready, 6 * l + n + 2)

            def projection(l):
                base = unit_base(l, "proj")

                def unit(k, i):
                    start_unit(i * 2 + k, base)
                    if k == 0:
                        products = first_gemm(slot(base, k), x_hi, x_lo, *operand(4 * l + 1))
                    else:
                        products = gemm(slot(base, k), 1 if k == PROJ_UNITS - 1 else 2, DT, x_hi, x_lo)
                    if k == 1:
                        statistics(l, 2, base)
                    for m, ins in enumerate(products):
                        if k == 1 and m == 0:
                            pe.wait_ge(root_ready, 6 * l + 3)
                    ins.then_inc(unit_done, 1)
                units(pe, PROJ_UNITS, unit)

            def forget_gates(l):
                if l:
                    pe.wait_ge(vres_sig, WT * l)
                pe.wait_ge(c_ready, l + 1)
                for j in range(NQ):
                    n = QT[j + 1] - QT[j]
                    ins = pe.transpose(ps[0:n, 4 + j // 4, (j % 4) * P:(j % 4 + 1) * P], c_all[:, QT[j]:QT[j + 1]], ident)
                ins.then_inc(c_turned, 1)
                pe.wait_ge(c_tok_ready, l + 1)

            def attend(l, pr, n_piece):
                pairs = pr + l * WT
                step = pairs * (2 * NQ)

                def scores(s):
                    j, a = divmod(s, 2)
                    nk = QT[j + 1]
                    wide = nk > 512
                    if s < 2:
                        pe.wait_ge(q_ready, pairs * 2 + (a + 1))
                        pe.wait_ge(c_key_ready, pairs * 2 + 2)
                    else:
                        pe.wait_ge(score_read, step + (s if wide else s - 1))
                    for half, (c0, c1) in enumerate([(0, HT), (HT, T)] if wide else [(0, nk)]):
                        ins = product(ps[0:nk - QT[j], 4 + (half if wide else a), 0:c1 - c0], qz[:, a, QT[j]:nk],
                                      tiles[:, bass.ds((pr + KF) * T + c0, c1 - c0)])
                    ins.then_inc(scored, 1)

                def turn(s):
                    j, a = divmod(s, 2)
                    n = QT[j + 1] - QT[j]
                    pe.wait_ge(diag_ready, step + (s + 1))
                    if s == 0:
                        pe.wait_ge(vz_ready, pairs + 1)
                    else:
                        pe.wait_ge(prob_t_ready, step + s)
                    for i in range(j + 1):
                        ni = QT[i + 1] - QT[i]
                        ins = product(ps[0:ni, 6, i * n:(i + 1) * n], prob[0:n, a, QT[i]:QT[i + 1]], diag[0:n, a, 0:n])
                    ins.then_inc(prob_turned, 1)

                def values(s):
                    j, a = divmod(s, 2)
                    n = QT[j + 1] - QT[j]
                    pe.wait_ge(prob_t_ready, step + (s + 1))
                    if a == 0 and j:
                        pe.wait_ge(att_read, pairs * NQ + j)
                    for i in range(j + 1):
                        ni = QT[i + 1] - QT[i]
                        ins = product(ps[:, 7, 0:n], vz[0:ni, a, i, :], prob_t[0:ni, a, i, 0:n],
                                      a == 0 and i == 0, a == 1 and i == j)
                    if a == 1:
                        ins.then_inc(att_done, 1)

                if n_piece in (1, 3):
                    a = n_piece // 2
                    pe.wait_ge(c_one_ready, pairs * 2 + (a + 1))
                    if a:
                        pe.wait_ge(c_key_ready, pairs * 2 + 1)
                    both(4, ones, c_one[:, a, :]).then_inc(c_spread, 1)
                elif n_piece == 2:
                    pe.wait_ge(v_copied, pairs + 1)
                    for j in range(NQ):
                        n = QT[j + 1] - QT[j]
                        ins = pe.transpose(ps[0:n, 6 + j // 4, (j % 4) * P:(j % 4 + 1) * P], v_pair[:, QT[j]:QT[j + 1]], ident)
                    ins.then_inc(v_turned, 1)
                elif n_piece == 4:
                    scores(0)
                elif n_piece > 4:
                    s, kind = step_piece(n_piece)
                    if kind == 0 and s + 1 < 2 * NQ:
                        scores(s + 1)
                    elif kind == 1:
                        turn(s)
                    elif kind == 2:
                        values(s)

            def low_rank(l):
                pe.wait_ge(evacuated, unit_base(l, "wo"))
                pe.wait_ge(lora_loaded, 16 * (l + 1))
                pe.wait_ge(lora_in, 3 * (l + 1))
                for m in range(WT):
                    n = WT * l + m
                    todo = [(WA, decay_done, decay_sig, n), (WA, iclr_done, iclr_sig, n), (MISC, vres_done, vres_sig, n - WT)]
                    for i, (src, done, read, count) in enumerate(todo[:3 if l else 2]):
                        if m:
                            pe.wait_ge(read, count)
                        both(2 * i, lora_w[:, i * WIDTH + m * P:i * WIDTH + (m + 1) * P], tile(src)).then_inc(done, 1)
                    pe.wait_ge(ksq_ready, n + 1)
                    if m:
                        pe.wait_ge(kmax_ready, n)
                    both(6, headsum, k_square[m % 2]).then_inc(knorm_done, 1)
                pe.wait_ge(decay_sig, WT * (l + 1))
                pe.wait_ge(iclr_sig, WT * (l + 1))
                pe.wait_ge(kmax_ready, WT * (l + 1))
                for m in range(WT):
                    if m == WT - 1:
                        forget_gates(l)
                    pe.wait_ge(rk_ready, WT * l + m + 1)
                    both(BONUS_BANKS[m], headsum, bonus[:, m, :]).then_inc(bonus_done, 1)

            def tail(l, place):
                def fox_sum(m):
                    pe.wait_ge(fsq_ready, WT * l + m + 1)
                    if m >= 2:
                        pe.wait_ge(fln_ready, WT * l + m - 1)
                    both(4 + 2 * (m % 2), headsum, ll[:, m, :]).then_inc(fsum_done, 1)

                def gate(m):
                    if m >= 2:
                        pe.wait_ge(g_kept, WT * l + m - 1)
                    else:
                        pe.wait_ge(fln_ready, WT * l + m + 3)
                    b = 4 + 2 * (m % 2)
                    both(b, gate_w[:, m * P:(m + 1) * P], tile(GD), True, False)
                    both(b, gate_w[:, WIDTH + m * P:WIDTH + (m + 1) * P], tile(MISC), False, True).then_inc(g_done, 1)

                if place == 1:
                    fox_sum(0)
                    fox_sum(1)
                elif place in (2, 3):
                    fox_sum(place)
                elif place in (4, 5, 6, 7):
                    if place == 4:
                        pe.wait_ge(gate_loaded, 16 * (l + 1))
                    gate(place - 4)

            def chunks(l):
                pe.wait_ge(bonus_ready, WT * (l + 1))
                pe.wait_ge(kmax_ready, WT * (l + 1))
                if l:
                    pe.wait_ge(vres_sig, WT * l)
                pe.wait_ge(bd_zero, 2 * (l + 1))

                def chunk(c, b, n, beside, follows, settles):
                    cc, w, levels = c + l * N_CHUNK, 2 * n, LEVEL_COUNT[n]
                    masked_before, solved_before = so_far(l, c, 0), so_far(l, c, 1)
                    pe.wait_ge(ar_built, cc + 1)
                    pe.wait_ge(bkv_built, cc * 4 + 4)
                    pe.wait_ge(v_built, cc + 1)
                    for pr in range(WT):
                        if pr >= 2:
                            pe.wait_ge(gram_ready, cc * WT + (pr - 1))
                        for i in range(2):
                            ins = product(ps[0:w, pr % 2, i * P:i * P + w], bkv[:, b, pr, i * P:i * P + w], ar[:, b, pr, 0:w])
                        ins.then_inc(gram_done, 1)
                        if pr >= 2:
                            pe.wait_ge(tok_ready, cc * WT + (pr - 1))
                        elif follows:
                            pe.wait_ge(*((o_read, cc) if pr == 0 else (state_ready, c + l * (N_CHUNK - 1))))
                        for i in range(3):
                            ins = pe.transpose(ps[0:w, 2 + pr % 2, i * P:(i + 1) * P], bkv[:, b, pr, i * P:i * P + w], ident)
                        ins.then_inc(turned, 1)
                    beside(0)
                    pe.wait_ge(gram_ready, cc * WT + WT)
                    pe.wait_ge(off_ready, masked_before + 1)
                    for pr in range(WT):
                        ins = pe.transpose(ps[0:w, 0, pr * P:pr * P + w], uo[0:w, pr, 0:w], ident[0:w, 0:w])
                    ins.then_inc(z0_done, 1)
                    beside(1)
                    pe.wait_ge(tok_ready, cc * WT + WT)
                    for v in range(1, levels):
                        pe.wait_ge(off_ready, masked_before + (v + 1))
                        pe.wait_ge(z_ready, solved_before + v)
                        for pr in range(WT):
                            ins = product(ps[0:w, 1, pr * P:pr * P + w], uo[0:w, pr, 0:w], zm[0:w, pr, 0:w])
                        ins.then_inc(q_done, 1)
                        beside(2 * v)
                        pe.wait_ge(qm_ready, solved_before + v)
                        pe.wait_ge(y_ready, masked_before + v)
                        if v < levels - 1:
                            for pr in range(WT):
                                ins = product(ps[0:w, 2, pr * P:pr * P + w], ym[0:w, pr, 0:w], qm[0:w, pr, 0:w])
                            ins.then_inc(zd_done, 1)
                        for pr in range(WT):
                            ins = product(ps[0:w, 3, pr * P:pr * P + w], qm[0:w, pr, 0:w], ym[0:w, pr, 0:w])
                        ins.then_inc(yd_done, 1)
                        beside(2 * v + 1)
                    for pr in range(WT):
                        product(ps[0:w, 0, pr * P:(pr + 1) * P], gm[0:w, pr, P:P + w], tok[0:w, pr, 256:384], True, False)
                        ins = product(ps[0:w, 0, pr * P:(pr + 1) * P], a_blocks[:, b, pr, 0:w], hs[:, pr, :], False, True)
                    ins.then_inc(r_done, 1)
                    beside(12)
                    pe.wait_ge(rb_ready, cc + 1)
                    pe.wait_ge(y_ready, masked_before + levels)
                    for pr in range(WT):
                        ins = product(ps[0:w, 1, pr * P:(pr + 1) * P], ym[0:w, pr, 0:w], rb[0:w, pr, :])
                    ins.then_inc(sa_done, 1)
                    beside(13)
                    pe.wait_ge(sa_ready, cc + 1)
                    for pr in range(WT):
                        o = ps[:, 2, pr * P:pr * P + n]
                        product(o, sa[0:w, pr, :], gm[0:w, pr, 2 * P:2 * P + n], True, False)
                        product(o, tok[0:w, pr, 256:384], gm[0:w, pr, 2 * P + HEAD:2 * P + HEAD + n], False, False)
                        ins = product(o, hs[:, pr, :], ar[:, b, pr, n:w], False, True)
                    ins.then_inc(o_done, 1)
                    if n == CHUNK:
                        for pr in range(WT):
                            d = ps[:, 3, pr * P:(pr + 1) * P]
                            product(d, tok[:, pr, 0:128], sa[:, pr, :], True, False)
                            ins = product(d, tok[:, pr, 128:256], tok[:, pr, 256:384], False, True)
                        ins.then_inc(hd_done, 1)
                    beside(14)
                    if settles and n == CHUNK:
                        pe.wait_ge(state_ready, c + (l * (N_CHUNK - 1) + 1))
                    if settles:
                        pe.wait_ge(o_read, cc + 1)

                def pair_of_chunks(pr, last):
                    for second in range(2):
                        chunk(pr * 2 + second, second, CHUNK, lambda place: [attend(l, pr, n) for n in pieces(second, place)],
                              second == 1, second == 1)
                    pe.wait_ge(score_read, (pr + l * WT) * (2 * NQ) + 2 * NQ)
                    pe.wait_ge(att_read, (pr + l * WT) * NQ + NQ)

                pair_loop(pe, pair_of_chunks)
                chunk(N_CHUNK - 1, 0, LAST, lambda place: tail(l, place), False, True)

            def head_outputs(l):
                pe.wait_ge(o_read, N_CHUNK * (l + 1))
                pe.wait_ge(y_ready, so_far(l + 1, 0, 0))
                pe.wait_ge(g_kept, WT * (l + 1))
                for m in range(WT):
                    both(2 * m, headsum, tile(R + m)).then_inc(mean_done, 1)
                for m in range(WT):
                    pe.wait_ge(osq_ready, WT * l + m + 1)
                    pe.wait_ge(oc_ready, WT * l + m + 1)
                    both(2 * m, headsum, aa[:, m, :]).then_inc(var_done, 1)

            def mixer_out(l):
                base = unit_base(l, "wo")
                order = [(m + WT) % DT for m in range(DT)]

                def unit(k, i):
                    start_unit(i * 2 + k, base)
                    if k == 0:
                        pe.wait_ge(oln_ready, WT * (l + 1))
                        count = {kt: DT * (4 * l + 2) + n + 1 for n, kt in enumerate(order)}
                        products = first_gemm(slot(base, k), x_hi, x_lo, lambda kt: pe.wait_ge(x_hi_ready, count[kt]),
                                              lambda kt: pe.wait_ge(x_lo_ready, count[kt]), order)
                    else:
                        products = gemm(slot(base, k), 2, DT, x_hi, x_lo)
                    for ins in products:
                        pass
                    ins.then_inc(unit_done, 1)
                units(pe, WO_UNITS, unit)
                statistics(l, 3, base + WO_UNITS - 1)
                pe.wait_ge(root_ready, 6 * l + 4)

            for l in range(DEPTH):
                ffn(l, "a", 2 * l, 4 * l, 0)
                projection(l)
                low_rank(l)
                chunks(l)
                head_outputs(l)
                mixer_out(l)
                ffn(l, "b", 2 * l + 1, 4 * l + 3, 4)

        @block.scalar
        def _(act):
            eps_pre, eps_half, eps_lnx, one = (eps[:, n:n + 1] for n in range(4))

            def copy(dst, src):
                return act.activation(dst, src, ACT.Copy)

            def split_hi(cols, base, k, i=0):
                u = i * 2 + k
                act.wait_ge(raw_loaded[slot(base, k)], i * 16 + 16 * ((base + k) // 2 + 1))
                wait(act, unit_done, u + (base - 1))
                copy(w_hi[:, slot(base, k), 0:cols], raw[:, slot(base, k), 0:cols]).then_inc(hi_ready, 1)

            def square(s, k, i, ap):
                if k == 0:
                    wait(act, stat_done, s)
                    act.activation(acc[:, :], ap, ACT.Square).then_inc(sq_ready, 1)
                else:
                    wait(act, acc_added, i * 2 + ((DT - 2) * s + max(k - 2, 0)))
                    act.activation(sqb[:, k % 2, :], ap, ACT.Square).then_inc(sq_ready, 1)

            def load_ln(n):
                act.activation(warm[:, n:n + 1], one, ACT.Ln)

            def inverse_root(l, n, scale, bias):
                count = 6 * l + n + 1
                act.wait_ge(stat_done, count)
                act.activation(halves(root[:, :]), pair(norm_bank(l, n)), ACT.Ln, bias=bias, scale=scale).then_inc(root_ready, 1)
                act.wait_ge(root_ready, count)
                act.activation((rs_pre, rs_post)[n % 2][:, :], root[:, :], ACT.Exp, scale=-0.5).then_inc(rs_ready, 1)

            def prepare(l, g, n, units_before):
                wait(act, unit_done, units_before)
                for m in range(DT):
                    if post_count(l, g):
                        act.wait_ge(h_ready, post_count(l, g) - DT + m + 1)
                    else:
                        act.wait_ge(h_loaded[m], 16)
                    act.activation(x_hi[:, m, :], h[:, m, :], ACT.Copy, scale=par(l, GAIN + n * DT + m)).then_inc(x_hi_ready, 1)
                    square(6 * l + n, m, 0, h[:, m, :])

            def ffn(l, which, f, n):
                for fh in range(2):
                    base = unit_base(l, which) + fh * (FH + DT)

                    def unit_in(k, i):
                        u, q = i * 2 + k, slot(base, k)
                        if k == FH - 1:
                            split_hi(OUT_UNIT, base, FH)
                        elif not (fh == 0 and k == 0):
                            split_hi(UNIT, base, k + 1, i)
                        if fh == 0 and k == 0:
                            inverse_root(l, n, 1.0 / D_MODEL, eps_pre)
                        act.wait_ge(gs_ready, u + (FH * (2 * f + fh) + 1))
                        act.activation(sg[:, q, :], gs[:, q, :], ACT.Silu).then_inc(sg_ready, 1)
                        act.wait_ge(hid_ready, u + (FH * (2 * f + fh) + 1))
                        copy(hid_hi[:, u, :], hid[:, q, :]).then_inc(hid_hi_ready, 1)

                    def unit_out(k, i):
                        u = i * 2 + k
                        if k < DT - 1:
                            split_hi(OUT_UNIT, base + FH, k + 1, i)
                        elif not (l == DEPTH - 1 and which == "b" and fh == 1):
                            split_hi(UNIT, base, FH + DT)
                        if fh == 1:
                            act.wait_ge(evacuated, u + (base + FH + 1))
                            square(6 * l + n + 1, k, i, y_ffn[:, u, :])

                    units(act, FH, unit_in)
                    if fh == 1:
                        load_ln(3 * l + n // 2)
                    units(act, DT, unit_out)
                if not (l == DEPTH - 1 and which == "b"):
                    split_hi(UNIT, base + FH + DT, 1)
                inverse_root(l, n + 1, 4.0 / D_MODEL, eps_half)

            def projection(l):
                base = unit_base(l, "proj")

                def unit(k, i):
                    if 0 < k < PROJ_UNITS - 1:
                        split_hi(UNIT // 2 if k == PROJ_UNITS - 2 else UNIT, base, k + 1, i)
                    if k == 0:
                        inverse_root(l, 2, 1.0 / D_MODEL, eps_pre)
                units(act, PROJ_UNITS, unit)

            def attend(l, pr, n_piece):
                pairs = pr + l * WT
                step = pairs * (2 * NQ)

                def exponent(s):
                    j, a = divmod(s, 2)
                    n = QT[j + 1] - QT[j]
                    act.wait_ge(max_ready, step + (s + 1))
                    if s >= 2:
                        act.wait_ge(prob_turned, step + (s - 1))
                    act.activation(prob[0:n, a, 0:QT[j + 1]], score[0:n, a, 0:QT[j + 1]], ACT.Exp,
                                   bias=neg_max[0:n, a:a + 1], accum_out=row_sum[0:n, a:a + 1]).then_inc(prob_ready, 1)

                def by_key(s):
                    j, a = divmod(s, 2)
                    n = QT[j + 1] - QT[j]
                    act.wait_ge(prob_turned, step + (s + 1))
                    if j:
                        act.wait_ge(att_done, pairs * NQ + j)
                    m = min(j + 1, 4)
                    ins = copy(prob_t[0:QT[1], a, 0:m, 0:n], ps[0:QT[1], 6, 0:m * n].rearrange("p (i c) -> p i c", i=m))
                    if j == 4:
                        ins = copy(prob_t[0:n, a, 4, 0:n], ps[0:n, 6, 4 * n:5 * n])
                    ins.then_inc(prob_t_ready, 1)

                if n_piece == 0:
                    for a in range(2):
                        rows = slice(a * HEAD, (a + 1) * HEAD)
                        act.activation(qz[rows, a, :], tiles[rows, bass.ds((pr + QF) * T, T)], ACT.Copy, scale=HEAD ** -0.5).then_inc(q_ready, 1)
                    copy(v_pair[:, :], tiles[:, bass.ds((pr + VF) * T, T)]).then_inc(v_copied, 1)
                elif n_piece in (1, 3):
                    act.wait_ge(c_spread, pairs * 2 + (n_piece // 2 + 1))
                    copy(halves(c_key[:, n_piece // 2, :]), pair(4)).then_inc(c_key_ready, 1)
                elif n_piece == 2:
                    act.wait_ge(v_turned, pairs + 1)
                    for a in range(2):
                        cols = slice(a * HEAD, (a + 1) * HEAD)
                        copy(vz[0:QT[1], a, 0:4, cols], ps[0:QT[1], 6, :].rearrange("p (j c) -> p j c", j=4)[:, :, cols])
                        ins = copy(vz[0:T - QT[4], a, 4, cols], ps[0:T - QT[4], 7, cols])
                    ins.then_inc(vz_ready, 1)
                elif n_piece == 4:
                    exponent(0)
                else:
                    s, kind = step_piece(n_piece)
                    if kind == 1:
                        by_key(s)
                    elif kind == 2 and s + 1 < 2 * NQ:
                        exponent(s + 1)

            def low_rank(l):
                act.wait_ge(evacuated, unit_base(l, "wo"))
                act.wait_ge(w_split, unit_base(l, "wo"))
                act.wait_ge(tiles_ready, 15 * (l + 1))

                def square_k(m):
                    if m >= 2:
                        act.wait_ge(knorm_done, WT * l + m - 1)
                    act.activation(k_square[m % 2], tile(K + m), ACT.Square, scale=par(l, KKG + m)).then_inc(ksq_ready, 1)

                act.activation(tile(GD), tile(GD), ACT.Sigmoid).then_inc(lora_in, 1)
                act.activation(tile(WA)[0:64, :], tile(WA)[0:64, :], ACT.Tanh).then_inc(lora_in, 1)
                act.activation(tile(MISC)[0:32, :], tile(MISC)[0:32, :], ACT.Sigmoid).then_inc(lora_in, 1)
                square_k(0)
                square_k(1)
                for m in range(WT):
                    n = WT * l + m
                    act.wait_ge(decay_done, n + 1)
                    act.activation(halves(ll[:, m, :]), pair(0), ACT.Sigmoid, bias=par(l, DBIAS + m)).then_inc(decay_sig, 1)
                    act.wait_ge(iclr_done, n + 1)
                    act.activation(halves(aa[:, m, :]), pair(2), ACT.Sigmoid, bias=par(l, IBIAS + m)).then_inc(iclr_sig, 1)
                    if l:
                        act.wait_ge(vres_done, n - WT + 1)
                        act.activation(halves(v_weight[m]), pair(4), ACT.Sigmoid, bias=par(l, VBIAS + m)).then_inc(vres_sig, 1)
                    else:
                        act.activation(v_first[:, m, :], tile(V + m), ACT.Copy)
                    if m < 2:
                        square_k(m + 2)

                row = slice(FORGET_ROW, FORGET_ROW + HEADS)
                act.wait_ge(fg_abs, l + 1)
                act.activation(fg[row, 1, :], fg[row, 1, :], ACT.Exp).then_inc(act_step, 1)
                act.wait_ge(act_step, l + 1)
                act.activation(fg[row, 1, :], fg[row, 1, :], ACT.Ln, bias=one[row, :]).then_inc(fg_exp, 1)
                for m in range(WT):
                    act.wait_ge(kmax_ready, WT * l + m + 1)
                    act.activation(k_inverse[m], k_inverse[m], ACT.Ln).then_inc(kln_ready, 1)
                for m in range(WT):
                    act.wait_ge(kln_ready, WT * l + m + 1)
                    act.activation(k_inverse[m], k_inverse[m], ACT.Exp, scale=-0.5).then_inc(kinv_ready, 1)
                act.wait_ge(c_turned, l + 1)
                for j in range(NQ):
                    n = QT[j + 1] - QT[j]
                    c0 = (j % 4) * P + FORGET_ROW
                    ins = copy(c_tok[0:n, j, :], ps[0:n, 4 + j // 4, c0:c0 + HEADS])
                ins.then_inc(c_tok_ready, 1)

            def tail(l, place):
                n = WT * l
                if place in (0, 1):
                    act.wait_ge(e_ready, N_CHUNK * (l + 1))
                    for m in (2 * place, 2 * place + 1):
                        act.activation(ll[:, m, :], tile(QF + m), ACT.Square).then_inc(fsq_ready, 1)
                elif place in (2, 3, 4):
                    for m in {2: (0, 1), 3: (2,), 4: (3,)}[place]:
                        act.wait_ge(fsum_done, n + m + 1)
                        act.activation(halves(ll[:, m, :]), pair(4 + 2 * (m % 2)), ACT.Ln, bias=eps_pre, scale=1.0 / HEAD).then_inc(fln_ready, 1)
                elif place in (5, 6):
                    for m in {5: (0, 1), 6: (2, 3)}[place]:
                        act.wait_ge(fln_ready, n + m + 1)
                        act.activation(ll[:, m, :], ll[:, m, :], ACT.Exp, scale=-0.5).then_inc(frs_ready, 1)

            def chunks(l):
                act.wait_ge(bonus_ready, WT * (l + 1))
                act.wait_ge(bd_zero, 2 * (l + 1))
                act.wait_ge(att_zero, l + 1)

                def prepare_chunk(c, b, n):
                    tokens = bass.ds(c * CHUNK, n)
                    act.activation(e_fwd[b][:, :, 1:n + 1], ll[:, :, tokens], ACT.Exp, scale=-DECAY)
                    act.activation(e_bwd[b][:, :, 0:n], ll[:, :, tokens], ACT.Exp, scale=DECAY).then_inc(e_ready, 1)
                    for a in range(2):
                        ins = copy(bkv[a * HEAD:(a + 1) * HEAD, b, :, 2 * P + a * n:2 * P + (a + 1) * n],
                                   group(V, p0=a * HEAD, p1=(a + 1) * HEAD)[:, :, tokens])
                    ins.then_inc(v_built, 1)

                def copy4(dst, bank, rows, cols=P):
                    return copy(dst[0:rows, :, 0:cols], ps[0:rows, bank, :].rearrange("p (m c) -> p m c", m=WT)[:, :, 0:cols])

                def chunk(c, b, n, following, beside):
                    cc, w = c + l * N_CHUNK, 2 * n
                    solved_before = so_far(l, c, 1)
                    for pr in range(WT):
                        act.wait_ge(turned, cc * WT + (pr + 1))
                        copy(tok[0:w, pr, :], ps[0:w, 2 + pr % 2, 0:3 * P]).then_inc(tok_ready, 1)
                    beside(0)
                    if following:
                        prepare_chunk(c + 1, 1 - b, following)
                    beside(1)
                    for v in range(1, LEVEL_COUNT[n]):
                        act.wait_ge(q_done, solved_before + v)
                        copy4(qm, 1, w, w).then_inc(qm_ready, 1)
                        beside(2 * v)
                        beside(2 * v + 1)
                    act.wait_ge(r_done, cc + 1)
                    copy4(rb, 0, w).then_inc(rb_ready, 1)
                    beside(12)
                    act.wait_ge(sa_done, cc + 1)
                    copy4(sa, 1, w).then_inc(sa_ready, 1)
                    beside(13)
                    act.wait_ge(o_done, cc + 1)
                    copy(group(R)[:, :, bass.ds(c * CHUNK, n)], ps[:, 2, :].rearrange("p (m c) -> p m c", m=WT)[:, :, 0:n]).then_inc(o_read, 1)
                    beside(14)

                def pair_of_chunks(pr, last):
                    for second in range(2):
                        chunk(pr * 2 + second, second, CHUNK, LAST if last and second else CHUNK,
                              lambda place: [attend(l, pr, n) for n in pieces(second, place)])
                    act.wait_ge(att_done, (pr + l * WT) * NQ + NQ)

                prepare_chunk(0, 0, CHUNK)
                pair_loop(act, pair_of_chunks)
                chunk(N_CHUNK - 1, 0, LAST, 0, lambda place: tail(l, place))

            def head_outputs(l):
                g, n = 4 * l + 2, WT * l

                def x_hi_of(m, src):
                    copy(x_hi[:, m, :], src).then_inc(x_hi_ready, 1)

                def x_hi_of_rwkv(m):
                    act.wait_ge(o_ready, n + m + 1)
                    x_hi_of(m, tile(R + m))

                act.wait_ge(f_ready, n + WT)
                for m in range(WT):
                    act.wait_ge(oc_ready, n + m + 1)
                    act.activation(aa[:, m, :], tile(R + m), ACT.Square).then_inc(osq_ready, 1)
                    x_hi_of(m + WT, tile(QF + m))
                for m in range(WT):
                    act.wait_ge(var_done, n + m + 1)
                    act.activation(halves(aa[:, m, :]), pair(2 * m), ACT.Ln, bias=eps_lnx, scale=1.0 / HEAD).then_inc(oln_ready, 1)
                for m in range(WT):
                    act.wait_ge(oln_ready, n + m + 1)
                    act.activation(aa[:, m, :], aa[:, m, :], ACT.Exp, scale=-0.5).then_inc(ors_ready, 1)
                for m in range(WT):
                    x_hi_of_rwkv(m)

            def mixer_out(l):
                base = unit_base(l, "wo")

                def unit(k, i):
                    if k < WO_UNITS - 1:
                        split_hi(UNIT, base, k + 1, i)
                    else:
                        split_hi(UNIT, base, WO_UNITS)
                    act.wait_ge(evacuated, i * 2 + (base + k + 1))
                    for j in range(2):
                        square(6 * l + 3, 2 * k + j, 0, y_mix[:, 2 * k + j, :])
                load_ln(3 * l + 1)
                for k in range(WO_UNITS):
                    unit(k, 0)
                split_hi(UNIT, base + WO_UNITS, 1)
                inverse_root(l, 3, 1.0 / D_MODEL, eps_pre)

            for m in range(DT):
                act.dma_start(h[:, m, :], h_in[:, m, :]).then_inc(h_loaded[m], 16)
            act.dma_start(cst[:, :], consts).then_inc(cst_loaded, 16)
            act.wait_ge(small_loaded, 16)
            act.wait_ge(eps_set, 4)
            split_hi(UNIT, 0, 0)
            split_hi(UNIT, 0, 1)
            for l in range(DEPTH):
                prepare(l, 0, 0, unit_base(l, "a"))
                ffn(l, "a", 2 * l, 0)
                prepare(l, 1, 2, unit_base(l, "proj"))
                projection(l)
                low_rank(l)
                chunks(l)
                act.wait_ge(mean_done, WT * l + 1)
                split_hi(UNIT, unit_base(l, "wo"), 0)
                head_outputs(l)
                mixer_out(l)
                prepare(l, 3, 4, unit_base(l, "b"))
                ffn(l, "b", 2 * l + 1, 4)

        @block.vector
        def _(dve):
            links = [0]

            def link(ins):
                links[0] += 1
                ins.then_inc(dve_step, 1)
                dve.wait_ge(dve_step, links[0])

            def step(ins):
                links[0] += 1
                ins.then_inc(dve_step, 1)
                return links[0]

            def split_lo(cols, base, k, i=0):
                q = slot(base, k)
                dve.wait_ge(hi_ready, i * 2 + (base + k + 1))
                dve.tensor_tensor(w_lo[:, q, 0:cols], raw[:, q, 0:cols], w_hi[:, q, 0:cols], ALU.subtract).then_inc(w_split, 1)

            def x_lo_of(l, g, n, m):
                dve.wait_ge(x_hi_ready, DT * (4 * l + g) + m + 1)
                dve.scalar_tensor_tensor(x_lo[:, m, :], h[:, m, :], par(l, GAIN + n * DT + m), x_hi[:, m, :],
                                         ALU.mult, ALU.subtract).then_inc(x_lo_ready, 1)

            def update(l, post, y, following):
                by_pool, own = len(POOL_TILES) * (3 * l + post), (DT - len(POOL_TILES)) * (3 * l + post)
                dve.wait_ge(rs_ready, 6 * l + 2 * post + 2)

                def scale(m):
                    dve.tensor_tensor(y[:, m, :], y[:, m, :], rs_post[:, :], ALU.mult).then_inc(y_scaled_dve, 1)

                todo = [m for m in range(DT) if m not in POOL_TILES]
                scale(todo[0])
                for m in range(DT):
                    if m + 1 < len(todo):
                        scale(todo[m + 1])
                    if m in POOL_TILES:
                        by_pool += 1
                        dve.wait_ge(y_scaled, by_pool)
                    else:
                        own += 1
                        dve.wait_ge(y_scaled_dve, own)
                    dve.scalar_tensor_tensor(h[:, m, :], y[:, m, :], par(l, GAIN + (2 * post + 1) * DT + m), h[:, m, :],
                                             ALU.mult, ALU.add).then_inc(h_ready, 1)
                if following:
                    for m in range(DT):
                        x_lo_of(*following, m)

            def ffn(l, which, f, n):
                for fh in range(2):
                    base = unit_base(l, which) + fh * (FH + DT)

                    def unit_in(k, i):
                        u, q = i * 2 + k, slot(base, k)
                        e = u + (FH * (2 * f + fh) + 1)
                        if k == FH - 1:
                            split_lo(OUT_UNIT, base, FH)
                        elif not (fh == 0 and k == 0):
                            split_lo(UNIT, base, k + 1, i)
                        dve.wait_ge(gate_done, e)
                        if fh == 0 and k == 0:
                            dve.wait_ge(rs_ready, 6 * l + n + 1)
                        dve.tensor_tensor(halves(gs[:, q, :]), pair(4 * q), halves(rs_pre[:, :]), ALU.mult).then_inc(gs_ready, 1)
                        dve.wait_ge(unit_done, u + (base + 1))
                        dve.tensor_tensor(halves(us[:, q, :]), pair(4 * q + 2), halves(rs_pre[:, :]), ALU.mult).then_inc(evacuated, 1)
                        dve.wait_ge(hid_hi_ready, e)
                        dve.tensor_tensor(hid_lo[:, u, :], hid[:, q, :], hid_hi[:, u, :], ALU.subtract).then_inc(hid_lo_ready, 1)

                    def unit_out(k, i):
                        u, q = i * 2 + k, slot(base + FH, k)
                        if k < DT - 1:
                            split_lo(OUT_UNIT, base + FH, k + 1, i)
                        elif not (l == DEPTH - 1 and which == "b" and fh == 1):
                            split_lo(UNIT, base, FH + DT)
                        dve.wait_ge(unit_done, u + (base + FH + 1))
                        if fh == 0:
                            dve.tensor_copy(halves(y_ffn[:, u, :]), pair(4 * q)).then_inc(evacuated, 1)
                        else:
                            dve.tensor_tensor(halves(y_ffn[:, u, :]), pair(4 * q), halves(y_ffn[:, u, :]), ALU.add).then_inc(evacuated, 1)

                    units(dve, FH, unit_in)
                    units(dve, DT, unit_out)
                if not (l == DEPTH - 1 and which == "b"):
                    split_lo(UNIT, base + FH + DT, 1)

            def projection(l):
                base = unit_base(l, "proj")

                def next_split(k, i):
                    if 0 < k < PROJ_UNITS - 1:
                        split_lo(UNIT // 2 if k == PROJ_UNITS - 2 else UNIT, base, k + 1, i)

                def heads_unit(k, i):
                    next_split(k, i)
                    dve.wait_ge(unit_done, i * 2 + (base + k + 1))
                    if k == 0:
                        dve.wait_ge(rs_ready, 6 * l + 3)
                    for j in range(2):
                        dst = tiles[:, bass.ds((i * 4 + (2 * k + j)) * T, T)] if not isinstance(i, int) else tile(2 * k + j)
                        ins = dve.tensor_tensor(halves(dst), pair(4 * slot(base, k) + 2 * j), halves(rs_pre[:, :]), ALU.mult)
                    ins.then_inc(evacuated, 1)

                def shifted_unit(k, i):
                    single = k == PROJ_UNITS - 1
                    next_split(k, i)
                    u = i * 2 + k
                    dve.wait_ge(unit_done, u + (base + 1))
                    wait(dve, tiles_ready, i * 4 + (15 * l + 2 * k - R))
                    for j in range(1 if single else 2):
                        ins = dve.tensor_tensor(halves(shifted[j][:, 1:T + 1]), pair(4 * slot(base, k) + 2 * j), halves(rs_pre[:, :]), ALU.mult)
                    ins.then_inc(evacuated, 1)
                    for j in range(1 if single else 2):
                        number = 2 * k + j - R
                        dve.wait_ge(delta_ready, i * 4 + (15 * l + number + 1))
                        if isinstance(i, int):
                            dst, mu = tile(R + number), par(l, MU + number)
                        else:
                            dst = tiles[:, bass.ds((i * 4 + (R + number)) * T, T)]
                            mu = prm[:, bass.ds(i * 4 + (l * N_PAR + MU + number), 1)]
                        dve.scalar_tensor_tensor(dst, delta[j], mu, shifted[j][:, 1:T + 1], ALU.mult, ALU.add).then_inc(tiles_ready, 1)

                for j in range(2):
                    link(dve.memset(shifted[j][:, 0:1], 0.0))
                units(dve, R // 2, heads_unit)
                units(dve, PROJ_UNITS - R // 2, shifted_unit, R // 2)

            def attend(l, pr, n_piece):
                pairs = pr + l * WT
                step = pairs * (2 * NQ)

                def soft(s):
                    j, a = divmod(s, 2)
                    nk = QT[j + 1]
                    n = nk - QT[j]
                    dve.wait_ge(scored, step + (s + 1))
                    c_query = c_tok[0:n, j, bass.ds(pr * 2 + a, 1)]
                    if nk <= 512:
                        dve.scalar_tensor_tensor(score[0:n, a, 0:nk], ps[0:n, 4 + a, 0:nk], c_query, c_key[0:n, a, 0:nk],
                                                 ALU.add, ALU.add).then_inc(score_read, 1)
                    else:
                        dve.scalar_tensor_tensor(halves(score[0:n, a, :]), ps[0:n, 4:6, 0:HT], c_query, halves(c_key[0:n, a, :]),
                                                 ALU.add, ALU.add).then_inc(score_read, 1)
                    dve.wait_ge(score_read, step + (s + 1))
                    own = score[0:n, a, QT[j]:nk]
                    dve.tensor_tensor(own, own, cst[0:n, CAUSAL:CAUSAL + n], ALU.add).then_inc(masked, 1)
                    dve.wait_ge(masked, step + (s + 1))
                    dve.tensor_reduce(neg_max[0:n, a:a + 1], score[0:n, a, 0:nk], AX.X, ALU.max, negate=True).then_inc(max_ready, 1)

                def scale(s):
                    j, a = divmod(s, 2)
                    n = QT[j + 1] - QT[j]
                    dve.wait_ge(prob_ready, step + (s + 1))
                    dve.reciprocal(inv_sum[0:n, a:a + 1], row_sum[0:n, a:a + 1]).then_inc(inv_ready, 1)
                    dve.wait_ge(inv_ready, step + (s + 1))
                    if s >= 2:
                        dve.wait_ge(prob_turned, step + (s - 1))
                    dve.tensor_scalar(diag[0:n, a, 0:n], cst[0:n, IDENT:IDENT + n], inv_sum[0:n, a:a + 1], None, ALU.mult).then_inc(diag_ready, 1)

                if n_piece == 0:
                    for a in range(2):
                        dve.tensor_scalar(c_one[:, a, :], c_all[:, :], cst[:, bass.ds(pr * 2 + (IDENT + FORGET_ROW + a), 1)], -1.0,
                                          ALU.mult, ALU.mult).then_inc(c_one_ready, 1)
                elif n_piece == 4:
                    soft(0)
                elif n_piece > 4:
                    s, kind = step_piece(n_piece)
                    j, a = divmod(s, 2)
                    if kind == 0:
                        scale(s)
                        if s + 1 < 2 * NQ:
                            soft(s + 1)
                    elif kind == 2 and a == 1:
                        n = QT[j + 1] - QT[j]
                        dve.wait_ge(att_done, pairs * NQ + (j + 1))
                        dve.tensor_copy(tiles[:, bass.ds((pr + QF) * T + QT[j], n)], ps[:, 7, 0:n]).then_inc(att_read, 1)

            def low_rank(l):
                row = slice(FORGET_ROW, FORGET_ROW + HEADS)
                link(dve.memset(c_all[:, :], 0.0))
                dve.wait_ge(tiles_ready, 15 * (l + 1))
                if l == 0:
                    dve.wait_ge(cst_loaded, 16)
                link(dve.tensor_scalar(fg[row, 0, :], tile(MISC)[row, :], par(l, FBIAS, FORGET_ROW, FORGET_ROW + HEADS), None, ALU.add))
                dve.scalar_tensor_tensor(fg[row, 1, :], fg[row, 0, :], -1.0, fg[row, 0, :], ALU.mult, ALU.min).then_inc(fg_abs, 1)
                for m in range(WT):
                    n = WT * l + m
                    k, b = tile(K + m), bonus[:, m, :]
                    dve.wait_ge(decay_sig, n + 1)
                    step(dve.tensor_tensor_scan(ll[:, m, :], cst[:, RESET:RESET + T], ll[:, m, :], 0.0, ALU.mult, ALU.add))
                    kk_scaled = step(dve.tensor_scalar(kk[:, m, :], k, par(l, KKG + m), None, ALU.mult))
                    dve.wait_ge(iclr_sig, n + 1)
                    a_scaled = step(dve.tensor_scalar(b, aa[:, m, :], 1.0, par(l, KAG + m), ALU.subtract, ALU.mult))
                    dve.wait_ge(knorm_done, n + 1)
                    dve.tensor_scalar(halves(k_inverse[m]), pair(6), 1e-24, None, ALU.max).then_inc(kmax_ready, 1)
                    dve.wait_ge(dve_step, max(kk_scaled, a_scaled))
                    link(dve.scalar_tensor_tensor(k, b, 1.0, k, ALU.add, ALU.mult))
                    dve.scalar_tensor_tensor(b, tile(R + m), par(l, RKG + m), k, ALU.mult, ALU.mult).then_inc(rk_ready, 1)
                dve.wait_ge(fg_exp, l + 1)
                link(dve.scalar_tensor_tensor(fg[row, 0, :], fg[row, 0, :], 0.0, fg[row, 1, :], ALU.min, ALU.subtract))
                dve.tensor_tensor_scan(c_all[row, :], cst[row, ONES:ONES + 1].broadcast_to([HEADS, T]), fg[row, 0, :], 0.0,
                                       ALU.mult, ALU.add).then_inc(c_ready, 1)
                normed = []
                for m in range(WT):
                    dve.wait_ge(kinv_ready, WT * l + m + 1)
                    normed.append(step(dve.tensor_tensor(kk[:, m, :], kk[:, m, :], k_inverse[m], ALU.mult)))
                    if m:
                        dve.wait_ge(dve_step, normed[m - 1])
                        step(dve.tensor_tensor(aa[:, m - 1, :], kk[:, m - 1, :], aa[:, m - 1, :], ALU.mult))
                dve.wait_ge(dve_step, normed[-1])
                link(dve.tensor_tensor(aa[:, WT - 1, :], kk[:, WT - 1, :], aa[:, WT - 1, :], ALU.mult))
                for m in range(WT):
                    n = WT * l + m
                    dve.wait_ge(bonus_done, n + 1)
                    if l:
                        dve.wait_ge(v_mixed, n - WT + 1)
                    dve.tensor_tensor(halves(bonus[:, m, :]), pair(BONUS_BANKS[m]), halves(tile(V + m)), ALU.mult).then_inc(bonus_ready, 1)
                dve.wait_ge(bonus_ready, WT * (l + 1))

            def tail(l, place):
                n = WT * l
                if place in (5, 6, 7, 12):
                    m = (5, 6, 7, 12).index(place)
                    dve.wait_ge(g_done, n + m + 1)
                    dve.tensor_copy(halves(tile(VF + m)), pair(4 + 2 * (m % 2))).then_inc(g_kept, 1)
                elif place == 14:
                    for m in range(WT):
                        dve.wait_ge(frs_ready, n + m + 1)
                        dve.scalar_tensor_tensor(tile(QF + m), tile(QF + m), par(l, FOXG + m), ll[:, m, :], ALU.mult, ALU.mult).then_inc(f_ready, 1)

            def chunks(l):
                for b in range(2):
                    dve.memset(e_fwd[b][:, :, 0:1], 1.0)
                dve.memset(hs, 0.0)
                dve.memset(a_blocks[:, :, :, :], 0.0).then_inc(bd_zero, 1)
                dve.wait_ge(bd_zero, 2 * (l + 1))

                def build_ar(c, b, n, cc):
                    tokens = bass.ds(c * CHUNK, n)
                    if n < CHUNK:
                        dve.memset(bkv[0:HEAD, b, :, :].rearrange("p m (i c) -> p m i c", i=3)[:, :, :, n:2 * n], 0.0)
                        dve.memset(a_blocks[0:HEAD, b, :, n:2 * n], 0.0)
                    dve.wait_ge(e_ready, cc + 1)
                    for a in range(2):
                        rows = slice(a * HEAD, (a + 1) * HEAD)
                        dve.scalar_tensor_tensor(a_blocks[rows, b, :, a * n:(a + 1) * n], kk[rows, :, tokens], -1.0, e_fwd[b][rows, :, 0:n], ALU.mult, ALU.mult)
                    dve.scalar_tensor_tensor(ar[:, b, :, 0:n], kk[:, :, tokens], -1.0, e_fwd[b][:, :, 0:n], ALU.mult, ALU.mult)
                    ins = dve.tensor_tensor(ar[:, b, :, n:2 * n], group(R)[:, :, tokens], e_fwd[b][:, :, 1:n + 1], ALU.mult)
                    ins.then_inc(ar_built, 1)

                def four(bank, w):
                    return ps[0:w, bank, :].rearrange("p (m c) -> p m c", m=WT)[:, :, 0:w]

                def chunk(c, b, n, following, beside):
                    cc, w, levels = c + l * N_CHUNK, 2 * n, LEVEL_COUNT[n]
                    masked_before, solved_before, turned_before = (so_far(l, c, k) for k in (0, 1, 2))
                    y, z, identity = ym[0:w, :, 0:w], zm[0:w, :, 0:w], spread(ident[0:w, 0:w], WT)
                    for pr in range(WT):
                        dve.wait_ge(gram_done, cc * WT + (pr + 1))
                        products = ps[0:w, pr % 2, 0:2 * P].rearrange("p (i c) -> p i c", i=2)
                        dve.tensor_tensor(gm[0:w, pr, 0:2 * P].rearrange("p (i c) -> p i c", i=2)[:, :, 0:w].rearrange("p i (a t) -> p i a t", a=2),
                                          products[:, :, 0:n].unsqueeze(2).broadcast_to([w, 2, 2, n]),
                                          cst[0:w, MASK[n]:MASK[n] + w].rearrange("p (a t) -> p a t", a=2).unsqueeze(1).broadcast_to([w, 2, 2, n]), ALU.mult)
                        dve.tensor_tensor(gm[0:w, pr, 2 * P:3 * P].rearrange("p (i t) -> p i t", i=2)[:, :, 0:n], products[:, :, n:w],
                                          spread(cst[0:w, MASK[n] + w:MASK[n] + w + n], 2), ALU.mult).then_inc(gram_ready, 1)
                    beside(0)
                    dve.wait_ge(off_ready, masked_before + 1)
                    dve.tensor_tensor(y, uo[0:w, :, 0:w], identity, ALU.add).then_inc(y_ready, 1)
                    dve.wait_ge(z0_done, cc + 1)
                    dve.tensor_tensor(z, four(0, w), identity, ALU.add).then_inc(z_ready, 1)
                    beside(1)
                    for v in range(1, levels):
                        beside(2 * v)
                        if v < levels - 1:
                            dve.wait_ge(zd_done, turned_before + v)
                            dve.tensor_tensor(z, four(2, w), z, ALU.add).then_inc(z_ready, 1)
                        dve.wait_ge(yd_done, solved_before + v)
                        dve.tensor_tensor(y, four(3, w), y, ALU.add).then_inc(y_ready, 1)
                        beside(2 * v + 1)
                        if v == 2 and following:
                            build_ar(c + 1, 1 - b, following, cc + 1)
                    beside(12)
                    beside(13)
                    if n == CHUNK:
                        full = c + (l * (N_CHUNK - 1) + 1)
                        dve.wait_ge(hd_done, full)
                        dve.tensor_tensor(hs, four(3, P), hs, ALU.add).then_inc(h_added, 1)
                        dve.wait_ge(h_added, full)
                        dve.tensor_tensor(hs, hs, e_fwd[b][:, :, n:n + 1].broadcast_to([P, WT, P]), ALU.mult).then_inc(state_ready, 1)
                    beside(14)

                def pair_of_chunks(pr, last):
                    for second in range(2):
                        chunk(pr * 2 + second, second, CHUNK, LAST if last and second else CHUNK,
                              lambda place: [attend(l, pr, n) for n in pieces(second, place)])
                    dve.wait_ge(prob_turned, (pr + l * WT) * (2 * NQ) + 2 * NQ)

                build_ar(0, 0, CHUNK, l * N_CHUNK)
                pair_loop(dve, pair_of_chunks)
                chunk(N_CHUNK - 1, 0, LAST, 0, lambda place: tail(l, place))

            def head_outputs(l):
                g, n = 4 * l + 2, WT * l

                def low(number, m, src):
                    dve.wait_ge(x_hi_ready, DT * g + number + 1)
                    dve.tensor_tensor(x_lo[:, m, :], src, x_hi[:, m, :], ALU.subtract).then_inc(x_lo_ready, 1)

                for m in range(WT):
                    dve.wait_ge(mean_done, n + m + 1)
                    dve.scalar_tensor_tensor(halves(tile(R + m)), pair(2 * m), -1.0 / HEAD, halves(tile(R + m)), ALU.mult, ALU.add).then_inc(oc_ready, 1)
                split_lo(UNIT, unit_base(l, "wo"), 0)
                for m in range(WT):
                    low(m, m + WT, tile(QF + m))
                scaled = []
                for m in range(WT):
                    dve.wait_ge(ors_ready, n + m + 1)
                    scaled.append(step(dve.scalar_tensor_tensor(tile(R + m), tile(R + m), par(l, LNW + m), aa[:, m, :], ALU.mult, ALU.mult)))
                    if m:
                        add_bonus(l, m - 1, scaled[m - 1])
                add_bonus(l, WT - 1, scaled[-1])
                for m in range(WT):
                    dve.wait_ge(o_ready, n + m + 1)
                    low(m + WT, m, tile(R + m))

            def add_bonus(l, m, scaled):
                dve.wait_ge(dve_step, scaled)
                dve.scalar_tensor_tensor(tile(R + m), tile(R + m), par(l, LNB + m), bonus[:, m, :], ALU.add, ALU.add).then_inc(o_built, 1)

            def mixer_out(l):
                base = unit_base(l, "wo")

                for k in range(WO_UNITS):
                    q = slot(base, k)
                    split_lo(UNIT, base, k + 1)
                    dve.wait_ge(unit_done, base + k + 1)
                    for j in range(2):
                        ins = dve.tensor_copy(halves(y_mix[:, 2 * k + j, :]), pair(4 * q + 2 * j))
                    ins.then_inc(evacuated, 1)
                split_lo(UNIT, base + WO_UNITS, 1)

            dve.memset(eps[:, 0:1], NORM_EPS).then_inc(eps_set, 1)
            dve.memset(eps[:, 1:2], 4 * NORM_EPS).then_inc(eps_set, 1)
            dve.memset(eps[:, 2:3], LNX_EPS).then_inc(eps_set, 1)
            dve.memset(eps[:, 3:4], 1.0).then_inc(eps_set, 1)
            dve.wait_ge(small_loaded, 16)
            split_lo(UNIT, 0, 0)
            split_lo(UNIT, 0, 1)
            for m in range(DT):
                dve.wait_ge(h_loaded[m], 16)
                x_lo_of(0, 0, 0, m)
            for l in range(DEPTH):
                ffn(l, "a", 2 * l, 0)
                update(l, 0, y_ffn, (l, 1, 2))
                projection(l)
                low_rank(l)
                chunks(l)
                head_outputs(l)
                mixer_out(l)
                update(l, 1, y_mix, (l, 3, 4))
                ffn(l, "b", 2 * l + 1, 4)
                update(l, 2, y_ffn, (l + 1, 0, 0) if l + 1 < DEPTH else None)

        @block.gpsimd
        def _(pool):
            def add_squares(s, k, i=0):
                if k in (0, DT - 1):
                    return
                count = i * 2 + ((DT - 2) * s + k)
                pool.wait_ge(sq_ready, i * 2 + (DT * s + k + 1))
                wait(pool, acc_added, count - 1)
                pool.tensor_tensor(acc[:, :], acc[:, :], sqb[:, k % 2, :], ALU.add).then_inc(acc_added, 1)

            def ffn(l, which, f, n):
                for m in range(DT):
                    add_squares(6 * l + n, m)
                for fh in range(2):
                    base = unit_base(l, which) + fh * (FH + DT)

                    def unit_in(k, i):
                        u, q = i * 2 + k, slot(base, k)
                        pool.wait_ge(sg_ready, u + (FH * (2 * f + fh) + 1))
                        pool.wait_ge(evacuated, u + (base + 1))
                        pool.tensor_tensor(hid[:, q, :], sg[:, q, :], us[:, q, :], ALU.mult).then_inc(hid_ready, 1)
                    units(pool, FH, unit_in)
                    if fh == 1:
                        units(pool, DT, lambda k, i: add_squares(6 * l + n + 1, k, i))

            def scale_y(l, post, y):
                pool.wait_ge(rs_ready, 6 * l + 2 * post + 2)
                for m in POOL_TILES:
                    pool.tensor_tensor(y[:, m, :], y[:, m, :], rs_post[:, :], ALU.mult).then_inc(y_scaled, 1)

            def projection(l):
                for m in range(DT):
                    add_squares(6 * l + 2, m)
                base = unit_base(l, "proj")

                def unit(k, i):
                    pool.wait_ge(evacuated, i * 2 + (base + k + 1))
                    for j in range(1 if k == PROJ_UNITS - 1 else 2):
                        pool.tensor_tensor(delta[j], shifted[j][:, 0:T], shifted[j][:, 1:T + 1], ALU.subtract).then_inc(delta_ready, 1)
                units(pool, PROJ_UNITS - R // 2, unit, R // 2)

            def mix_values(l):
                for m in range(WT):
                    n = WT * (l - 1) + m
                    v, mix = tile(V + m), v_mix[m % 2]
                    if m >= 2:
                        pool.wait_ge(v_mixed, n - 1)
                    pool.tensor_tensor(mix, v_first[:, m, :], v, ALU.subtract).then_inc(v_step, 1)
                    pool.wait_ge(v_step, 2 * n + 1)
                    pool.wait_ge(vres_sig, n + 1)
                    pool.tensor_tensor(mix, mix, v_weight[m], ALU.mult).then_inc(v_step, 1)
                    pool.wait_ge(v_step, 2 * n + 2)
                    pool.tensor_tensor(v, v, mix, ALU.add).then_inc(v_mixed, 1)

            def chunks(l):
                pool.memset(bkv[:, :, :, :], 0.0).then_inc(bd_zero, 1)
                if l:
                    mix_values(l)
                pool.wait_ge(bd_zero, 2 * (l + 1))
                pool.wait_ge(bonus_ready, WT * (l + 1))

                def build_bk(c, b, n, cc):
                    tokens = bass.ds(c * CHUNK, n)
                    pool.wait_ge(e_ready, cc + 1)
                    for a in range(2):
                        rows = slice(a * HEAD, (a + 1) * HEAD)
                        for i, src in enumerate((aa[rows, :, :], group(K, p0=a * HEAD, p1=(a + 1) * HEAD))):
                            pool.tensor_tensor(bkv[rows, b, :, i * P + a * n:i * P + (a + 1) * n], src[:, :, tokens],
                                               e_bwd[b][rows, :, 0:n], ALU.mult).then_inc(bkv_built, 1)
                            pool.wait_ge(bkv_built, cc * 4 + (2 * a + i + 1))

                def chunk(c, b, n, following):
                    cc, w = c + l * N_CHUNK, 2 * n
                    masked_before, solved_before = so_far(l, c, 0), so_far(l, c, 1)
                    pool.wait_ge(gram_ready, cc * WT + WT)
                    for v in range(LEVEL_COUNT[n]):
                        if v == 1:
                            pool.wait_ge(z0_done, cc + 1)
                            pool.wait_ge(y_ready, masked_before + 1)
                        if v > 1:
                            pool.wait_ge(q_done, solved_before + (v - 1))
                        pool.tensor_tensor(uo[0:w, :, 0:w], gm[0:w, :, 0:w], spread(cst[0:w, LEVEL + v * P:LEVEL + v * P + w], WT), ALU.mult).then_inc(off_ready, 1)
                        if v == 2 and following:
                            pool.wait_ge(off_ready, masked_before + 3)
                            build_bk(c + 1, 1 - b, following, cc + 1)

                def pair_of_chunks(pr, last):
                    chunk(pr * 2, 0, CHUNK, CHUNK)
                    chunk(pr * 2 + 1, 1, CHUNK, LAST if last else CHUNK)

                build_bk(0, 0, CHUNK, l * N_CHUNK)
                pair_loop(pool, pair_of_chunks)
                chunk(N_CHUNK - 1, 0, LAST, 0)

            for l in range(DEPTH):
                ffn(l, "a", 2 * l, 0)
                scale_y(l, 0, y_ffn)
                projection(l)
                pool.wait_ge(evacuated, unit_base(l, "wo"))
                pool.wait_ge(tiles_ready, 15 * (l + 1))
                pool.memset(qz[:, :, :], 0.0)
                pool.memset(vz[:, :, :, :], 0.0).then_inc(att_zero, 1)
                chunks(l)
                for m in range(WT):
                    pool.wait_ge(o_built, WT * l + m + 1)
                    pool.wait_ge(g_kept, WT * l + m + 1)
                    pool.tensor_tensor(tile(R + m), tile(R + m), tile(VF + m), ALU.mult).then_inc(o_ready, 1)
                for m in range(DT):
                    add_squares(6 * l + 3, m)
                scale_y(l, 1, y_mix)
                ffn(l, "b", 2 * l + 1, 4)
                scale_y(l, 2, y_ffn)


_OUT = (P, DT, SEQ)


def constants():
    c = np.zeros((P, N_CONST), np.float32)
    s, t = np.arange(P)[:, None], np.arange(P)[None, :]
    same = s // HEAD == t // HEAD
    c[:, IDENT:IDENT + P] = s == t
    c[:, ONES:ONES + P] = 1
    c[:, HEADSUM:HEADSUM + P] = same
    c[:, CAUSAL:CAUSAL + P] = np.where(t > s, NEG, 0)
    for n, col in MASK.items():
        w = 2 * n
        c[0:w, col:col + w] = ((s // n == t // n) & (s < t))[0:w, 0:w]
        c[0:w, col + w:col + w + n] = (s % n <= t)[0:w, 0:n]
    for v in range(LEVELS):
        b = 1 << v
        c[:, LEVEL + v * P:LEVEL + (v + 1) * P] = same & (s < t) & (s // (2 * b) == t // (2 * b)) & (s // b != t // b)
    c[:, RESET:RESET + T] = np.arange(T)[None, :] % CHUNK != 0
    return c


def lay_out(x, meta_tokens, norm_gains, ffn_w_in, ffn_w_out, w_in, w_in_vres, shift_mu, shift_mu_vres,
            decay_up, decay_bias, iclr_up, iclr_bias, gate_up, vres_up, vres_bias, k_k, k_a, r_k,
            ln_x_w, ln_x_b, forget_bias, fox_out_gain, w_out):
    f = np.float32
    tokens = np.concatenate([meta_tokens, x[0]], axis=0)
    h_in = tokens.T.reshape(DT, P, T).transpose(1, 0, 2)
    win = ffn_w_in.reshape(DEPTH * 2, DT, P, 2, FT, P).transpose(0, 4, 2, 3, 1, 5).reshape(DEPTH * 2, FT, P, UNIT)
    wout = ffn_w_out.reshape(DEPTH * 2, 2, FH, P, DT, P).transpose(0, 1, 4, 3, 2, 5).reshape(DEPTH * 2, 2, DT, P, OUT_UNIT)
    w3 = 3 * WIDTH
    n_rwkv = w3 + 64 + 64 + 160
    cols = np.zeros((DEPTH, D_MODEL, (N_TILES + 1) * P), f)
    mu = np.zeros((DEPTH, (N_TILES - R) * P), f)
    cols[:, :, 0:w3] = w_in[:, :, n_rwkv:n_rwkv + w3]
    cols[:, :, w3:2 * w3 + 256] = w_in[:, :, 0:w3 + 256]
    mu[:, 0:w3 + 256] = shift_mu[:, 0:w3 + 256]
    misc = MISC * P
    cols[:, :, misc:misc + 32] = w_in[:, :, w3 + 256:n_rwkv]
    mu[:, misc - R * P:misc - R * P + 32] = shift_mu[:, w3 + 256:n_rwkv]
    cols[1:, :, misc + 32:misc + 64] = w_in_vres
    mu[1:, misc - R * P + 32:misc - R * P + 64] = shift_mu_vres
    cols[:, :, misc + FORGET_ROW:misc + FORGET_ROW + HEADS] = w_in[:, :, n_rwkv + w3:]
    proj = cols.reshape(DEPTH, DT, P, PROJ_UNITS, 2, P).transpose(0, 3, 2, 4, 1, 5).reshape(DEPTH, PROJ_UNITS, P, UNIT)
    wo = w_out.reshape(DEPTH, DT, P, WO_UNITS, 2, P).transpose(0, 3, 2, 4, 1, 5).reshape(DEPTH, WO_UNITS, P, UNIT)
    lora = np.zeros((DEPTH, P, 5 * WIDTH), f)
    lora[:, 0:64, 0:WIDTH] = decay_up
    lora[:, 64:128, WIDTH:2 * WIDTH] = iclr_up
    lora[1:, 32:64, 2 * WIDTH:3 * WIDTH] = vres_up
    lora[:, :, 3 * WIDTH:4 * WIDTH] = gate_up[:, 0:P]
    lora[:, 0:32, 4 * WIDTH:5 * WIDTH] = gate_up[:, P:]
    params = np.zeros((P, DEPTH, N_PAR), f)

    def columns(col, a):
        a = a.reshape(DEPTH, -1, P).transpose(2, 0, 1)
        params[:, :, col:col + a.shape[2]] = a
    columns(GAIN, norm_gains)
    columns(MU, mu)
    vb = np.zeros((DEPTH, WIDTH), f)
    vb[1:] = vres_bias
    for col, a in ((DBIAS, decay_bias), (IBIAS, iclr_bias), (VBIAS, vb), (KKG, k_k), (KAG, k_a), (RKG, r_k),
                   (LNW, ln_x_w), (LNB, ln_x_b), (FOXG, fox_out_gain)):
        columns(col, a)
    params[FORGET_ROW:FORGET_ROW + HEADS, :, FBIAS] = forget_bias.T
    return {"h_in": h_in, "ffn_in": win, "ffn_out": wout, "proj": proj, "w_out": wo, "lora": lora,
            "params": params.reshape(P, DEPTH * N_PAR), "consts": constants()}


def kernel(**inputs):
    import concourse.bacc as bacc
    from concourse.bass_utils import run_bass_kernel_spmd

    arrays = {k: np.ascontiguousarray(v) for k, v in lay_out(**{k: np.asarray(v) for k, v in inputs.items()}).items()}
    nc = bacc.Bacc("TRN2", target_bir_lowering=False, num_devices=1, dynamic_dma_scratch_size=1024)
    args = [nc.dram_tensor(f"in_{k}", a.shape, F32, kind="ExternalInput").ap() for k, a in arrays.items()]
    out = nc.dram_tensor("out_h", _OUT, F32, kind="ExternalOutput").ap()
    build(nc, *args, out)
    r = run_bass_kernel_spmd(nc, [{f"in_{k}": a for k, a in arrays.items()}], core_ids=[0])
    got = r.results[0]["out_h"]
    return np.ascontiguousarray(got.transpose(2, 1, 0)).reshape(1, SEQ, D_MODEL)
```
